# Optimizing a Trainium2 kernel written in Bass

```python
import math
import jax
import jax.numpy as jnp
from jax import lax
import numpy as np

D_MODEL = 1024
BATCH = 1
SEQ = 1024
DEPTH = 1
DEC_BATCH = 8
DEC_SEQ = 1
PAST_LEN = 512
PAGE_SIZE = 128

D_MIX = D_MODEL
D_GROUP = D_MIX // 4
HEAD_DIM = D_GROUP // 4
H_FOX = D_GROUP // HEAD_DIM
H_NSA = D_GROUP // HEAD_DIM
G_NSA = 2
H_MEM = D_GROUP // HEAD_DIM
D_FOX = H_FOX * HEAD_DIM
D_NSA = H_NSA * HEAD_DIM
D_POOL = D_GROUP
D_MEMX = H_MEM * HEAD_DIM
KV_NSA = G_NSA * HEAD_DIM
POOL_WINDOWS = (2, 4, 8, 16)
N_POOL_GROUPS = len(POOL_WINDOWS)
POOL_GW = D_POOL // N_POOL_GROUPS
POOL_BUF = max(POOL_WINDOWS) - 1
N_MEM = 256
NSA_BLOCK = 64
NSA_TOPN = 16
NSA_WINDOW = 512
NSA_CMP_HID = 256
Q_BLOCK = 128
FGT_BIAS_MEAN = 3.0
RMS_EPS = 1e-6
NEG_INF = -1e30
FORCE_SCORE = 1e4
D_IN = 3 * D_FOX + H_FOX + D_NSA + 6 * KV_NSA + 3 * H_NSA + D_POOL + D_MEMX + D_MIX

kernel_name = "hymba_fox_nsa_pool_decoder_step"

F32 = jnp.float32

def rms_norm(x, g):
    xf = x.astype(F32)
    y = xf * lax.rsqrt(jnp.mean(xf * xf, axis=-1, keepdims=True) + RMS_EPS)
    return (y * g.astype(F32)).astype(x.dtype)

def masked_softmax(s, mask):
    s = jnp.where(mask, s, NEG_INF)
    e = jnp.where(mask, jnp.exp(s - jnp.max(s, axis=-1, keepdims=True)), 0.0)
    return e / jnp.maximum(jnp.sum(e, axis=-1, keepdims=True), 1e-30)

def alibi_slopes(n):
    return jnp.asarray([2.0 ** (-8.0 * (h + 1) / n) for h in range(n)], F32)

def split_projection(p):
    B, T = p.shape[:2]
    sizes = (3 * D_FOX, H_FOX, D_NSA, 6 * KV_NSA, 3 * H_NSA, D_POOL, D_MEMX, D_MIX)
    pts, acc = [], 0
    for s in sizes[:-1]:
        acc += s
        pts.append(acc)
    fox_qkv, fox_f, nsa_q, nsa_kv, nsa_g, pool_u, mem_q, z = jnp.split(p, pts, axis=-1)
    return (fox_qkv.reshape(B, T, 3, H_FOX, HEAD_DIM), fox_f,
            nsa_q.reshape(B, T, H_NSA, HEAD_DIM), nsa_kv.reshape(B, T, 6, G_NSA, HEAD_DIM),
            nsa_g.reshape(B, T, H_NSA, 3), pool_u, mem_q.reshape(B, T, H_MEM, HEAD_DIM), z)

def fox_attention(q, qpos, cq, k, v, kpos, ck):
    s = jnp.einsum('bqhd,bkhd->bhqk', q, k).astype(F32) * (HEAD_DIM ** -0.5)
    s = s + jnp.swapaxes(cq, 1, 2)[:, :, :, None] - jnp.swapaxes(ck, 1, 2)[:, :, None, :]
    mask = (kpos[None, :] <= qpos[:, None])[None, None]
    p = masked_softmax(s, mask)
    return jnp.einsum('bhqk,bkhd->bqhd', p.astype(v.dtype), v)

def fox_prompt(q, k, v, lf):
    B, T = q.shape[:2]
    c = jnp.cumsum(lf, axis=1)
    kpos = jnp.arange(T)

    def block(i):
        q0 = i * Q_BLOCK
        qb = lax.dynamic_slice_in_dim(q, q0, Q_BLOCK, axis=1)
        cb = lax.dynamic_slice_in_dim(c, q0, Q_BLOCK, axis=1)
        return fox_attention(qb, q0 + jnp.arange(Q_BLOCK), cb, k, v, kpos, c)

    o = lax.map(block, jnp.arange(T // Q_BLOCK))
    return jnp.swapaxes(o, 0, 1).reshape(B, T, H_FOX * HEAD_DIM)

def nsa_compress(rows, pe, w1, w2):
    B, L, G, dh = rows.shape
    nb = L // NSA_BLOCK
    blk = rows.reshape(B, nb, NSA_BLOCK, G, dh) + pe[:, None, :].astype(rows.dtype)
    flat = jnp.transpose(blk, (0, 1, 3, 2, 4)).reshape(B, nb, G, NSA_BLOCK * dh)
    hid = jax.nn.silu(jnp.einsum('bngf,fe->bnge', flat, w1))
    return jnp.einsum('bnge,ed->bngd', hid, w2)

def nsa_attention(q, qpos, gates, k_cmp, v_cmp, k_sel, v_sel, k_win, v_win, wpos):
    B, Q = q.shape[:2]
    R = H_NSA // G_NSA
    nb = k_cmp.shape[1]
    scale = HEAD_DIM ** -0.5
    slopes = alibi_slopes(H_NSA).reshape(G_NSA, R)[None, None, :, :, None]
    qg = q.reshape(B, Q, G_NSA, R, HEAD_DIM)
    blk = jnp.arange(nb)
    cmp_end = blk * NSA_BLOCK + (NSA_BLOCK - 1)
    s_c = jnp.einsum('bqgrd,bngd->bqgrn', qg, k_cmp).astype(F32) * scale
    s_c = s_c - slopes * (qpos[:, None] - cmp_end[None, :]).astype(F32)[None, :, None, None, :]
    m_c = (cmp_end[None, :] <= qpos[:, None])[None, :, None, None, :]
    p_c = masked_softmax(s_c, m_c)
    o_c = jnp.einsum('bqgrn,bngd->bqgrd', p_c.astype(v_cmp.dtype), v_cmp)
    cur = qpos // NSA_BLOCK
    imp = jnp.sum(p_c, axis=3)
    forced = (blk[None, :] == 0) | (blk[None, :] == cur[:, None]) | (blk[None, :] == cur[:, None] - 1)
    future = blk[None, :] > cur[:, None]
    score = jnp.where(future[None, :, None, :], -1.0,
                      jnp.where(forced[None, :, None, :], FORCE_SCORE, imp))
    top_val, top_idx = lax.top_k(score, min(NSA_TOPN, nb))
    n = top_idx.shape[-1]
    k_blk = jnp.transpose(k_sel.reshape(B, nb, NSA_BLOCK, G_NSA, HEAD_DIM), (0, 3, 1, 2, 4))
    v_blk = jnp.transpose(v_sel.reshape(B, nb, NSA_BLOCK, G_NSA, HEAD_DIM), (0, 3, 1, 2, 4))
    bi = jnp.arange(B)[:, None, None, None]
    gi = jnp.arange(G_NSA)[None, None, :, None]
    k_g = k_blk[bi, gi, top_idx]
    v_g = v_blk[bi, gi, top_idx]
    spos = top_idx[..., None] * NSA_BLOCK + jnp.arange(NSA_BLOCK)
    m_s = (top_val >= 0)[..., None] & (spos <= qpos[None, :, None, None, None])
    s_s = jnp.einsum('bqgrd,bqgnsd->bqgrns', qg, k_g).astype(F32) * scale
    s_s = s_s - slopes[..., None] * (qpos[None, :, None, None, None] - spos).astype(F32)[:, :, :, None]
    p_s = masked_softmax(s_s.reshape(B, Q, G_NSA, R, n * NSA_BLOCK),
                         m_s[:, :, :, None].reshape(B, Q, G_NSA, 1, n * NSA_BLOCK))
    o_s = jnp.einsum('bqgrns,bqgnsd->bqgrd',
                     p_s.reshape(B, Q, G_NSA, R, n, NSA_BLOCK).astype(v_g.dtype), v_g)
    dist = qpos[:, None] - wpos[None, :]
    s_w = jnp.einsum('bqgrd,bkgd->bqgrk', qg, k_win).astype(F32) * scale
    s_w = s_w - slopes * dist.astype(F32)[None, :, None, None, :]
    m_w = ((dist >= 0) & (dist <= NSA_WINDOW) & (wpos[None, :] >= 0))[None, :, None, None, :]
    p_w = masked_softmax(s_w, m_w)
    o_w = jnp.einsum('bqgrk,bkgd->bqgrd', p_w.astype(v_win.dtype), v_win)
    g = jax.nn.sigmoid(gates.astype(F32)).reshape(B, Q, G_NSA, R, 3)
    o = g[..., 0:1] * o_c + g[..., 1:2] * o_s + g[..., 2:3] * o_w
    return o.reshape(B, Q, H_NSA * HEAD_DIM).astype(q.dtype)

def nsa_prompt(q, kv, gates, pe, w1, w2):
    B, T = q.shape[:2]
    k_cmp = nsa_compress(kv[:, :, 0], pe[0], w1[0], w2[0])
    v_cmp = nsa_compress(kv[:, :, 1], pe[1], w1[1], w2[1])
    k_sel, v_sel = kv[:, :, 2], kv[:, :, 3]
    pad = ((0, 0), (NSA_WINDOW, 0), (0, 0), (0, 0))
    k_w = jnp.pad(kv[:, :, 4], pad)
    v_w = jnp.pad(kv[:, :, 5], pad)
    lw = NSA_WINDOW + Q_BLOCK

    def block(i):
        q0 = i * Q_BLOCK
        qpos = q0 + jnp.arange(Q_BLOCK)
        wpos = q0 - NSA_WINDOW + jnp.arange(lw)
        return nsa_attention(lax.dynamic_slice_in_dim(q, q0, Q_BLOCK, axis=1), qpos,
                             lax.dynamic_slice_in_dim(gates, q0, Q_BLOCK, axis=1),
                             k_cmp, v_cmp, k_sel, v_sel,
                             lax.dynamic_slice_in_dim(k_w, q0, lw, axis=1),
                             lax.dynamic_slice_in_dim(v_w, q0, lw, axis=1), wpos)

    o = lax.map(block, jnp.arange(T // Q_BLOCK))
    return jnp.swapaxes(o, 0, 1).reshape(B, T, H_NSA * HEAD_DIM)

def nsa_sample(q, kv_new, gates, kv_past, win_buf, pe, w1, w2):
    DB, DS = q.shape[:2]
    past = kv_past.shape[1]
    L = past + DS
    Lp = -(-L // NSA_BLOCK) * NSA_BLOCK
    rows = jnp.concatenate([kv_past, kv_new[:, :, :4]], axis=1)
    rows = jnp.pad(rows, ((0, 0), (0, Lp - L), (0, 0), (0, 0), (0, 0)))
    k_cmp = nsa_compress(rows[:, :, 0], pe[0], w1[0], w2[0])
    v_cmp = nsa_compress(rows[:, :, 1], pe[1], w1[1], w2[1])
    w_buf = win_buf.shape[1]
    win = jnp.concatenate([win_buf, kv_new[:, :, 4:6]], axis=1)
    wpos = past - w_buf + jnp.arange(w_buf + DS)
    qpos = past + jnp.arange(DS)
    o = nsa_attention(q, qpos, gates, k_cmp, v_cmp, rows[:, :, 2], rows[:, :, 3],
                      win[:, :, 0], win[:, :, 1], wpos)
    return o, win[:, win.shape[1] - w_buf:]

def pool_mix(u_ext, pos_ext, n_out, w_pool, scale):
    N = u_ext.shape[1]
    cz = jnp.pad(jnp.cumsum(u_ext.astype(F32), axis=1), ((0, 0), (1, 0), (0, 0)))
    idx = jnp.arange(N - n_out, N)
    cnt_pos = pos_ext[N - n_out:]
    u_out = u_ext[:, N - n_out:].astype(F32)
    outs = []
    for g, w in enumerate(POOL_WINDOWS):
        sl = slice(g * POOL_GW, (g + 1) * POOL_GW)
        lo = jnp.maximum(idx + 1 - w, 0)
        cnt = jnp.minimum(cnt_pos + 1, w).astype(F32)[None, :, None]
        mean = (cz[:, idx + 1, sl] - cz[:, lo, sl]) / cnt
        outs.append(jnp.einsum('btc,ce->bte', mean - u_out[:, :, sl], w_pool[g].astype(F32)))
    return (jnp.concatenate(outs, axis=-1) * scale.astype(F32)).astype(u_ext.dtype)

def mem_attention(q, mem_kv):
    B, T = q.shape[:2]
    s = jnp.einsum('bthd,bmhd->bhtm', q, mem_kv[:, :, 0]).astype(F32) * (HEAD_DIM ** -0.5)
    p = jax.nn.softmax(s, axis=-1)
    return jnp.einsum('bhtm,bmhd->bthd', p.astype(q.dtype), mem_kv[:, :, 1]).reshape(B, T, H_MEM * HEAD_DIM)

def mix_out(x, outs, z, w_out):
    o = jnp.concatenate(outs, axis=-1) * jax.nn.silu(z)
    return x + jnp.einsum('bte,ed->btd', o, w_out)

def layer_prompt(x, mem, lw):
    g_n, w_in, b_f, pe, w1, w2, p_w, p_s, w_mkv, w_o = lw
    B, T, _ = x.shape
    hn = rms_norm(x, g_n)
    fox_qkv, fox_f, nsa_q, nsa_kv, nsa_g, pool_u, mem_q, z = split_projection(
        jnp.einsum('btd,de->bte', hn, w_in))
    lf = jax.nn.log_sigmoid(fox_f.astype(F32) + b_f.astype(F32))
    o_a = fox_prompt(fox_qkv[:, :, 0], fox_qkv[:, :, 1], fox_qkv[:, :, 2], lf)
    o_b = nsa_prompt(nsa_q, nsa_kv, nsa_g, pe, w1, w2)
    o_c = pool_mix(pool_u, jnp.arange(T), T, p_w, p_s)
    mem_kv = jnp.einsum('bmd,de->bme', mem, w_mkv).reshape(B, N_MEM, 2, H_MEM, HEAD_DIM)
    o_m = mem_attention(mem_q, mem_kv)
    y = mix_out(x, [o_a, o_b, o_c, o_m], z, w_o)
    w_keep = min(NSA_WINDOW, T)
    return y, (fox_qkv[:, :, 1:3], lf, nsa_kv[:, :, :4], nsa_kv[:, T - w_keep:, 4:6],
               pool_u[:, T - POOL_BUF:], mem_kv)

def layer_sample(x, c_fox_kv, c_fox_lf, c_nsa_kv, s_win, s_pool, c_mem_kv, page_table, lw):
    g_n, w_in, b_f, pe, w1, w2, p_w, p_s, w_mkv, w_o = lw
    DB, DS, _ = x.shape
    past = page_table.shape[1] * PAGE_SIZE
    hn = rms_norm(x, g_n)
    fox_qkv, fox_f, nsa_q, nsa_kv, nsa_g, pool_u, mem_q, z = split_projection(
        jnp.einsum('btd,de->bte', hn, w_in))
    lf = jax.nn.log_sigmoid(fox_f.astype(F32) + b_f.astype(F32))
    fox_past = c_fox_kv[page_table].reshape(DB, past, 2, H_FOX, HEAD_DIM)
    lf_past = c_fox_lf[page_table].reshape(DB, past, H_FOX).astype(F32)
    k_all = jnp.concatenate([fox_past[:, :, 0], fox_qkv[:, :, 1]], axis=1)
    v_all = jnp.concatenate([fox_past[:, :, 1], fox_qkv[:, :, 2]], axis=1)
    c_all = jnp.cumsum(jnp.concatenate([lf_past, lf], axis=1), axis=1)
    qpos = past + jnp.arange(DS)
    o_a = fox_attention(fox_qkv[:, :, 0], qpos, c_all[:, past:], k_all, v_all,
                        jnp.arange(past + DS), c_all).reshape(DB, DS, H_FOX * HEAD_DIM)
    nsa_past = c_nsa_kv[page_table].reshape(DB, past, 4, G_NSA, HEAD_DIM)
    o_b, new_win = nsa_sample(nsa_q, nsa_kv, nsa_g, nsa_past, s_win, pe, w1, w2)
    u_ext = jnp.concatenate([s_pool, pool_u], axis=1)
    o_c = pool_mix(u_ext, past - POOL_BUF + jnp.arange(POOL_BUF + DS), DS, p_w, p_s)
    o_m = mem_attention(mem_q, c_mem_kv)
    y = mix_out(x, [o_a, o_b, o_c, o_m], z, w_o)
    return y, (fox_qkv[:, :, 1:3], lf, nsa_kv[:, :, :4], new_win, u_ext[:, u_ext.shape[1] - POOL_BUF:])

def setup_inputs(seed: int = 0) -> dict:
    key = jax.random.key(seed)
    k = jax.random.split(key, 24)
    n_pages = PAST_LEN // PAGE_SIZE
    n_used = DEC_BATCH * n_pages
    n_phys = n_used + max(1, n_used // 4)
    w_buf = min(NSA_WINDOW, PAST_LEN)

    def nrm(kk, shape, s=1.0):
        return s * jax.random.normal(kk, shape, F32)

    return {
        "x_prompt": nrm(k[0], (BATCH, SEQ, D_MODEL)),
        "x_sample": nrm(k[1], (DEC_BATCH, DEC_SEQ, D_MODEL)),
        "cache_fox_kv": nrm(k[2], (DEPTH, n_phys, PAGE_SIZE, 2, H_FOX, HEAD_DIM)),
        "cache_fox_lf": jax.nn.log_sigmoid(FGT_BIAS_MEAN + nrm(k[3], (DEPTH, n_phys, PAGE_SIZE, H_FOX))),
        "cache_nsa_kv": nrm(k[4], (DEPTH, n_phys, PAGE_SIZE, 4, G_NSA, HEAD_DIM)),
        "state_nsa_win": nrm(k[5], (DEPTH, DEC_BATCH, w_buf, 2, G_NSA, HEAD_DIM)),
        "state_pool": nrm(k[6], (DEPTH, DEC_BATCH, POOL_BUF, D_POOL)),
        "cache_mem_kv": nrm(k[7], (DEPTH, DEC_BATCH, N_MEM, 2, H_MEM, HEAD_DIM)),
        "page_table": jax.random.permutation(k[8], n_phys)[:n_used].reshape(DEC_BATCH, n_pages).astype(jnp.int32),
        "mem_prompt": nrm(k[9], (BATCH, N_MEM, D_MODEL)),
        "norm_g": 1.0 + nrm(k[10], (DEPTH, D_MODEL), 0.05),
        "w_in": nrm(k[11], (DEPTH, D_MODEL, D_IN), D_MODEL ** -0.5),
        "b_fgt": FGT_BIAS_MEAN + nrm(k[12], (DEPTH, H_FOX), 0.5),
        "nsa_pe": nrm(k[13], (DEPTH, 2, NSA_BLOCK, HEAD_DIM), 0.1),
        "nsa_w1": nrm(k[14], (DEPTH, 2, NSA_BLOCK * HEAD_DIM, NSA_CMP_HID), (NSA_BLOCK * HEAD_DIM) ** -0.5),
        "nsa_w2": nrm(k[15], (DEPTH, 2, NSA_CMP_HID, HEAD_DIM), (NSA_CMP_HID / 2.0) ** -0.5),
        "pool_w": nrm(k[16], (DEPTH, N_POOL_GROUPS, POOL_GW, POOL_GW), POOL_GW ** -0.5),
        "pool_scale": 1.0 + nrm(k[17], (DEPTH, D_POOL), 0.1),
        "w_mem_kv": nrm(k[18], (DEPTH, D_MODEL, 2 * D_MEMX), D_MODEL ** -0.5),
        "w_out": nrm(k[19], (DEPTH, D_MIX, D_MODEL), D_MIX ** -0.5),
        "final_g": 1.0 + nrm(k[20], (D_MODEL,), 0.05),
    }

def reference(x_prompt, x_sample, cache_fox_kv, cache_fox_lf, cache_nsa_kv, state_nsa_win,
              state_pool, cache_mem_kv, page_table, mem_prompt, norm_g, w_in, b_fgt, nsa_pe,
              nsa_w1, nsa_w2, pool_w, pool_scale, w_mem_kv, w_out, final_g):
    hp, hs = x_prompt, x_sample
    sp = [[] for _ in range(6)]
    ss = [[] for _ in range(5)]
    for l in range(DEPTH):
        lw = (norm_g[l], w_in[l], b_fgt[l], nsa_pe[l], nsa_w1[l], nsa_w2[l],
              pool_w[l], pool_scale[l], w_mem_kv[l], w_out[l])
        hp, st_p = layer_prompt(hp, mem_prompt, lw)
        hs, st_s = layer_sample(hs, cache_fox_kv[l], cache_fox_lf[l], cache_nsa_kv[l],
                                state_nsa_win[l], state_pool[l], cache_mem_kv[l], page_table, lw)
        for acc, s in zip(sp, st_p):
            acc.append(s)
        for acc, s in zip(ss, st_s):
            acc.append(s)
    y_prompt = rms_norm(hp, final_g)
    y_sample = rms_norm(hs, final_g)
    fox_kv_p = jnp.stack(sp[0])
    fox_lf_p = jnp.stack(sp[1])
    nsa_kv_p = jnp.stack(sp[2])
    nsa_win_p = jnp.stack(sp[3])
    pool_p = jnp.stack(sp[4])
    mem_kv_p = jnp.stack(sp[5])
    fox_kv_s = jnp.stack(ss[0])
    fox_lf_s = jnp.stack(ss[1])
    nsa_kv_s = jnp.stack(ss[2])
    nsa_win_s = jnp.stack(ss[3])
    pool_s = jnp.stack(ss[4])
    return (y_prompt, y_sample, fox_kv_p, fox_lf_p, nsa_kv_p, nsa_win_p, pool_p, mem_kv_p,
            fox_kv_s, fox_lf_s, nsa_kv_s, nsa_win_s, pool_s)


_drawn_inputs = setup_inputs


def setup_inputs(seed=0):
    import zlib

    import numpy as np

    out = dict(_drawn_inputs(seed))
    spreads = {}
    factors = {'cache_fox_lf': 4.847, 'nsa_pe': 4.883}
    for name, (base, spread) in spreads.items():
        noise = np.random.default_rng([zlib.crc32(name.encode()), seed]).standard_normal(out[name].shape)
        drawn = base * np.exp(spread * noise) if base else spread * noise
        out[name] = jnp.asarray(drawn.astype(out[name].dtype))
    for name, factor in factors.items():
        out[name] = (out[name] * factor).astype(out[name].dtype)
    return out
```

```python
from contextlib import ExitStack

import concourse.bass as bass
from concourse import mybir

F32 = mybir.dt.float32
F32R = mybir.dt.float32r
BF16 = mybir.dt.bfloat16
I32 = mybir.dt.int32
ALU = mybir.AluOpType
ACT = mybir.ActivationFunctionType
AX = mybir.AxisListType

P = 128
D = 1024
KC = D // P
T = 1024
NB = 8
TT = T + NB
NQ = T // P
H = 4
DH = 64
SCALE = DH ** -0.5
NEG = -1e30
EPS = 1e-6
PAST = 512
NPG = PAST // P
NMEM = 256
WIN_T = 512 // P
CH = TT // 3
BLK = 64
NCB = T // BLK
SCB = PAST // BLK
SLOPES = [2.0 ** (-8.0 * (h + 1) / H) for h in range(H)]
POOLW = (2, 4, 8, 16)
R_PROMPT = 2 * NCB
R_ALL = R_PROMPT + 2 * NB * SCB
NJ = BLK // 2

C_FOXQ, C_FOXK, C_FOXV, C_F = 0, 256, 512, 768
C_NSAQ, C_NSAKV, C_G, C_POOL, C_MEMQ, C_Z = 772, 1028, 1796, 1808, 2064, 2320

TILES = [("memk", 0, 0), ("memk", 1, 128), ("memv", 0, 256), ("memv", 1, 384),
         ("memq", 0, C_MEMQ), ("memq", 1, C_MEMQ + 128),
         ("gate", 0, C_F),
         ("foxq", 0, C_FOXQ), ("foxq", 1, C_FOXQ + 128), ("foxk", 0, C_FOXK), ("foxk", 1, C_FOXK + 128),
         ("foxv", 0, C_FOXV), ("foxv", 1, C_FOXV + 128),
         ("kc", 0, C_NSAKV), ("nsaq", 0, C_NSAQ), ("vc", 0, C_NSAKV + 128), ("nsaq", 1, C_NSAQ + 128),
         ("ks", 0, C_NSAKV + 256), ("vs", 0, C_NSAKV + 384), ("kw", 0, C_NSAKV + 512), ("vw", 0, C_NSAKV + 640),
         ("pool", 0, C_POOL), ("pool", 1, C_POOL + 128)]
TILES += [("z", j, C_Z + 128 * j) for j in range(8)]
NT = len(TILES)
AT = {(w, j): m for m, (w, j, _) in enumerate(TILES)}
DVE_TAKES = [sum(1 for w, _, _ in TILES[:m] if w not in ("z", "gate")) for m in range(NT + 1)]
VSI = {("foxv", 0): 0, ("foxv", 1): 1, ("kc", 0): 2, ("vc", 0): 3, ("vs", 0): 4, ("vw", 0): 5,
       ("pool", 0): 6, ("pool", 1): 7}
KNI = {"foxk": 0, "ks": 4, "kw": 6}
QNI = {"foxq": 0, "nsaq": 4, "memq": 8}
O_SLOT = [0, 2, 3, 1]


def attention_units():
    order = [7, 0, 6, 1, 5, 2, 4, 3]
    mem = [("mem", h, i, 0, NMEM // P) for i in range(NQ) for h in range(H)]
    fox = [("fox", h, i, 0, i + 1) for i in order for h in range(H)]
    sel = [("sel", h, i, 0, i + 1) for i in order for h in range(H)]
    win = [("win", h, i, max(0, i - WIN_T), min(i, WIN_T) + 1) for i in order for h in range(H)]
    both = [u for a, b in zip(sel, win) for u in (a, b)]
    return mem, fox, both


MEM_U, FOX_U, NSA_U = attention_units()
UNITS = MEM_U + FOX_U + NSA_U
G0 = [0]
for _u in UNITS:
    G0.append(G0[-1] + (_u[4] + 3) // 4)


STEPS = [("item", 0), ("item", 1), ("item", 2), ("item", 3), ("project", 0), ("item", 4),
         ("project", 1), ("natural", 0), ("item", 5), ("project", 2), ("natural", 1), ("item", 6),
         ("project", 3), ("natural", 2), ("item", 7), ("natural", 3), ("item", 8), ("item", 9), ("item", 10),
         ("project", 4), ("project", 5), ("project", 6), ("attend", 0),
         ("gates", 0), ("project", 7), ("forget", 0), ("project", 8), ("pair", 0), ("project", 9), ("pair", 1),
         ("project", 10), ("natural", 9), ("pair", 2), ("project", 11), ("natural", 10), ("pair", 3),
         ("project", 12), ("natural", 11), ("pair", 4), ("natural", 12), ("pair", 5), ("pair", 6), ("pair", 7),
         ("attend", 1),
         ("project", 13), ("project", 14), ("natural", 13), ("compress", 0), ("project", 15), ("pair", 8), ("pair", 9),
         ("pair", 10), ("pair", 11), ("project", 16), ("natural", 15), ("pair", 12), ("pair", 13), ("pair", 14), ("pair", 15),
         ("compress", 1), ("project", 17), ("cmp_scores", 0), ("project", 18), ("natural", 17), ("project", 19),
         ("natural", 18), ("cmp_turn", 0), ("project", 20), ("natural", 19), ("cmp_out", 0), ("natural", 20),
         ("attend", 2),
         ("project", 21), ("pool_last", 0), ("project", 22), ("pool_last", 1), ("project", 23), ("project", 24),
         ("pool_map", 0), ("project", 25), ("project", 26), ("pool_map", 1)] + [
         ("project", m) for m in range(27, 31)] + [
         ("sample_new", 0), ("sample_keys", 0), ("sample_values", 0), ("mix", 0)]
PHASE = [(0, len(MEM_U)), (len(MEM_U), len(MEM_U) + len(FOX_U)), (len(MEM_U) + len(FOX_U), len(UNITS))]


def even(g):
    return (g + 1) // 2


def odd(g):
    return g // 2


def build(nc, x_p, x_s, c_fox, c_lf, c_nsa, st_win, st_pool, c_mem, ptab, mem_p, norm_g, w_in, b_f, pe_, w1,
          w2, pool_w, pool_s, w_mem, w_out, fin_g,
          y_p, y_s, o_foxkv, o_lf, o_nsakv, o_nsawin, o_pool, o_memkv, o_foxkv_s, o_lf_s, o_nsakv_s, o_win_s,
          o_pool_s):
    with ExitStack() as ctx:
        def sb(name, shape, dt=F32):
            return ctx.enter_context(nc.sbuf_tensor(name, shape, dt))

        def sem(name):
            return ctx.enter_context(nc.semaphore(name))

        ctx.enter_context(nc.allow_non_contiguous_dma(reason="small strided rows"))

        HH = sb("HH", [P, KC * TT], F32R)
        HL = sb("HL", [P, KC * TT], F32R)
        WR = sb("WR", [P, 2, KC, P])
        WH = sb("WH", [P, 2, KC, P], F32R)
        WL = sb("WL", [P, 2, KC, P], F32R)
        AUG = sb("AUG", [P, 8, TT])
        XT = sb("XT", [P, TT])
        NAT = sb("NAT", [P, NQ * 512])
        VW = sb("VW", [P, NQ * P])
        KW = sb("KW", [P, 4 * P])
        PP = sb("PP", [P, 4 * 1024])
        OB = sb("OB", [P, 4096 + NJ * (R_ALL + 1)])
        ident = sb("ident", [P, P])
        identb = sb("identb", [P, P], BF16)
        m_diag = sb("m_diag", [P, P], BF16)
        m_win = sb("m_win", [P, P], BF16)
        m_cmp = sb("m_cmp", [P, NQ, NCB], BF16)
        seen0 = sb("seen0", [P, NCB])
        lf = sb("lf", [P, NQ + 1, H])
        fga = sb("fga", [P, NQ + 1, 16])
        bfb = sb("bfb", [P, H])
        stat = sb("stat", [P, 16])
        rms = sb("rms", [P, 32])
        epsc = sb("epsc", [P, 1])
        QKN = sb("QKN", [P, 12, NB])
        QNs, KNs = QKN[0:DH], QKN[DH:P, 0:8]
        VS = sb("VS", [P, 8, NB])
        KCa = sb("KCa", [DH + 2, 2, NCB])
        KCs = sb("KCs", [P, NB * SCB])
        VCP = sb("VCP", [96, 2 * P])
        VCs = VCP[0:NB * SCB, 0:P]
        pes = VCP[64:96, :].rearrange("p (k c) -> p k c", k=2)
        W2 = sb("W2", [P, 2, 2, DH])
        PLW = sb("PLW", [P, 2, DH])
        PLT = sb("PLT", [P, 2, NB])
        rcnt = sb("rcnt", [P, 2, 16])
        peb = sb("peb", [P, 2])
        cs = sb("cs", [P, 96])
        onesc = sb("onesc", [P, 1])
        SLC = sb("SLC", [P, 1])
        BC = sb("BC", [P, SCB])
        GC = sb("GC", [P, 2])
        E8 = sb("E8", [P, NB])
        XC = cs
        ptb = sb("ptb", [1, NB * NPG], I32)
        oTs = VS

        PLS = OB[:, 7168:7296].rearrange("p (j c) -> p j c", j=2)
        slope_row = OB[:, 7296:7424]
        FG = OB[:, 7424:7424 + (NQ + 1) * 16].rearrange("p (t c) -> p t c", t=NQ + 1)

        hh = HH[:, 0:KC * TT].rearrange("p (k t) -> p k t", k=KC)
        hl = HL[:, 0:KC * TT].rearrange("p (k t) -> p k t", k=KC)
        woh = HH[:, 0:KC * D].rearrange("p (k t) -> p k t", k=KC)
        wol = HL[:, 0:KC * D].rearrange("p (k t) -> p k t", k=KC)
        mth, mtl = hh[:, :, T - NMEM:T], hl[:, :, T - NMEM:T]
        TH = WH[:, :, :, :].rearrange("p s k c -> p (s k c)")
        TL = WL[:, :, :, :].rearrange("p s k c -> p (s k c)")
        nat = NAT[:, :].rearrange("p (t c) -> p t c", t=NQ)
        vw = VW[:, :].rearrange("p (t c) -> p t c", t=NQ)
        kw = KW[:, :].rearrange("p (t c) -> p t c", t=4)
        o_nat = OB[:, 0:8192].rearrange("p (g t c) -> p g t c", g=4, t=NQ)
        FT = OB[:, 4096:4096 + NJ * (R_ALL + 1)].rearrange("p (j r) -> p j r", j=NJ)
        xr = OB[:, 0:4096].rearrange("p (s c) -> p s c", s=4)
        xn = OB[:, 4096:6144].rearrange("p (s c) -> p s c", s=2)
        gbc = OB[:, 6144:7168]

        def pair_slot(q):
            if q < 16:
                where = PP[:, q * 256:(q + 1) * 256]
            elif 20 <= q < 28:
                where = NAT[:, (q - 20) * 512 + 256:(q - 19) * 512]
            else:
                where = VW[:, q % 4 * 256:(q % 4 + 1) * 256]
            return where.rearrange("p (a c) -> p a c", a=2)

        w1s = PP[:, :].rearrange("p (s j e) -> p s j e", s=2, j=8)
        HS = KW[:, 0:2 * R_ALL].rearrange("p (a r) -> p a r", a=2)

        PS = ctx.enter_context(nc.psum_tensor("PS", [P, 8, 512], F32))

        def bk(i):
            return PS[:, i, :]

        def flat(b0, blocks):
            return PS[:, b0:b0 + 2, :].rearrange("p a c -> p (a c)")[:, 0:blocks * P]

        G2 = NAT[:, 0:2048].rearrange("p (s c) -> p s c", s=2)
        gf = NAT[:, 2048:3072]
        XN8 = XC[:, 80:88]

        def ft_cols(n):
            return FT[:, :, R_PROMPT:R_ALL].rearrange("p j (g b n) -> p b g n j", g=2, b=NB)[:, n]

        def ft_prompt(par, g):
            return FT[par * DH:(par + 1) * DH, :, g * NCB:(g + 1) * NCB].rearrange("p j n -> p n j")

        def xt_pairs(par, g):
            return XT[g * DH:(g + 1) * DH, 0:T].rearrange("p (n j r) -> p r n j", n=NCB, r=2)[:, par]

        def nat_place(what, j):
            return {"memk": (nat, P * j), "memv": (nat, 256 + P * j), "foxk": (nat, P * j),
                    "foxv": (nat, 256 + P * j), "kc": (nat, 0), "vc": (nat, P), "ks": (nat, 256),
                    "vs": (nat, 384), "kw": (kw, 0), "vw": (vw, 0)}[what]

        def nat_free(eng, m):
            if m == 9:
                eng.wait_ge(s_nst, 16)
            if m == 13:
                eng.wait_ge(s_nst, 32)

        def xt_free(eng, m):
            if m in (AT["foxv", 0], AT["foxv", 1]):
                a, d = mark["natural", 11] if m == 12 else mark["gates", 0]
                eng.wait_ge(s_TA, a)
                eng.wait_ge(s_TD, d)

        s_x = [sem(f"s_x{i}") for i in range(4)]
        s_gb = sem("s_gb")
        s_std = sem("s_std")
        s_sq = sem("s_sq")
        s_xn = sem("s_xn")
        s_itT = sem("s_itT")
        s_hi = sem("s_hi")
        s_lo = sem("s_lo")
        s_w = [sem(f"s_w{i}") for i in range(2)]
        s_wcp = sem("s_wcp")
        s_split = sem("s_split")
        s_proj = sem("s_proj")
        s_eva = sem("s_eva")
        s_evd = sem("s_evd")
        s_TA = sem("s_TA")
        s_TD = sem("s_TD")
        s_fA = sem("s_fA")
        s_fD = sem("s_fD")
        s_S = sem("s_S")
        s_nm = sem("s_nm")
        s_P = sem("s_P")
        s_pT = sem("s_pT")
        s_cD = sem("s_cD")
        s_cA = sem("s_cA")
        s_pv = sem("s_pv")
        s_on = sem("s_on")
        s_cst = sem("s_cst")
        s_pc = sem("s_pc")
        s_pb = sem("s_pb")
        s_v = sem("s_v")
        s_a = sem("s_a")
        s_fgv = sem("s_fgv")
        s_fga = sem("s_fga")
        s_c = sem("s_c")
        s_aug = sem("s_aug")
        s_st = sem("s_st")
        s_nst = sem("s_nst")
        s_pair = [sem(f"s_pair{n}") for n in range(NB)]
        s_w1 = [sem(f"s_w1{i}") for i in range(2)]
        s_w1u = sem("s_w1u")
        s_fta = sem("s_fta")
        s_ftd = sem("s_ftd")
        s_hs = sem("s_hs")
        s_cm = sem("s_cm")
        s_cma = sem("s_cma")
        s_cmv = sem("s_cmv")
        s_pd = sem("s_pd")
        s_kv = [sem(f"s_kv{i}") for i in range(4)]
        s_lfp = sem("s_lfp")
        s_sd = sem("s_sd")
        s_sS = sem("s_sS")
        s_vr = sem("s_vr")
        s_oT = sem("s_oT")
        s_g = sem("s_g")
        s_gh = sem("s_gh")
        s_gl = sem("s_gl")
        s_y = sem("s_y")
        s_y1 = sem("s_y1")
        s_ys = sem("s_ys")
        s_yo = sem("s_yo")
        s_yst = [sem(f"s_yst{i}") for i in range(2)]
        s_xf = [sem(f"s_xf{i}") for i in range(2)]
        s_pt = sem("s_pt")
        s_wg = sem("s_wg")
        s_lf = sem("s_lf")
        s_gate = sem("s_gate")
        s_qz = sem("s_qz")
        s_psum = sem("s_psum")
        s_psd = sem("s_psd")
        s_stp = sem("s_stp")
        s_lfr = sem("s_lfr")
        s_sx = sem("s_sx")
        s_se = sem("s_se")
        s_px = sem("s_px")
        s_gf = sem("s_gf")

        ring = PP[:, :].rearrange("p (s c) -> p s c", s=4)
        KTA = NAT[:, 0:1024].rearrange("p (s c) -> p s c", s=2)
        KTD = NAT[:, 1024:2048].rearrange("p (s c) -> p s c", s=2)
        QZF = NAT[:, 2048:2560].rearrange("p (a b r) -> p a b r", a=2, b=NB)
        QZM = NAT[:, 2560:3072].rearrange("p (a b r) -> p a b r", a=2, b=NB)
        QZN = NAT[:, 3072:3328].rearrange("p (b r) -> p b r", b=NB)
        KNF = NAT[:, 3328:3344].rearrange("p (a b) -> p a b", a=2)
        KNS = NAT[:, 3344:3352]
        KNW = NAT[:, 3352:3360]
        PTs = NAT[:, 3360:3872].rearrange("p (g r) -> p g r", g=NPG)
        PTn = NAT[0:NB, 3872:4000]
        PTc = NAT[0:NB * SCB, 4000:4032]
        VNEW = VW[0:NB, :]
        KNEW = KW[64:64 + NB, :]
        LFP = KW[0:32, :]
        LFR = XT[0:32, 516:516 + PAST]
        LFT = XT[32:64, 516:516 + PAST + 1]
        CT = XT[64:96, 516:516 + PAST + 1]
        BIAS = XT[:, 0:PAST + 1]
        OT0 = 4096 + 4096
        X = OB[:, OT0:OT0 + PAST + 1]
        poolp = OB[0:15, OT0 + 520:OT0 + 776]
        PSUMS = OB[0:NB, OT0 + 776:OT0 + 1032]
        STP = [PP[0:NB, 3152:3216], PP[0:NB, 3216:3408], PP[0:NB, 3408:3856], NAT[0:NB, 3096:4056]]
        POOLD = NAT[:, 0:2048].rearrange("p (j t) -> p j t", j=2)

        block = ctx.enter_context(nc.Block())
        mark = {}

        @block.tensor
        def _(pe):
            mm, tr = nc.tensor.matmul, nc.tensor.transpose
            nA, nD = [0], [0]

            def job_a():
                if nA[0]:
                    pe.wait_ge(s_fA, nA[0])
                nA[0] += 1
                return bk(6)

            def job_d():
                if nD[0]:
                    pe.wait_ge(s_fD, nD[0])
                nD[0] += 1
                return bk(7)

            def jobs_taken():
                pe.wait_ge(s_fA, nA[0])
                pe.wait_ge(s_fD, nD[0])

            def item(i):
                rows = NB if i == 10 else P
                if i < 2:
                    pe.wait_ge(s_x[i % 4], 16)
                    src = xr[:, i % 4, :]
                else:
                    pe.wait_ge(s_xn, i - 1)
                    src = xn[0:rows, i % 2, :]
                if i >= 2:
                    pe.wait_ge(s_lo, i - 1)
                for k in range(KC):
                    last = tr(bk(2 * (i % 2) + k // 4)[:, (k % 4) * P:(k % 4) * P + rows],
                              src[:, k * P:(k + 1) * P], ident[0:rows, 0:rows])
                last.then_inc(s_itT, 1)

            def passes(out, lhs, rhs, k):
                mm(out, lhs[0], rhs[0], start=(k == 0), stop=False)
                mm(out, lhs[0], rhs[1], start=False, stop=False)
                return mm(out, lhs[1], rhs[0], start=False, stop=(k == KC - 1))

            def project(m):
                what = TILES[m][0]
                s = m % 2
                pe.wait_ge(s_split, m + 1)
                if m >= 2:
                    pe.wait_ge(s_eva, m - 1)
                    pe.wait_ge(s_evd, DVE_TAKES[m - 1])
                if what in ("memk", "memv"):
                    for k in range(KC):
                        last = passes(bk(4 + s)[:, 0:NMEM], (WH[:, s, k, :], WL[:, s, k, :]),
                                      (mth[:, k, :], mtl[:, k, :]), k)
                else:
                    for c in range(3):
                        for k in range(KC):
                            t = slice(c * CH, (c + 1) * CH)
                            last = passes(bk(3 * s + c)[:, 0:CH], (WH[:, s, k, :], WL[:, s, k, :]),
                                          (hh[:, k, t], hl[:, k, t]), k)
                last.then_inc(s_proj, 1)

            def taken(m):
                pe.wait_ge(s_eva, m + 1)
                pe.wait_ge(s_evd, DVE_TAKES[m + 1])

            def natural(m):
                what = TILES[m][0]
                taken(m)
                halves = {"memk": ((0,), (1,)), "memv": ((0,), (1,)), "kw": ((4, 5), (6, 7))}.get(
                    what, (range(4), range(4, 8)))
                for side, tiles in enumerate(halves):
                    out = job_a() if side == 0 else job_d()
                    for n, t in enumerate(tiles):
                        if what in ("memk", "foxk", "ks", "kw"):
                            slot = 4 + {"memk": 2 * TILES[m][1], "foxk": 2 * TILES[m][1], "ks": 0, "kw": 2}[what]
                            for a in range(2):
                                last = tr(out[:, n * P + a * DH:n * P + a * DH + DH],
                                          AUG[0:DH, slot + a, t * P:(t + 1) * P], ident[0:DH, 0:DH])
                        else:
                            last = tr(out[:, n * P:(n + 1) * P], XT[:, t * P:(t + 1) * P], ident[:, :])
                    last.then_inc(s_TA if side == 0 else s_TD, 1)

            def scores(u):
                what, h, i, k0, nk = UNITS[u]
                rows = DH if what == "mem" else DH + 2
                slot = {"mem": 4 + h, "fox": 4 + h, "sel": 4 + h // 2, "win": 6 + h // 2}[what]
                if u >= 2:
                    pe.wait_ge(s_P, u - 1)
                s0 = 2 * (u % 2)
                masks = {}
                if what != "mem":
                    masks[nk - 1] = m_diag
                if what == "win" and i >= WIN_T:
                    masks[0] = m_win
                for c in range(0, nk, 4):
                    n = min(4, nk - c)
                    inside = [b for b in masks if c <= b < c + n]
                    last = mm(bk(s0 + c // 4)[:, 0:n * P], AUG[0:rows, h, i * P:(i + 1) * P],
                              AUG[0:rows, slot, (k0 + c) * P:(k0 + c + n) * P], start=True, stop=not inside)
                    for b in inside:
                        last = mm(bk(s0 + c // 4)[:, (b - c) * P:(b - c + 1) * P], identb[:, :], masks[b][:, :],
                                  start=False, stop=(b == inside[-1]))
                last.then_inc(s_S, 1)

            def transpose_p(u):
                nk = UNITS[u][4]
                pe.wait_ge(s_P, u + 1)
                for c in range(0, nk, 4):
                    g = G0[u] + c // 4
                    if g >= 2:
                        pe.wait_ge(s_cA if g % 2 else s_cD, odd(g - 1) if g % 2 else even(g - 1))
                    for b in range(c, min(c + 4, nk)):
                        last = tr(bk(4 + g % 2)[:, (b - c) * P:(b - c + 1) * P],
                                  PP[:, (u % 2) * 1024 + b * P:(u % 2) * 1024 + (b + 1) * P], ident[:, :])
                    last.then_inc(s_pT, 1)

            def weigh_v(u):
                what, h, i, k0, nk = UNITS[u]
                if even(G0[u + 1]):
                    pe.wait_ge(s_cD, even(G0[u + 1]))
                if odd(G0[u + 1]):
                    pe.wait_ge(s_cA, odd(G0[u + 1]))
                if u >= 2:
                    pe.wait_ge(s_on, u - 1)
                for b in range(nk):
                    t = k0 + b
                    v = {"mem": nat[:, t, 256 + h * DH:256 + (h + 1) * DH],
                         "fox": nat[:, t, 256 + h * DH:256 + (h + 1) * DH],
                         "sel": nat[:, t, 384 + (h // 2) * DH:384 + (h // 2 + 1) * DH],
                         "win": vw[:, t, (h // 2) * DH:(h // 2 + 1) * DH]}[what]
                    last = mm(bk(6 + u % 2)[:, 0:DH],
                              PP[:, 2048 + (u % 2) * 1024 + b * P:2048 + (u % 2) * 1024 + (b + 1) * P], v,
                              start=(b == 0), stop=(b == nk - 1))
                last.then_inc(s_pv, 1)

            def attend(u0, u1):
                pe.wait_ge(s_fA, nA[0])
                pe.wait_ge(s_fD, nD[0])
                scores(u0)
                scores(u0 + 1)
                for u in range(u0, u1):
                    transpose_p(u)
                    if u > u0:
                        weigh_v(u - 1)
                    if u + 2 < u1:
                        scores(u + 2)
                weigh_v(u1 - 1)
                pe.wait_ge(s_on, u1)
                if even(G0[u1]):
                    pe.wait_ge(s_cD, even(G0[u1]))
                if odd(G0[u1]):
                    pe.wait_ge(s_cA, odd(G0[u1]))

            def pair_job(n, kind):
                out = job_a() if n % 2 == 0 else job_d()
                pe.wait_ge(s_pair[n], 128 * (kind + 1))
                for a in range(2):
                    q = 16 * kind + 2 * n + a
                    for g in range(2):
                        last = tr(out[:, (2 * g + a) * P:(2 * g + a + 1) * P],
                                  pair_slot(q)[:, g, :], ident[:, :])
                last.then_inc(s_TA if n % 2 == 0 else s_TD, 1)
                mark["pair", kind, n] = (s_TA, nA[0]) if n % 2 == 0 else (s_TD, nD[0])

            def compress(kind):
                out = job_d()
                tr(out[:, 0:NJ], pes[:, kind, :], ident[64:96, 64:96]).then_inc(s_TD, 1)
                jobs_taken()
                pe.wait_ge(s_fta, kind + 1)
                pe.wait_ge(s_ftd, kind + 1)
                for c in range(4):
                    n = 4 * kind + c
                    pe.wait_ge(s_w1[n % 2], 16 * (n // 2 + 1))
                    for jj in range(8):
                        j = 8 * c + jj
                        for e in range(2):
                            last = mm(bk(3 + e)[:, 0:R_ALL + 1], w1s[:, n % 2, jj, e * P:(e + 1) * P], FT[:, j, :],
                                      start=(j == 0), stop=(j == NJ - 1))
                    last.then_inc(s_w1u, 1)

            def compress_out(kind):
                pe.wait_ge(s_hs, kind + 1)
                if kind == 0:
                    out = job_a()
                    for a in range(2):
                        mm(out[0:DH, 0:R_PROMPT], W2[:, 0, a, :], HS[:, a, 0:R_PROMPT], start=(a == 0), stop=(a == 1))
                    for g in range(2):
                        c0 = R_PROMPT + g * NB * SCB
                        for a in range(2):
                            last = mm(out[g * DH:(g + 1) * DH, 64:64 + NB * SCB], W2[:, 0, a, :],
                                      HS[:, a, c0:c0 + NB * SCB], start=(a == 0), stop=(a == 1))
                    last.then_inc(s_TA, 1)
                else:
                    out = job_d()
                    for h in range(H):
                        g = h // 2
                        for a in range(2):
                            mm(out[32 * h:32 * h + NCB, h * DH:(h + 1) * DH], HS[:, a, g * NCB:(g + 1) * NCB],
                               W2[:, 1, a, :], start=(a == 0), stop=(a == 1))
                    for g in range(2):
                        c0 = R_PROMPT + g * NB * SCB
                        for a in range(2):
                            last = mm(out[0:NB * SCB, 256 + g * DH:256 + (g + 1) * DH], HS[:, a, c0:c0 + NB * SCB],
                                      W2[:, 1, a, :], start=(a == 0), stop=(a == 1))
                    last.then_inc(s_TD, 1)

            def gates():
                taken(6)
                out = job_d()
                for t in range(NQ + 1):
                    rows = NB if t == NQ else P
                    last = tr(out[0:rows, t * 16:(t + 1) * 16], XT[0:16, t * P:t * P + rows], ident[0:16, 0:16])
                last.then_inc(s_TD, 1)

            def forget_t():
                pe.wait_ge(s_lf, 1)
                for half in range(2):
                    out = job_d()
                    for t in range(4):
                        last = tr(out[0:H, t * P:(t + 1) * P], lf[:, 4 * half + t, :], ident[:, :])
                    last.then_inc(s_TD, 1)

            def cmp_scores():
                pe.wait_ge(s_aug, 48)
                jobs_taken()
                taken(16)
                out = job_d()
                for i in range(NQ):
                    for h in range(H):
                        last = mm(out[:, (4 * i + h) * NCB:(4 * i + h + 1) * NCB],
                                  AUG[0:DH + 2, h, i * P:(i + 1) * P], KCa[:, h // 2, :], start=True, stop=True)
                last.then_inc(s_TD, 1)

            def cmp_turn():
                pe.wait_ge(s_cm, 1)
                for half in range(2):
                    out = job_a() if half == 0 else job_d()
                    for t in range(4 * half, 4 * half + 4):
                        last = tr(out[:, (t % 4) * P:(t % 4 + 1) * P], PP[:, 1024 + t * P:1024 + (t + 1) * P], ident[:, :])
                    last.then_inc(s_TA if half == 0 else s_TD, 1)

            def cmp_out():
                jobs_taken()
                for q in range(4):
                    out = job_a() if q % 2 == 0 else job_d()
                    for a in range(2):
                        i = 2 * q + a
                        last = mm(out[:, a * 256:(a + 1) * 256], PP[:, 2048 + i * P:2048 + (i + 1) * P],
                                  PP[:, 3072:3072 + 256], start=True, stop=True)
                    last.then_inc(s_TA if q % 2 == 0 else s_TD, 1)

            def pool_last(j):
                taken(21 + j)
                out = job_d()
                tr(out[0:15, 0:P], PP[:, j * 1056 + T:j * 1056 + T + 15], ident[:, :]).then_inc(s_TD, 1)

            def pool_map(j):
                pe.wait_ge(s_pd, j + 1)
                for half in range(2):
                    for a in range(2):
                        out = job_a() if a == 0 else job_d()
                        for n in range(4):
                            t = 4 * half + n
                            last = mm(out[:, n * DH:(n + 1) * DH], POOLD[a * DH:(a + 1) * DH, j, t * P:(t + 1) * P],
                                      PLW[a * DH:(a + 1) * DH, j, :], start=True, stop=True)
                        last.then_inc(s_TA if a == 0 else s_TD, 1)

            def sample_new():
                for q in range(2):
                    out = job_a() if q == 0 else job_d()
                    for n in range(4):
                        last = tr(out[0:NB, n * P:(n + 1) * P], VS[:, 4 * q + n, :], ident[:, :])
                    last.then_inc(s_TA if q == 0 else s_TD, 1)
                out = job_a()
                for n in range(8):
                    last = tr(out[0:NB, n * DH:(n + 1) * DH], KNs[:, n, :], ident[DH:P, DH:P])
                last.then_inc(s_TA, 1)

            JOBS = [("A", 0, [(pg, 0) for pg in range(4)]), ("D", 0, [(pg, 1) for pg in range(4)]),
                    ("A", 1, [(pg, 0) for pg in range(4)]), ("D", 2, [(pg, 0) for pg in range(4)]),
                    ("A", 3, [(pg, a) for a in range(2) for pg in range(2)])]
            NTH = [0, 0, 1, 1, 2]

            def keys_t(b, jn):
                side, br, blocks = JOBS[jn]
                width = 256 if br in (0, 3) else P
                pe.wait_ge(s_kv[br], (64 if br in (0, 1) else 16) * (b + 1))
                out = job_a() if side == "A" else job_d()
                for n, (pg, a) in enumerate(blocks):
                    last = tr(out[:, n * P:(n + 1) * P], ring[:, br, pg * width + a * P:pg * width + a * P + P],
                              ident[:, :])
                last.then_inc(s_TA if side == "A" else s_TD, 1)

            def key_scores(b, jn):
                side, br, _ = JOBS[jn]
                n = (3 if side == "A" else 2) * b + NTH[jn]
                if side == "A":
                    pe.wait_ge(s_fA, mark["K"][0] + n + 1)
                else:
                    pe.wait_ge(s_fD, mark["K"][1] + n + 1)
                kt = (KTA if side == "A" else KTD)[:, n % 2, :]
                rows = slice(32 * br, 32 * br + 32)
                if br == 0:
                    a = jn
                    last = mm(PS[rows, 0, :], QZF[:, a, b, :], kt, start=(b == 0 and a == 0),
                              stop=(b == NB - 1 and a == 1))
                elif br == 3:
                    for a in range(2):
                        last = mm(PS[rows, 0, 0:256], QZM[:, a, b, :], kt[:, a * 256:(a + 1) * 256],
                                  start=(b == 0 and a == 0), stop=(b == NB - 1 and a == 1))
                else:
                    last = mm(PS[rows, 0, :], QZN[:, b, :], kt, start=(b == 0), stop=(b == NB - 1))
                last.then_inc(s_sS, 1)

            def sample_keys():
                jobs_taken()
                taken(NT - 1)
                pe.wait_ge(s_qz, 1)
                mark["K"] = (nA[0], nD[0])
                for b in range(NB):
                    for jn in range(5):
                        keys_t(b, jn)
                        if jn:
                            key_scores(b, jn - 1)
                    key_scores(b, 4)
                for b in range(NB):
                    for a in range(2):
                        mm(PS[0:32, 4, 0:1], QZF[:, a, b, :], KNF[:, a, b:b + 1], start=(b == 0 and a == 0),
                           stop=(b == NB - 1 and a == 1))
                for b in range(NB):
                    mm(PS[32:64, 4, 0:1], QZN[:, b, :], KNS[:, b:b + 1], start=(b == 0), stop=(b == NB - 1))
                for b in range(NB):
                    mm(PS[64:96, 4, 0:1], QZN[:, b, :], KNW[:, b:b + 1], start=(b == 0), stop=(b == NB - 1))
                for b in range(NB):
                    last = mm(PS[0:32, 5, 0:SCB], QZN[:, b, :], KCs[:, b * SCB:(b + 1) * SCB], start=(b == 0),
                              stop=(b == NB - 1))
                last.then_inc(s_sS, 1)

            def sample_values():
                pe.wait_ge(s_px, 1)
                out = job_a()
                for pg in range(NPG):
                    last = tr(out[:, pg * P:(pg + 1) * P], X[:, pg * P:(pg + 1) * P], ident[:, :])
                last.then_inc(s_TA, 1)
                out = job_d()
                tr(out[0:NB, 0:P], XN8[:, :], ident[:, :])
                tr(out[0:NB * SCB, P:P + 32], XC[0:32, 16:16 + NB * SCB], ident[0:32, 0:32]).then_inc(s_TD, 1)
                pe.wait_ge(s_psd, 1)
                out = job_a()
                for j in range(2):
                    last = tr(out[:, j * NB:(j + 1) * NB], PSUMS[:, j * P:(j + 1) * P], ident[0:NB, 0:NB])
                last.then_inc(s_TA, 1)
                jobs_taken()
                mm(bk(0)[:, 0:32], VNEW[:, 0:P], PTn[:, 0:32], start=True, stop=False)
                mm(bk(3)[:, 0:32], VNEW[:, P:2 * P], PTn[:, 0:32], start=True, stop=False)
                mm(bk(1)[:, 0:32], VNEW[:, 4 * P:5 * P], PTn[:, 32:64], start=True, stop=False)
                mm(bk(1)[:, 0:32], VNEW[:, 5 * P:6 * P], PTn[:, 64:96], start=False, stop=False)
                mm(bk(1)[:, 0:32], VCs[:, :], PTc, start=False, stop=False)
                for b in range(NB):
                    for br in range(4):
                        pe.wait_ge(s_kv[br], (64 if br in (0, 1) else 16) * (NB + b + 1))
                        npg = 2 if br == 3 else 4
                        for pg in range(npg):
                            if br in (0, 3):
                                for a in range(2):
                                    c = 4 * b + 2 * a
                                    dst = bk({(0, 0): 0, (0, 1): 3, (3, 0): 2, (3, 1): 4}[br, a])[:, c:c + 2]
                                    last = mm(dst, ring[:, br, pg * 256 + a * P:pg * 256 + a * P + P],
                                              PTs[:, pg, 32 * br + c:32 * br + c + 2], start=(br == 3 and pg == 0),
                                              stop=(pg == npg - 1 and (br == 3 or b == NB - 1)))
                            else:
                                last = mm(bk(1)[:, 4 * b:4 * b + 4], ring[:, br, pg * P:(pg + 1) * P],
                                          PTs[:, pg, 32 * br + 4 * b:32 * br + 4 * b + 4], start=False,
                                          stop=(pg == 3 and br == 2 and b == NB - 1))
                        last.then_inc(s_vr, 1)
                out = job_d()
                for j in range(2):
                    for a in range(2):
                        last = mm(out[a * DH:(a + 1) * DH, j * NB:(j + 1) * NB], PLW[a * DH:(a + 1) * DH, j, :],
                                  PLT[a * DH:(a + 1) * DH, j, :], start=True, stop=True)
                last.then_inc(s_TD, 1)

            def turn(t):
                if t >= 2:
                    pe.wait_ge(s_g, t - 1)
                for c in range(KC):
                    last = tr(bk(4 + 2 * (t % 2) + c // 4)[:, (c % 4) * P:(c % 4 + 1) * P],
                              o_nat[:, O_SLOT[c // 2], t, (c % 2) * P:(c % 2 + 1) * P], ident[:, :])
                last.then_inc(s_oT, 1)

            def mix():
                jobs_taken()
                turn(0)
                pe.wait_ge(s_split, NT + KC)
                for t in range(NQ + 1):
                    if t + 1 < NQ:
                        turn(t + 1)
                    pe.wait_ge(s_gl, t + 1)
                    if t >= 2:
                        pe.wait_ge(s_y1, t - 1)
                    s = t % 2
                    for half in range(2):
                        for k in range(KC):
                            sl = slice(s * 1024 + k * P, s * 1024 + (k + 1) * P)
                            c = slice(half * 512, (half + 1) * 512)
                            last = passes(bk(2 * s + half), (TH[:, sl], TL[:, sl]), (woh[:, k, c], wol[:, k, c]), k)
                    last.then_inc(s_y, 1)

            for step, n in STEPS:
                if step == "item":
                    if n == 0:
                        pe.wait_ge(s_pc, 1)
                    item(n)
                elif step == "project":
                    if n == 0:
                        pe.wait_ge(s_lo, 2)
                    if n == 4:
                        pe.wait_ge(s_lo, 11)
                    project(n)
                elif step == "natural":
                    natural(n)
                elif step == "pair":
                    pair_job(n % 8, n // 8)
                elif step == "attend":
                    if n == 0:
                        taken(6)
                        attend(0, len(MEM_U))
                    elif n == 1:
                        taken(12)
                        pe.wait_ge(s_aug, 32)
                        attend(len(MEM_U), len(MEM_U) + len(FOX_U))
                    else:
                        taken(20)
                        attend(len(MEM_U) + len(FOX_U), len(UNITS))
                elif step == "gates":
                    gates()
                elif step == "forget":
                    forget_t()
                elif step == "compress":
                    compress(n)
                    compress_out(n)
                elif step == "cmp_scores":
                    cmp_scores()
                elif step == "cmp_turn":
                    cmp_turn()
                elif step == "cmp_out":
                    cmp_out()
                elif step == "pool_last":
                    pool_last(n)
                elif step == "pool_map":
                    pool_map(n)
                elif step == "sample_new":
                    sample_new()
                elif step == "sample_keys":
                    sample_keys()
                elif step == "sample_values":
                    sample_values()
                elif step == "mix":
                    mix()
                mark[step, n] = (nA[0], nD[0])

        @block.scalar
        def _(act):
            act1 = nc.scalar.activation
            nA, own = [0], [0]

            def link(ins):
                own[0] += 1
                ins.then_inc(s_a, 1)
                act.wait_ge(s_a, own[0])

            def job():
                nA[0] += 1
                act.wait_ge(s_TA, nA[0])
                return bk(6)

            def done(ins):
                ins.then_inc(s_fA, 1)

            def copy(out, in_, scale=None):
                if scale is None:
                    return act1(out, in_, ACT.Copy)
                return act1(out, in_, ACT.Copy, scale=scale)

            def square(i):
                j = i - 2
                rows = NB if i == 10 else P
                act.wait_ge(s_x[i % 4], 16 * (i // 4 + 1))
                if j == 0:
                    act.wait_ge(s_pc, 1)
                act1(NAT[0:rows, 3072:4096], xr[0:rows, i % 4, :], ACT.Square, accum_out=rms[0:rows, j:j + 1]).then_inc(s_sq, 1)
                act.wait_ge(s_sq, j + 1)
                act1(rms[0:rows, 16 + j:17 + j], rms[0:rows, j:j + 1], ACT.Sqrt, bias=epsc[0:rows, :],
                     scale=1.0 / D).then_inc(s_std, 1)

            def hi(i):
                rows = NB if i == 10 else P
                act.wait_ge(s_itT, i + 1)
                src = PS[:, 2 * (i % 2):2 * (i % 2) + 2, :].rearrange("p a (k t) -> p (a k) t", k=4)[:, :, 0:rows]
                dst = mth[:, :, i * P:(i + 1) * P] if i < 2 else hh[:, :, (i - 2) * P:(i - 2) * P + rows]
                copy(dst, src).then_inc(s_hi, 1)

            def take(m):
                what, j, _ = TILES[m]
                s = m % 2
                act.wait_ge(s_proj, m + 1)
                src = PS[0:DH, 3 * s:3 * s + 3, 0:CH]
                news = PS[0:DH, 3 * s + 2, CH - NB:CH]
                cut = lambda ap: ap.rearrange("p (c t) -> p c t", c=3)
                if what == "gate":
                    act.wait_ge(s_TD, mark["natural", 3][1])
                    copy(cut(XT[0:16, :]), PS[0:16, 3 * s:3 * s + 3, 0:CH]).then_inc(s_eva, 1)
                elif what == "z":
                    act1(cut(AUG[:, j, :]), PS[:, 3 * s:3 * s + 3, 0:CH], ACT.Silu).then_inc(s_eva, 1)
                elif what == "memk":
                    copy(AUG[0:DH, 4 + 2 * j, 0:NMEM], bk(4 + s)[0:DH, 0:NMEM]).then_inc(s_eva, 1)
                elif what == "memv":
                    if j:
                        act.wait_ge(s_TA, 3)
                        act.wait_ge(s_TD, 3)
                    copy(XT[0:DH, 0:NMEM], bk(4 + s)[0:DH, 0:NMEM]).then_inc(s_eva, 1)
                elif what in QNI:
                    copy(QNs[:, QNI[what] + 2 * j, :], news, SCALE)
                    copy(cut(AUG[0:DH, 2 * j, :]), src, SCALE).then_inc(s_eva, 1)
                elif what in KNI:
                    slot = {"foxk": 4 + 2 * j, "ks": 4, "kw": 6}[what]
                    copy(KNs[:, KNI[what] + 2 * j, :], news)
                    copy(cut(AUG[0:DH, slot, :]), src).then_inc(s_eva, 1)
                else:
                    copy(VS[0:DH, VSI[what, j], :], news)
                    if what == "pool":
                        copy(cut(PP[0:DH, j * 1056 + 15:j * 1056 + 15 + TT]), src).then_inc(s_eva, 1)
                    else:
                        xt_free(act, m)
                        copy(cut(XT[0:DH, :]), src).then_inc(s_eva, 1)

            def natural(m):
                what, j, _ = TILES[m]
                out = job()
                nat_free(act, m)
                n = {"memk": 1, "memv": 1, "kw": 2}.get(what, 4)
                dst, c = nat_place(what, j)
                copy(dst[:, 0:n, c:c + P], out[:, 0:n * P].rearrange("p (t c) -> p t c", c=P)).then_inc(s_fA, 1)

            def attend(u0, u1):
                for u in [u0, u0 + 1] + list(range(u0 + 2, u1 + 2)):
                    if u < u1:
                        nk = UNITS[u][4]
                        act.wait_ge(s_nm, u + 1)
                        if u >= 2:
                            act.wait_ge(s_pT, G0[u - 1])
                        s0 = 2 * (u % 2)
                        act1(PP[:, (u % 2) * 1024:(u % 2) * 1024 + nk * P], flat(s0, nk), ACT.Exp,
                             bias=stat[:, u % 4:u % 4 + 1], accum_out=stat[:, 4 + u % 4:5 + u % 4]).then_inc(s_P, 1)
                    v = u - 1
                    if u0 <= v < u1:
                        for g in range(G0[v], G0[v + 1]):
                            if g % 2:
                                act.wait_ge(s_pT, g + 1)
                                if v >= 2:
                                    act.wait_ge(s_pv, v - 1)
                                c = 4 * (g - G0[v])
                                n = min(4, UNITS[v][4] - c)
                                o = 2048 + (v % 2) * 1024 + c * P
                                copy(PP[:, o:o + n * P], bk(5)[:, 0:n * P]).then_inc(s_cA, 1)

            def const(dst, src):
                act.dma_start(dst, src).then_inc(s_cst, 16)

            act.dma_start(gbc, norm_g.partition_broadcast(P)).then_inc(s_gb, 16)
            const(bfb[:, :], b_f.partition_broadcast(P))
            const(pes[:, :, :], pe_[0].rearrange("k (j r) d -> j k (r d)", r=2))
            const(W2[:, :, :, :], w2[0].rearrange("k (a p) d -> p k a d", p=P))
            const(PLW[:, :, :], pool_w[0].rearrange("(j a) c e -> (a c) j e", a=2))
            for a in range(2):
                const(PLS[a * DH:(a + 1) * DH, :, :],
                      pool_s.rearrange("o (j a e) -> o a j e", a=2, e=DH)[:, a].partition_broadcast(DH))
            for step, n in STEPS:
                if step == "item":
                    if n < 9:
                        square(n + 2)
                    hi(n)
                elif step == "project":
                    take(n)
                elif step == "natural":
                    natural(n)
                elif step == "pair" and n % 2 == 0:
                    out = job()
                    if n >= 8:
                        act.wait_ge(s_w1u, 4)
                    done(copy(ft_cols(n % 8), out.rearrange("p (g n j) -> p g n j", g=2, n=8)))
                elif step == "attend":
                    attend(*PHASE[n])
                elif step == "gates":
                    act.wait_ge(s_fgv, 1)
                    act1(fga[:, :, 0:H], fga[:, :, 0:H], ACT.Exp, scale=-1.0)
                    act1(fga[:, :, H:16], FG[:, :, H:16], ACT.Exp, scale=-1.0).then_inc(s_fga, 1)
                    act.wait_ge(s_fga, 1)
                    act1(fga[:, :, 0:H], fga[:, :, 0:H], ACT.Ln, bias=1.0).then_inc(s_fga, 1)
                elif step == "compress":
                    act.wait_ge(s_eva, AT["vc" if n else "kc", 0] + 1)
                    if n:
                        act.wait_ge(s_w1u, 4)
                    for par in range(2):
                        last = copy(ft_prompt(par, 0), xt_pairs(par, 0))
                    last.then_inc(s_fta, 1)
                    act.wait_ge(s_w1u, 4 * (n + 1))
                    for a in range(2):
                        link(copy(peb[:, a:a + 1], bk(3 + a)[:, R_ALL:R_ALL + 1]))
                    for a in range(2):
                        last = act1(HS[:, a, :], bk(3 + a)[:, 0:R_ALL], ACT.Silu, bias=peb[:, a:a + 1])
                    last.then_inc(s_hs, 1)
                    if n == 0:
                        out = job()
                        copy(KCa[0:DH, :, :], out[0:DH, 0:R_PROMPT].rearrange("p (g n) -> p g n", g=2))
                        done(copy(KCs[:, :], out[:, 64:64 + NB * SCB]))
                elif step == "cmp_scores":
                    act.wait_ge(s_cmv, 1)
                    act1(PP[:, 0:512], PP[:, 0:512], ACT.Exp).then_inc(s_cma, 1)
                elif step == "cmp_turn":
                    out = job()
                    done(copy(PP[:, 2048:2560], out))
                elif step == "cmp_out":
                    for q in (0, 2):
                        out = job()
                        done(copy(o_nat[:, 2, 2 * q:2 * q + 2, :], out.rearrange("p (t c) -> p t c", t=2)))
                elif step == "pool_map":
                    for half in range(2):
                        out = job()
                        done(copy(o_nat[:, 3, 4 * half:4 * half + 4, n * P:n * P + DH],
                                  out[:, 0:256].rearrange("p (t c) -> p t c", t=4)))
                elif step == "sample_new":
                    out = job()
                    act.wait_ge(s_nst, 80)
                    done(copy(VNEW[:, 0:512], out[0:NB, :]))
                    out = job()
                    done(copy(KNEW, out[0:NB, :]))
                elif step == "sample_keys":
                    act.wait_ge(s_qz, 1)
                    for b in range(NB):
                        for c in range(3):
                            q = 3 * b + c
                            out = job()
                            if q >= 2:
                                act.wait_ge(s_sS, 5 * ((q - 2) // 3) + 2 * ((q - 2) % 3) + 1)
                            done(copy(KTA[:, q % 2, :], out))
                elif step == "sample_values":
                    act.wait_ge(s_sx, 1)
                    act1(X[:, :], X[:, :], ACT.Exp, bias=XC[:, 0:1], accum_out=XC[:, 1:2])
                    act1(XC[0:32, 8:16], XC[0:32, 8:16], ACT.Exp, bias=XC[0:32, 4:5],
                         accum_out=XC[0:32, 5:6]).then_inc(s_se, 1)
                    out = job()
                    done(copy(PTs.rearrange("p g r -> p (g r)"), out))
                    out = job()
                    done(copy(PLT.rearrange("p j b -> p (j b)"), out[:, 0:2 * NB]))
                elif step == "mix":
                    def hi_part(t):
                        cols = NB if t == NQ else P
                        act.wait_ge(s_g, t + 1)
                        if t >= 2:
                            act.wait_ge(s_y, t - 1)
                        gg = G2[:, t % 2, :].rearrange("p (k c) -> p k c", k=KC)[:, :, 0:cols]
                        hv = TH[:, (t % 2) * 1024:(t % 2 + 1) * 1024].rearrange("p (k c) -> p k c", k=KC)[:, :, 0:cols]
                        copy(hv, gg).then_inc(s_gh, 1)

                    hi_part(0)
                    for t in range(NQ + 1):
                        if t < NQ:
                            hi_part(t + 1)
                        rows = NB if t == NQ else P
                        s = t % 2
                        act.wait_ge(s_y1, t + 1)
                        act1(PP[0:rows, 2048 + s * 1024:3072 + s * 1024], PP[0:rows, s * 1024:(s + 1) * 1024], ACT.Square,
                             accum_out=rms[0:rows, t:t + 1]).then_inc(s_sq, 1)
                        act.wait_ge(s_sq, NQ + 2 + t)
                        act1(rms[0:rows, 16 + t:17 + t], rms[0:rows, t:t + 1], ACT.Sqrt, bias=epsc[0:rows, :],
                             scale=1.0 / D).then_inc(s_ys, 1)
                assert (step, n) not in mark or mark[step, n][0] == nA[0], (step, n, mark[step, n], nA)

        @block.vector
        def _(dve):
            v = nc.vector
            nD, own = [0], [0]

            def link(ins):
                own[0] += 1
                ins.then_inc(s_v, 1)
                dve.wait_ge(s_v, own[0])

            def job():
                nD[0] += 1
                dve.wait_ge(s_TD, nD[0])
                return bk(7)

            def done(ins):
                ins.then_inc(s_fD, 1)

            def normalise(i):
                j = i - 2
                rows = NB if i == 10 else P
                dve.wait_ge(s_std, j + 1)
                dve.wait_ge(s_x[i % 4], 16 * (i // 4 + 1))
                if j == 0:
                    dve.wait_ge(s_gb, 16)
                if j >= 2:
                    dve.wait_ge(s_itT, i - 1)
                link(v.reciprocal(rms[0:rows, 16 + j:17 + j], rms[0:rows, 16 + j:17 + j]))
                v.scalar_tensor_tensor(out=xn[0:rows, j % 2, :], in0=xr[0:rows, i % 4, :],
                                       scalar=rms[0:rows, 16 + j:17 + j], in1=gbc[0:rows, :],
                                       op0=ALU.mult, op1=ALU.mult).then_inc(s_xn, 1)

            def lo(i):
                rows = NB if i == 10 else P
                dve.wait_ge(s_hi, i + 1)
                src = PS[:, 2 * (i % 2):2 * (i % 2) + 2, :].rearrange("p a (k t) -> p (a k) t", k=4)[:, :, 0:rows]
                if i < 2:
                    a, b = mth[:, :, i * P:(i + 1) * P], mtl[:, :, i * P:(i + 1) * P]
                else:
                    t = slice((i - 2) * P, (i - 2) * P + rows)
                    a, b = hh[:, :, t], hl[:, :, t]
                v.tensor_tensor(b, src, a.bitcast(F32), ALU.subtract).then_inc(s_lo, 1)

            def take(m):
                what, j, _ = TILES[m]
                if what in ("z", "gate"):
                    return
                s = m % 2
                dve.wait_ge(s_proj, m + 1)
                src = PS[DH:P, 3 * s:3 * s + 3, 0:CH]
                news = PS[DH:P, 3 * s + 2, CH - NB:CH]
                cut = lambda ap: ap.rearrange("p (c t) -> p c t", c=3)
                if what == "memk":
                    last = v.tensor_copy(AUG[0:DH, 5 + 2 * j, 0:NMEM], bk(4 + s)[DH:P, 0:NMEM])
                elif what == "memv":
                    if j:
                        dve.wait_ge(s_TA, 3)
                        dve.wait_ge(s_TD, 3)
                    last = v.tensor_copy(XT[DH:P, 0:NMEM], bk(4 + s)[DH:P, 0:NMEM])
                elif what in QNI:
                    v.tensor_scalar(QNs[:, QNI[what] + 2 * j + 1, :], news, SCALE, None, ALU.mult)
                    last = v.tensor_scalar(cut(AUG[0:DH, 2 * j + 1, :]), src, SCALE, None, ALU.mult)
                elif what in KNI:
                    slot = {"foxk": 5 + 2 * j, "ks": 5, "kw": 7}[what]
                    v.tensor_copy(KNs[:, KNI[what] + 2 * j + 1, :], news)
                    last = v.tensor_copy(cut(AUG[0:DH, slot, :]), src)
                else:
                    v.tensor_copy(VS[DH:P, VSI[what, j], :], news)
                    if what == "pool":
                        if j == 0:
                            v.memset(PP[:, 0:15], 0.0)
                            v.memset(PP[:, 1056:1071], 0.0)
                        last = v.tensor_copy(cut(PP[DH:P, j * 1056 + 15:j * 1056 + 15 + TT]), src)
                    else:
                        xt_free(dve, m)
                        last = v.tensor_copy(cut(XT[DH:P, :]), src)
                last.then_inc(s_evd, 1)

            def natural(m):
                what, j, _ = TILES[m]
                out = job()
                nat_free(dve, m)
                n = {"memk": 1, "memv": 1, "kw": 2}.get(what, 4)
                dst, c = nat_place(what, j)
                done(v.tensor_copy(dst[:, n:2 * n, c:c + P], out[:, 0:n * P].rearrange("p (t c) -> p t c", c=P)))

            def negmax(u):
                nk = UNITS[u][4]
                dve.wait_ge(s_S, u + 1)
                v.tensor_reduce(stat[:, u % 4:u % 4 + 1], flat(2 * (u % 2), nk), AX.X, ALU.max,
                                negate=True).then_inc(s_nm, 1)

            def norm(u):
                what, h, i, _, _ = UNITS[u]
                dve.wait_ge(s_pv, u + 1)
                dst = o_nat[:, {"mem": 1, "fox": 0, "sel": 2, "win": 2}[what], i, h * DH:(h + 1) * DH]
                src = bk(6 + u % 2)[:, 0:DH]
                r, c = stat[:, 8 + u % 4:9 + u % 4], stat[:, 12 + u % 4:13 + u % 4]
                link(v.reciprocal(r, stat[:, 4 + u % 4:5 + u % 4]))
                if what in ("mem", "fox"):
                    v.tensor_scalar(dst, src, r, None, ALU.mult).then_inc(s_on, 1)
                else:
                    g = H + 3 * h + (1 if what == "sel" else 2)
                    link(v.tensor_tensor(c, r, fga[:, i, g:g + 1], ALU.mult))
                    v.scalar_tensor_tensor(out=dst, in0=src, scalar=c, in1=dst, op0=ALU.mult,
                                           op1=ALU.add).then_inc(s_on, 1)

            def attend(u0, u1):
                negmax(u0)
                negmax(u0 + 1)
                for u in range(u0, u1):
                    for g in range(G0[u], G0[u + 1]):
                        if g % 2 == 0:
                            dve.wait_ge(s_pT, g + 1)
                            if u >= 2:
                                dve.wait_ge(s_pv, u - 1)
                            c = 4 * (g - G0[u])
                            n = min(4, UNITS[u][4] - c)
                            o = 2048 + (u % 2) * 1024 + c * P
                            v.tensor_copy(PP[:, o:o + n * P], bk(4)[:, 0:n * P]).then_inc(s_cD, 1)
                    if u > u0:
                        norm(u - 1)
                    if u + 2 < u1:
                        negmax(u + 2)
                norm(u1 - 1)

            def pool_mean(j):
                dve.wait_ge(s_eva, 22 + j)
                dve.wait_ge(s_nst, 80)
                U = PP[:, j * 1056:j * 1056 + 15 + T]
                A, B = NAT[:, 2048:2048 + 15 + T], PP[:, 2112:2112 + 15 + T]
                n = 15 + T

                def add(out, a, lo_, shift, rows=slice(0, P)):
                    link(v.tensor_tensor(out[rows, lo_:n], a[rows, lo_:n], a[rows, lo_ - shift:n - shift], ALU.add))

                add(A, U, 1, 1)
                if j == 0:
                    add(B, A, 3, 2, slice(DH, P))
                    parts = ((0, A, 2), (1, B, 4))
                else:
                    add(B, A, 3, 2)
                    add(A, B, 7, 4)
                    add(B, A, 15, 8, slice(DH, P))
                    parts = ((0, A, 8), (1, B, 16))
                for a, S_, w in parts:
                    r = slice(a * DH, (a + 1) * DH)
                    v.scalar_tensor_tensor(out=POOLD[r, j, 16:T], in0=S_[r, 31:n], scalar=1.0 / w, in1=U[r, 31:n],
                                           op0=ALU.mult, op1=ALU.subtract)
                    link(v.tensor_tensor(POOLD[r, j, 0:16], S_[r, 15:31], rcnt[r, j, :], ALU.mult))
                    last = v.tensor_tensor(POOLD[r, j, 0:16], POOLD[r, j, 0:16], U[r, 15:31], ALU.subtract)
                last.then_inc(s_pd, 1)

            for step, n in STEPS:
                if step == "item":
                    if n == 1:
                        normalise(2)
                    if 2 <= n < 10:
                        normalise(n + 1)
                    lo(n)
                elif step == "project":
                    take(n)
                elif step == "natural":
                    natural(n)
                elif step == "pair" and n % 2 == 1:
                    out = job()
                    if n >= 8:
                        dve.wait_ge(s_w1u, 4)
                    done(v.tensor_copy(ft_cols(n % 8), out.rearrange("p (g n j) -> p g n j", g=2, n=8)))
                elif step == "attend":
                    attend(*PHASE[n])
                elif step == "gates":
                    dve.wait_ge(s_pc, 2)
                    dve.wait_ge(s_cst, 96)
                    link(v.tensor_tensor(slope_row, slope_row, ident[:, :], ALU.mult))
                    link(v.tensor_reduce(SLC[:, :], slope_row, AX.X, ALU.add))
                    link(v.tensor_scalar(BC[:, :], BC[:, :], SLC[:, 0:1], None, ALU.mult))
                    for g, w in enumerate(POOLW):
                        r = slice((g % 2) * DH, (g % 2 + 1) * DH)
                        link(v.tensor_scalar(rcnt[r, g // 2, :], rcnt[r, g // 2, :], float(w), None, ALU.min))
                    link(v.reciprocal(rcnt[:, :, :], rcnt[:, :, :]))
                    link(v.tensor_tensor(PLW[:, :, :], PLW[:, :, :], PLS[:, :, :], ALU.mult))
                    out = job()
                    v.tensor_copy(FG[:, 0:NQ, :], out[:, 0:16 * NQ].rearrange("p (t c) -> p t c", c=16))
                    link(v.memset(FG[:, NQ, :], 0.0))
                    done(v.tensor_copy(FG[0:NB, NQ, :], out[0:NB, 16 * NQ:16 * (NQ + 1)]))
                    dve.wait_ge(s_fD, nD[0])
                    link(v.tensor_tensor(lf[:, :, :], FG[:, :, 0:H],
                                         bfb[:, :].unsqueeze(1).to_broadcast([P, NQ + 1, H]), ALU.add))
                    v.scalar_tensor_tensor(out=fga[:, :, 0:H], in0=lf[:, :, :], scalar=-1.0, in1=lf[:, :, :],
                                           op0=ALU.mult, op1=ALU.max).then_inc(s_fgv, 1)
                    dve.wait_ge(s_fga, 2)
                    v.scalar_tensor_tensor(out=lf[:, :, :], in0=lf[:, :, :], scalar=0.0, in1=fga[:, :, 0:H],
                                           op0=ALU.min, op1=ALU.subtract).then_inc(s_lf, 1)
                    link(v.tensor_scalar(fga[:, :, H:16], fga[:, :, H:16], 1.0, None, ALU.add))
                    v.reciprocal(fga[:, :, H:16], fga[:, :, H:16]).then_inc(s_gate, 1)
                    dve.wait_ge(s_gate, 1)
                elif step == "forget":
                    for half in range(2):
                        out = job()
                        ini = 0.0 if half == 0 else OB[0:H, 511:512]
                        v.tensor_tensor_scan(OB[0:H, half * 512:(half + 1) * 512], onesc[0:H, 0:1].to_broadcast([H, 512]),
                                             out[0:H, :], ini, ALU.mult, ALU.add).then_inc(s_fD, 1)
                        dve.wait_ge(s_fD, nD[0])
                    v.tensor_scalar(OB[0:H, 1024:2048], OB[0:H, 0:1024], -1.0, None, ALU.mult).then_inc(s_c, 1)
                elif step == "compress":
                    if n:
                        dve.wait_ge(s_w1u, 4)
                    for par in range(2):
                        last = v.tensor_copy(ft_prompt(par, 1), xt_pairs(par, 1))
                    last.then_inc(s_ftd, 1)
                    out = job()
                    done(v.tensor_copy(FT[:, :, R_ALL], out[:, 0:NJ]))
                    if n == 1:
                        out = job()
                        link(v.memset(PP[:, 3072:3328], 0.0))
                        for h in range(H):
                            r = slice(32 * h, 32 * h + NCB)
                            v.tensor_copy(PP[r, 3072 + h * DH:3072 + (h + 1) * DH], out[r, h * DH:(h + 1) * DH])
                        done(v.tensor_copy(VCs[:, :], out[0:NB * SCB, 256:384]))
                elif step == "cmp_scores":
                    out = job()
                    E = PP[:, 0:512].rearrange("p (i h n) -> p i h n", i=NQ, h=H)
                    E3 = PP[:, 0:512].rearrange("p (q n) -> p q n", n=NCB)
                    v.tensor_tensor(E, out.rearrange("p (i h n) -> p i h n", i=NQ, h=H),
                                    m_cmp[:, :, :].unsqueeze(2).to_broadcast([P, NQ, H, NCB]), ALU.add).then_inc(s_fD, 1)
                    dve.wait_ge(s_fD, nD[0])
                    link(v.tensor_reduce(cs[:, 0:32], E3, AX.X, ALU.max))
                    v.tensor_tensor(E3, E3, cs[:, 0:32].unsqueeze(2).to_broadcast([P, 32, NCB]),
                                    ALU.subtract).then_inc(s_cmv, 1)
                    dve.wait_ge(s_cma, 1)
                    link(v.tensor_tensor(E3[:, 0:H, :], E3[:, 0:H, :], seen0[:, :].unsqueeze(1).to_broadcast([P, H, NCB]),
                                         ALU.mult))
                    link(v.tensor_reduce(cs[:, 32:64], E3, AX.X, ALU.add))
                    link(v.tensor_scalar(cs[:, 32:64], cs[:, 32:64], 1e-30, None, ALU.max))
                    link(v.reciprocal(cs[:, 32:64], cs[:, 32:64]))
                    link(v.tensor_tensor(cs[:, 64:96].rearrange("p (i h) -> p i h", i=NQ),
                                         cs[:, 32:64].rearrange("p (i h) -> p i h", i=NQ),
                                         fga[:, 0:NQ, H:16:3], ALU.mult))
                    link(v.memset(PP[:, 1024:2048], 0.0))
                    v.tensor_tensor(PP[:, 1024:2048].rearrange("p (q n) -> p q n", n=32)[:, :, 0:NCB], E3,
                                    cs[:, 64:96].unsqueeze(2).to_broadcast([P, 32, NCB]), ALU.mult).then_inc(s_cm, 1)
                elif step == "cmp_turn":
                    out = job()
                    done(v.tensor_copy(PP[:, 2560:3072], out))
                elif step == "cmp_out":
                    for q in (1, 3):
                        out = job()
                        done(v.tensor_copy(o_nat[:, 2, 2 * q:2 * q + 2, :], out.rearrange("p (t c) -> p t c", t=2)))
                elif step == "pool_last":
                    out = job()
                    done(v.tensor_copy(poolp[:, n * P:(n + 1) * P], out[0:15, 0:P]))
                    pool_mean(n)
                    if n == 1:
                        dve.wait_ge(s_stp, 64)
                        for g, w in enumerate(POOLW):
                            last = v.tensor_reduce(PSUMS[:, g * DH:(g + 1) * DH],
                                                   STP[g].rearrange("p (r c) -> p c r", c=DH), AX.X, ALU.add)
                        last.then_inc(s_psum, 1)
                elif step == "pool_map":
                    for half in range(2):
                        out = job()
                        done(v.tensor_copy(o_nat[:, 3, 4 * half:4 * half + 4, n * P + DH:(n + 1) * P],
                                           out[:, 0:256].rearrange("p (t c) -> p t c", t=4)))
                elif step == "sample_new":
                    link(v.memset(NAT[:, 2048:3328], 0.0))
                    for a in range(2):
                        for p_ in range(2):
                            h = 2 * a + p_
                            r = slice(p_ * DH, (p_ + 1) * DH)
                            diag = lambda z, h_: z.rearrange("p b r -> p (b r)")[:, h_:h_ + 36 * (NB - 1) + 1:36]
                            v.tensor_copy(diag(QZF[r, a], h), QNs[:, h, :])
                            v.tensor_copy(diag(QZM[r, a], h), QNs[:, 8 + h, :])
                            v.tensor_copy(diag(QZN[a * DH:(a + 1) * DH], h), QNs[:, 4 + h, :])
                            v.tensor_copy(KNF[r, a, :], KNs[:, h, :])
                    for g in range(2):
                        r = slice(g * DH, (g + 1) * DH)
                        v.tensor_copy(KNS[r, :], KNs[:, 4 + g, :])
                        last = v.tensor_copy(KNW[r, :], KNs[:, 6 + g, :])
                    last.then_inc(s_qz, 1)
                    out = job()
                    dve.wait_ge(s_nst, 80)
                    done(v.tensor_copy(VNEW[:, 512:1024], out[0:NB, :]))
                    dve.wait_ge(s_fD, nD[0])
                    link(v.tensor_tensor(PSUMS, PSUMS, VNEW[:, 768:1024], ALU.add))
                    for g, w in enumerate(POOLW):
                        c = slice(g * DH, (g + 1) * DH)
                        last = v.scalar_tensor_tensor(out=PSUMS[:, c], in0=PSUMS[:, c], scalar=1.0 / w,
                                                      in1=VNEW[:, 768 + g * DH:768 + (g + 1) * DH], op0=ALU.mult,
                                                      op1=ALU.subtract)
                    last.then_inc(s_psd, 1)
                    dve.wait_ge(s_lfp, 16 * NB * NPG)
                    v.tensor_copy(LFR.rearrange("p (h t) -> p h t", h=H),
                                  LFP.rearrange("p (t h) -> p h t", h=H)).then_inc(s_lfr, 1)
                elif step == "sample_keys":
                    for b in range(NB):
                        for c in range(2):
                            q = 2 * b + c
                            out = job()
                            if q >= 2:
                                dve.wait_ge(s_sS, 5 * ((q - 2) // 2) + 2 * ((q - 2) % 2) + 2)
                            done(v.tensor_copy(KTD[:, q % 2, :], out))
                        if b == 0:
                            one = onesc[:, 0:1].to_broadcast([P, PAST + 1])
                            link(v.tensor_tensor_scan(BIAS, one, one, float(-PAST - 1), ALU.mult, ALU.add))
                            link(v.tensor_scalar(BIAS, BIAS, SLC[:, 0:1], None, ALU.mult))
                        if b == 1:
                            dve.wait_ge(s_sd, 16 * 8)
                            link(v.tensor_tensor_scan(CT, onesc[32:64, 0:1].to_broadcast([32, PAST + 1]), LFT, 0.0,
                                                      ALU.mult, ALU.add))
                            link(v.tensor_scalar(XT[0:32, 0:PAST + 1], CT, -1.0, CT[:, PAST:PAST + 1], ALU.mult,
                                                 ALU.add))
                elif step == "sample_values":
                    dve.wait_ge(s_sS, 5 * NB + 1)
                    v.tensor_tensor(X[0:96, 0:PAST], PS[0:96, 0, :], BIAS[0:96, 0:PAST], ALU.add)
                    v.tensor_tensor(X[0:96, PAST:PAST + 1], PS[0:96, 4, 0:1], BIAS[0:96, PAST:PAST + 1], ALU.add)
                    v.tensor_copy(X[96:P, 0:NMEM], PS[96:P, 0, 0:NMEM])
                    link(v.memset(X[96:P, NMEM:PAST + 1], NEG))
                    link(v.tensor_reduce(XC[:, 0:1], X, AX.X, ALU.max, negate=True))
                    link(v.tensor_tensor(XC[0:32, 8:16], PS[0:32, 5, 0:SCB], BC[0:32, :], ALU.add))
                    v.tensor_reduce(XC[0:32, 4:5], XC[0:32, 8:16], AX.X, ALU.max, negate=True).then_inc(s_sx, 1)
                    dve.wait_ge(s_se, 1)
                    link(v.reciprocal(XC[:, 2:3], XC[:, 1:2]))
                    link(v.tensor_tensor(XC[:, 2:3], XC[:, 2:3], GC[:, 0:1], ALU.mult))
                    link(v.tensor_scalar(X, X, XC[:, 2:3], None, ALU.mult))
                    v.tensor_scalar(XN8[:, :], E8[:, :], X[:, PAST:PAST + 1], None, ALU.mult)
                    link(v.reciprocal(XC[0:32, 6:7], XC[0:32, 5:6]))
                    link(v.tensor_tensor(XC[0:32, 6:7], XC[0:32, 6:7], GC[0:32, 1:2], ALU.mult))
                    link(v.tensor_scalar(XC[0:32, 8:16], XC[0:32, 8:16], XC[0:32, 6:7], None, ALU.mult))
                    v.tensor_tensor(XC[0:32, 16:80].rearrange("p (b n) -> p b n", b=NB),
                                    E8[0:32, :].unsqueeze(2).to_broadcast([32, NB, SCB]),
                                    XC[0:32, 8:16].unsqueeze(1).to_broadcast([32, NB, SCB]), ALU.mult).then_inc(s_px, 1)
                    out = job()
                    v.tensor_copy(PTn, out[0:NB, 0:P])
                    done(v.tensor_copy(PTc, out[0:NB * SCB, P:P + 32]))
                    dve.wait_ge(s_vr, 4 * NB)
                    for a in range(2):
                        for p_ in range(2):
                            h = 2 * a + p_
                            r, q = slice(p_ * DH, (p_ + 1) * DH), slice(a * DH, (a + 1) * DH)
                            v.tensor_copy(oTs[r, a, :], bk(3 * a)[r, h:32:4])
                            v.tensor_copy(oTs[r, 6 + a, :], bk(2 + 2 * a)[r, h:32:4])
                            v.tensor_copy(oTs[r, 2 + a, :], bk(1)[q, h:32:4])
                    out = job()
                    done(v.tensor_copy(oTs[:, 4:6, :], out[:, 0:2 * NB].rearrange("p (j b) -> p j b", j=2)))
                    dve.wait_ge(s_fD, nD[0])
                elif step == "mix":
                    def gate(t):
                        cols = NB if t == NQ else P
                        gg = G2[:, t % 2, :].rearrange("p (k c) -> p k c", k=KC)[:, :, 0:cols]
                        sz = AUG[:, :, t * P:t * P + cols]
                        if t >= 2:
                            dve.wait_ge(s_gh, t - 1)
                        if t == NQ:
                            v.tensor_tensor(gg, oTs[:, :, :], sz, ALU.mult).then_inc(s_g, 1)
                        else:
                            dve.wait_ge(s_oT, t + 1)
                            b0 = 4 + 2 * (t % 2)
                            src = PS[:, b0:b0 + 2, :].rearrange("p a (k c) -> p (a k) c", k=4)
                            v.tensor_tensor(gg, src, sz, ALU.mult).then_inc(s_g, 1)
                        dve.wait_ge(s_gh, t + 1)
                        if t >= 2:
                            dve.wait_ge(s_y, t - 1)
                        part = lambda x_: x_[:, (t % 2) * 1024:(t % 2 + 1) * 1024].rearrange(
                            "p (k c) -> p k c", k=KC)[:, :, 0:cols]
                        v.tensor_tensor(part(TL), gg, part(TH).bitcast(F32), ALU.subtract).then_inc(s_gl, 1)

                    def final(t):
                        rows = NB if t == NQ else P
                        dve.wait_ge(s_ys, t + 1)
                        if t == 0:
                            dve.wait_ge(s_gf, 16)
                        y1 = PP[0:rows, (t % 2) * 1024:(t % 2 + 1) * 1024]
                        link(v.reciprocal(rms[0:rows, 16 + t:17 + t], rms[0:rows, 16 + t:17 + t]))
                        v.scalar_tensor_tensor(out=y1, in0=y1, scalar=rms[0:rows, 16 + t:17 + t], in1=gf[0:rows, :],
                                               op0=ALU.mult, op1=ALU.mult).then_inc(s_yo, 1)

                    gate(0)
                    for t in range(NQ + 1):
                        if t < NQ:
                            gate(t + 1)
                        if t > 0:
                            final(t - 1)
                        rows = NB if t == NQ else P
                        s = t % 2
                        dve.wait_ge(s_y, t + 1)
                        dve.wait_ge(s_xf[s], 16 * (t // 2 + 1))
                        if t >= 2:
                            dve.wait_ge(s_yst[s], 16 * (t // 2))
                        v.tensor_tensor(PP[0:rows, s * 1024:(s + 1) * 1024],
                                        PS[0:rows, 2 * s:2 * s + 2, :].rearrange("p a c -> p (a c)"),
                                        PP[0:rows, 2048 + s * 1024:3072 + s * 1024], ALU.add).then_inc(s_y1, 1)
                    final(NQ)
                assert mark[step, n][1] == nD[0], (step, n, mark[step, n], nD)

        @block.gpsimd
        def _(pool):
            g = nc.gpsimd
            own = [0]

            def link(ins):
                own[0] += 1
                ins.then_inc(s_pb, 1)
                pool.wait_ge(s_pb, own[0])

            link(g.memset(ident[:, :], 0.0))
            link(g.affine_select(out=ident[:, :], in_=ident[:, :], compare_op=ALU.not_equal, fill=1.0, base=0,
                                 pattern=[[-1, P]], channel_multiplier=1))
            g.memset(epsc[:, :], EPS)
            g.memset(onesc[:, :], 1.0).then_inc(s_pc, 1)

            ones = onesc[:, 0:1].unsqueeze(2).to_broadcast([P, KC, P])

            def split(s, landed, hi_, lo_, count):
                pool.wait_ge(s_w[s], landed)
                g.tensor_tensor(hi_, WR[:, s, :, :], ones, ALU.mult).then_inc(s_wcp, 1)
                pool.wait_ge(s_wcp, count)
                g.tensor_tensor(lo_, WR[:, s, :, :], hi_.bitcast(F32), ALU.subtract).then_inc(s_split, 1)
                pool.wait_ge(s_split, count)

            def split_pair(it):
                for s in range(2):
                    used, landed, count = it * 2 + (s - 1), it * 16 + 16, it * 2 + (s + 1)
                    pool.wait_ge(s_proj, used)
                    split(s, landed, WH[:, s, :, :], WL[:, s, :, :], count)

            pool.wait_ge(s_pc, 1)
            for s in range(2):
                split(s, 16, WH[:, s, :, :], WL[:, s, :, :], s + 1)
            with pool.Fori(1, 3) as it:
                split_pair(it)
            pool.wait_ge(s_wg, 16)
            split_pair(3)

            for h in range(H):
                g.memset(slope_row[:, h:P:H], SLOPES[h])
            g.iota(BC[:, :], pattern=[[BLK, SCB]], base=BLK - 1 - PAST, channel_multiplier=0,
                   allow_small_or_imprecise_dtypes=True)
            g.iota(rcnt[:, :, :], pattern=[[0, 2], [1, 16]], base=1, channel_multiplier=0,
                   allow_small_or_imprecise_dtypes=True)
            g.memset(GC[:, :], 1.0)
            link(g.tensor_copy(identb[:, :], ident[:, :]))
            link(g.memset(m_diag[:, :], 0.0))
            link(g.affine_select(out=m_diag[:, :], in_=m_diag[:, :], compare_op=ALU.is_ge, fill=NEG, base=0,
                                 pattern=[[-1, P]], channel_multiplier=1))
            link(g.memset(m_win[:, :], 0.0))
            link(g.affine_select(out=m_win[:, :], in_=m_win[:, :], compare_op=ALU.is_ge, fill=NEG, base=0,
                                 pattern=[[1, P]], channel_multiplier=-1))
            link(g.memset(m_cmp[:, :, :], 0.0))
            link(g.affine_select(out=m_cmp[:, :, :], in_=m_cmp[:, :, :], compare_op=ALU.is_ge, fill=NEG,
                                 base=-(BLK - 1), pattern=[[P, NQ], [-BLK, NCB]], channel_multiplier=1))
            link(g.memset(seen0[:, :], 1.0))
            link(g.affine_select(out=seen0[:, :], in_=seen0[:, :], compare_op=ALU.is_ge, fill=0.0,
                                 base=-(BLK - 1), pattern=[[-BLK, NCB]], channel_multiplier=1))
            for br in range(4):
                r = slice(32 * br, 32 * br + 32)
                link(g.memset(E8[r, :], 1.0))
                link(g.affine_select(out=E8[r, :], in_=E8[r, :], compare_op=ALU.is_ge, fill=0.0, base=0,
                                     pattern=[[-H, NB]], channel_multiplier=1))
                link(g.affine_select(out=E8[r, :], in_=E8[r, :], compare_op=ALU.is_ge, fill=0.0, base=H - 1,
                                     pattern=[[H, NB]], channel_multiplier=-1))
            link(g.memset(AUG[DH:DH + 2, :, :], 1.0))
            link(g.iota(AUG[96:98, 0:4, :], pattern=[[0, 4], [1, TT]], base=0, channel_multiplier=0,
                        allow_small_or_imprecise_dtypes=True))
            for h in range(H):
                link(g.tensor_scalar(AUG[96:98, h, :], AUG[96:98, h, :], -SLOPES[h], None, ALU.mult))
                link(g.memset(AUG[96:97, h, :], SLOPES[h]))
            link(g.memset(AUG[96:98, 4:8, :], 1.0))
            link(g.iota(AUG[96:97, 4:8, :], pattern=[[0, 4], [1, TT]], base=0, channel_multiplier=0,
                        allow_small_or_imprecise_dtypes=True))
            link(g.memset(KCa[DH:DH + 2, :, :], 1.0))
            g.iota(KCa[DH:DH + 1, :, :], pattern=[[0, 2], [BLK, NCB]], base=BLK - 1, channel_multiplier=0,
                   allow_small_or_imprecise_dtypes=True).then_inc(s_pc, 1)
            pool.wait_ge(s_pc, 2)
            with pool.Fori(4, NT // 2) as it:
                split_pair(it)
            pool.wait_ge(s_proj, NT - 2)
            split(0, 16 * (NT // 2 + 1), WH[:, 0, :, :], WL[:, 0, :, :], NT)
            pool.wait_ge(s_proj, NT)
            for j in range(KC):
                c = slice(j * P, (j + 1) * P)
                split((NT + j) % 2, 16 * ((NT + j) // 2 + 1), woh[:, :, c], wol[:, :, c], NT + j + 1)

        @block.sync
        def _(sp):
            xp, xs = x_p[0], x_s[:, 0, :]
            win, wout = w_in[0], w_out[0]

            def load_x(i):
                src = mem_p[0, i * P:(i + 1) * P, :] if i < 2 else xs if i == 10 else xp[(i - 2) * P:(i - 1) * P, :]
                rows = NB if i == 10 else P
                if 4 <= i < 6:
                    sp.wait_ge(s_itT, i - 3)
                elif i >= 6:
                    sp.wait_ge(s_xn, i - 5)
                sp.dma_start(xr[0:rows, i % 4, :], src).then_inc(s_x[i % 4], 16)

            def load_w(m):
                if m >= 2:
                    sp.wait_ge(s_split, m - 1)
                if m == AT["gate", 0]:
                    for dst, c, sem_ in ((slice(0, H), C_F, s_w[m % 2]), (slice(H, 16), C_G, s_wg)):
                        sp.dma_start(WR[:, m % 2, :, dst],
                                     win[:, c:c + dst.stop - dst.start].rearrange("(k p) c -> p k c", p=P)).then_inc(sem_, 16)
                    return
                if m >= NT:
                    src = wout[:, (m - NT) * P:(m - NT + 1) * P]
                else:
                    what, _, c = TILES[m]
                    src = (w_mem[0] if what in ("memk", "memv") else win)[:, c:c + P]
                sp.dma_start(WR[:, m % 2, :, :], src.rearrange("(k p) c -> p k c", p=P)).then_inc(s_w[m % 2], 16)

            def page(i):
                return sp.value_load(ptb[0:1, bass.ds(i, 1)], min_val=0, max_val=c_fox.shape[1] - 1)

            def load_pair(q):
                kind, n, half = q // 16, (q % 16) // 2, q % 2
                if q == 0:
                    sp.wait_ge(s_on, PHASE[0][1])
                if q == 20:
                    sp.wait_ge(s_nst, 32)
                if q >= 28:
                    sem_, val = mark["pair", 1, (q - 28) // 2]
                    sp.wait_ge(sem_, val)
                for a in range(2):
                    pg = page(NPG * n + 2 * half + a)
                    for g in range(2):
                        src = c_nsa[0, bass.ds(pg, 1), :, kind, g, :].rearrange("o (j r) d -> (o j) r d", r=2)
                        dst = pair_slot(q)[a * DH:(a + 1) * DH, g, :].rearrange("p (r d) -> p r d", r=2)
                        sp.dma_start(dst, src).then_inc(s_pair[n], 16)

            def load_w1(n):
                kind, c = n // 4, n % 4
                if n >= 2:
                    sp.wait_ge(s_w1u, n - 1)
                src = w1[0, kind, c * 1024:(c + 1) * 1024, :].rearrange("(j p) e -> p j e", p=P)
                sp.dma_start(w1s[:, n % 2, :, :], src).then_inc(s_w1[n % 2], 16)

            def store_nat(dst, what):
                sp.dma_start(dst, what).then_inc(s_nst, 16)

            def jobs_done(step, n):
                a, d = mark[step, n]
                sp.wait_ge(s_fA, a)
                sp.wait_ge(s_fD, d)

            sp.dma_start(ptb[:, :], ptab.rearrange("(o b) n -> o (b n)", o=1)).then_inc(s_pt, 16)
            for i in range(4):
                load_x(i)
            load_w(0)
            load_w(1)
            for i, m in zip(range(4, 11), (2, 3, 4, 5, None, None, None)):
                load_x(i)
                if m is not None and m < 4:
                    load_w(m)
            load_w(4)
            load_w(5)
            load_w(6)
            sp.wait_ge(s_pt, 16)
            jobs_done("natural", 3)
            store_nat(o_memkv[0, 0].rearrange("(t p) a h d -> p t (a h d)", p=P), nat[:, 0:2, :])
            load_w(7)
            load_w(8)
            for q in range(4):
                load_pair(q)
            sp.wait_ge(s_lf, 1)
            sp.dma_start(o_lf[0, 0].rearrange("(t p) h -> p t h", p=P), lf[:, 0:NQ, :]).then_inc(s_st, 16)
            sp.dma_start(o_lf_s[0, :, 0, :], lf[0:NB, NQ, :]).then_inc(s_st, 16)
            load_w(9)
            sp.wait_ge(s_c, 1)
            sp.wait_ge(s_pc, 2)
            sp.dma_start(AUG[65:66, 0:4, 0:T], OB[0:H, 0:1024]).then_inc(s_aug, 16)
            sp.dma_start(AUG[64:65, 4:8, 0:T], OB[0:H, 1024:2048]).then_inc(s_aug, 16)
            for n in range(5):
                load_w(10 + n)
                if n < 4:
                    for q in range(4 + 3 * n, 7 + 3 * n):
                        load_pair(q)
            jobs_done("natural", 12)
            store_nat(o_foxkv[0, 0].rearrange("(t p) a h d -> p t (a h d)", p=P), nat)
            load_w(15)
            load_w(16)
            for q in range(16, 20):
                load_pair(q)
            sp.wait_ge(s_on, PHASE[1][1])
            sp.dma_start(AUG[64:66, :, :], AUG[96:98, :, :]).then_inc(s_aug, 16)
            load_w1(0)
            load_w1(1)
            for q in range(20, 28):
                load_pair(q)
            load_w(17)
            load_w1(2)
            load_w1(3)
            load_w(18)
            load_w1(4)
            load_w1(5)
            for q in range(28, 32):
                load_pair(q)
            load_w1(6)
            load_w1(7)
            load_w(19)
            load_w(20)
            load_w(21)
            jobs_done("natural", 18)
            store_nat(o_nsakv[0, 0].rearrange("(t p) a g d -> p t (a g d)", p=P), nat)
            jobs_done("natural", 20)
            ow = o_nsawin[0, 0].rearrange("(t p) a g d -> p t a (g d)", p=P)
            store_nat(ow[:, :, 0, :], kw)
            store_nat(ow[:, :, 1, :], vw[:, 4:8, :])
            load_w(22)
            sp.wait_ge(s_on, len(UNITS))
            sp.wait_ge(s_nst, 80)
            for g, w in enumerate(POOLW):
                src = st_pool[0, :, 16 - w:15, g * DH:(g + 1) * DH]
                sp.dma_start(STP[g].rearrange("p (r c) -> p r c", c=DH), src).then_inc(s_stp, 16)
            load_w(23)
            sp.dma_start(o_pool_s[0, :, 0:14, :], st_pool[0, :, 1:15, :]).then_inc(s_st, 16)
            sp.dma_start(o_win_s[0, :, 0:511], st_win[0, :, 1:512]).then_inc(s_st, 16)
            for b in range(NB):
                for pg in range(NPG):
                    pn = page(NPG * b + pg)
                    sp.dma_start(LFP[pg * NB + b:pg * NB + b + 1, :],
                                 c_lf[0, bass.ds(pn, 1)].rearrange("o t h -> o (t h)")).then_inc(s_lfp, 16)
            load_w(24)
            jobs_done("pool_last", 1)
            sp.dma_start(o_pool[0, 0], poolp).then_inc(s_st, 16)
            for m in range(25, NT):
                load_w(m)

            def pages(b):
                return [page(b * NPG + pg) for pg in range(NPG)]

            def load_kv(b, br, kv, pn):
                if br in (0, 1):
                    for pg in range(NPG):
                        if br == 0:
                            dst = ring[:, 0, pg * 256:(pg + 1) * 256]
                            src = c_fox[0, bass.ds(pn[pg], 1), :, kv, :, :].rearrange("o t h d -> (o t) (h d)")
                        else:
                            dst = ring[:, 1, pg * P:(pg + 1) * P]
                            src = c_nsa[0, bass.ds(pn[pg], 1), :, 2 + kv, :, :].rearrange("o t g d -> (o t) (g d)")
                        sp.dma_start(dst, src).then_inc(s_kv[br], 16)
                elif br == 2:
                    src = st_win[0, bass.ds(b, 1), :, kv, :, :].rearrange("o (t p) g d -> p (o t) (g d)", p=P)
                    sp.dma_start(ring[:, 2, 0:512].rearrange("p (t c) -> p t c", t=4), src).then_inc(s_kv[2], 16)
                else:
                    src = c_mem[0, bass.ds(b, 1), :, kv, :, :].rearrange("o (t p) h d -> p (o t) (h d)", p=P)
                    sp.dma_start(ring[:, 3, 0:512].rearrange("p (t c) -> p t c", t=2), src).then_inc(s_kv[3], 16)

            sp.wait_ge(s_pd, 2)
            sp.wait_ge(s_psum, 1)
            first = pages(0)
            for br in range(4):
                load_kv(0, br, 0, first)
            sp.wait_ge(s_lfr, 1)
            for pg in range(NPG):
                sp.dma_start(LFT[:, pg * P:(pg + 1) * P],
                             LFR[pg * NB:(pg + 1) * NB, :].rearrange("b (h t) -> b h t", h=H)).then_inc(s_sd, 16)
            sp.dma_start(LFT[:, PAST:PAST + 1], lf[0:NB, NQ, :]).then_inc(s_sd, 16)
            for dst, c in ((GC[32:64, 0:1], 1), (GC[64:96, 0:1], 2), (GC[0:32, 1:2], 0)):
                sp.dma_start(dst, fga[0:NB, NQ, H + c:16:3]).then_inc(s_sd, 16)
            jobs_done("sample_new", 0)
            sp.dma_start(o_foxkv_s[0, :, 0, 0].rearrange("b h d -> b (h d)"), KNEW[:, 0:256]).then_inc(s_st, 16)
            sp.dma_start(o_foxkv_s[0, :, 0, 1].rearrange("b h d -> b (h d)"), VNEW[:, 0:256]).then_inc(s_st, 16)
            sp.dma_start(o_nsakv_s[0, :, 0, 0:2].rearrange("b a g d -> b (a g d)"), VNEW[:, 256:512]).then_inc(s_st, 16)
            sp.dma_start(o_nsakv_s[0, :, 0, 2].rearrange("b g d -> b (g d)"), KNEW[:, 256:384]).then_inc(s_st, 16)
            sp.dma_start(o_nsakv_s[0, :, 0, 3].rearrange("b g d -> b (g d)"), VNEW[:, 512:640]).then_inc(s_st, 16)
            sp.dma_start(o_win_s[0, :, 511, 0].rearrange("b g d -> b (g d)"), KNEW[:, 384:512]).then_inc(s_st, 16)
            sp.dma_start(o_win_s[0, :, 511, 1].rearrange("b g d -> b (g d)"), VNEW[:, 640:768]).then_inc(s_st, 16)
            sp.dma_start(o_pool_s[0, :, 14, :], VNEW[:, 768:1024]).then_inc(s_st, 16)
            for m in (NT, NT + 1):
                load_w(m)
            ka, kd = mark["K"]

            def slot_read(b, br):
                if br == 0:
                    sp.wait_ge(s_TA, b * 3 + (ka + 1))
                    sp.wait_ge(s_TD, b * 2 + (kd + 1))
                elif br == 2:
                    sp.wait_ge(s_TD, b * 2 + (kd + 2))
                else:
                    sp.wait_ge(s_TA, b * 3 + (ka + (2 if br == 1 else 3)))

            with sp.Fori(1, NB) as b:
                pn = pages(b)
                for br in range(4):
                    slot_read(b - 1, br)
                    load_kv(b, br, 0, pn)
            for m in range(NT + 2, NT + KC):
                load_w(m)
            first = pages(0)
            for br in range(4):
                slot_read(NB - 1, br)
                load_kv(0, br, 1, first)
            with sp.Fori(1, NB) as b:
                pn = pages(b)
                for br in range(4):
                    sp.wait_ge(s_vr, b * 4 + (br - 3))
                    load_kv(b, br, 1, pn)
            sp.wait_ge(s_vr, 4 * NB)
            sp.dma_start(gf, fin_g.rearrange("(o d) -> o d", o=1).partition_broadcast(P)).then_inc(s_gf, 16)

            def load_x2(t):
                rows = NB if t == NQ else P
                if t >= 2:
                    sp.wait_ge(s_ys, t - 1)
                sp.dma_start(PP[0:rows, 2048 + (t % 2) * 1024:3072 + (t % 2) * 1024],
                             xs if t == NQ else xp[t * P:(t + 1) * P, :]).then_inc(s_xf[t % 2], 16)

            load_x2(0)
            load_x2(1)
            for t in range(NQ + 1):
                rows = NB if t == NQ else P
                sp.wait_ge(s_yo, t + 1)
                sp.dma_start(y_s[:, 0, :] if t == NQ else y_p[0, t * P:(t + 1) * P, :],
                             PP[0:rows, (t % 2) * 1024:(t % 2 + 1) * 1024]).then_inc(s_yst[t % 2], 16)
                if t + 2 <= NQ:
                    load_x2(t + 2)
            sp.wait_ge(s_yst[0], 16 * 5)
            sp.wait_ge(s_yst[1], 16 * 4)
            sp.wait_ge(s_nst, 80)
            sp.wait_ge(s_st, 16 * 13)


_INS = ["x_prompt", "x_sample", "cache_fox_kv", "cache_fox_lf", "cache_nsa_kv", "state_nsa_win", "state_pool",
        "cache_mem_kv", "page_table", "mem_prompt", "norm_g", "w_in", "b_fgt", "nsa_pe", "nsa_w1", "nsa_w2",
        "pool_w", "pool_scale", "w_mem_kv", "w_out", "final_g"]
_OUTS = [(1, T, D), (NB, 1, D), (1, 1, T, 2, H, DH), (1, 1, T, H), (1, 1, T, 4, 2, DH), (1, 1, 512, 2, 2, DH),
         (1, 1, 15, 256), (1, 1, NMEM, 2, H, DH), (1, NB, 1, 2, H, DH), (1, NB, 1, H), (1, NB, 1, 4, 2, DH),
         (1, NB, 512, 2, 2, DH), (1, NB, 15, 256)]


def kernel(**inputs):
    import numpy as np
    import concourse.bacc as bacc
    from concourse.bass_utils import run_bass_kernel_spmd

    nc = bacc.Bacc("TRN2", target_bir_lowering=False, num_devices=1)
    arrays, args = {}, []
    for name in _INS:
        a = np.ascontiguousarray(inputs[name])
        arrays[f"in_{name}"] = a
        args.append(nc.dram_tensor(f"in_{name}", a.shape, mybir.dt.from_np(a.dtype), kind="ExternalInput").ap())
    for i, shape in enumerate(_OUTS):
        args.append(nc.dram_tensor(f"out_{i}", shape, F32, kind="ExternalOutput").ap())
    build(nc, *args)
    r = run_bass_kernel_spmd(nc, [arrays], core_ids=[0])
    return tuple(r.results[0][f"out_{i}"] for i in range(len(_OUTS)))
```

```python
from contextlib import ExitStack

import concourse.bass as bass
from concourse import mybir

F32 = mybir.dt.float32
F32R = mybir.dt.float32r
BF16 = mybir.dt.bfloat16
I32 = mybir.dt.int32
ALU = mybir.AluOpType
ACT = mybir.ActivationFunctionType
AX = mybir.AxisListType

P = 128
D = 1024
KC = D // P
T = 1024
NB = 8
TT = T + NB
NQ = T // P
H = 4
DH = 64
SCALE = DH ** -0.5
NEG = -1e30
EPS = 1e-6
PAST = 512
NPG = PAST // P
NMEM = 256
WIN_T = 512 // P
CH = TT // 3
BLK = 64
NCB = T // BLK
SCB = PAST // BLK
SLOPES = [2.0 ** (-8.0 * (h + 1) / H) for h in range(H)]
POOLW = (2, 4, 8, 16)
R_PROMPT = 2 * NCB
R_ALL = R_PROMPT + 2 * NB * SCB
NJ = BLK // 2

C_FOXQ, C_FOXK, C_FOXV, C_F = 0, 256, 512, 768
C_NSAQ, C_NSAKV, C_G, C_POOL, C_MEMQ, C_Z = 772, 1028, 1796, 1808, 2064, 2320

TILES = [("memk", 0, 0), ("memk", 1, 128), ("memv", 0, 256), ("memv", 1, 384),
         ("memq", 0, C_MEMQ), ("memq", 1, C_MEMQ + 128),
         ("gate", 0, C_F),
         ("foxq", 0, C_FOXQ), ("foxq", 1, C_FOXQ + 128), ("foxk", 0, C_FOXK), ("foxk", 1, C_FOXK + 128),
         ("foxv", 0, C_FOXV), ("foxv", 1, C_FOXV + 128),
         ("kc", 0, C_NSAKV), ("nsaq", 0, C_NSAQ), ("vc", 0, C_NSAKV + 128), ("nsaq", 1, C_NSAQ + 128),
         ("ks", 0, C_NSAKV + 256), ("vs", 0, C_NSAKV + 384), ("kw", 0, C_NSAKV + 512), ("vw", 0, C_NSAKV + 640),
         ("pool", 0, C_POOL), ("pool", 1, C_POOL + 128)]
TILES += [("z", j, C_Z + 128 * j) for j in range(8)]
NT = len(TILES)
AT = {(w, j): m for m, (w, j, _) in enumerate(TILES)}
DVE_TAKES = [sum(1 for w, _, _ in TILES[:m] if w not in ("z", "gate")) for m in range(NT + 1)]
VSI = {("foxv", 0): 0, ("foxv", 1): 1, ("kc", 0): 2, ("vc", 0): 3, ("vs", 0): 4, ("vw", 0): 5,
       ("pool", 0): 6, ("pool", 1): 7}
KNI = {"foxk": 0, "ks": 4, "kw": 6}
QNI = {"foxq": 0, "nsaq": 4, "memq": 8}
O_SLOT = [0, 2, 3, 1]


def attention_units():
    order = [7, 0, 6, 1, 5, 2, 4, 3]
    mem = [("mem", hp, i, 0, 2 * NMEM // P) for i in range(NQ) for hp in range(H // 2)]
    fox = [("fox", h, i, 0, i + 1) for i in order for h in range(H)]
    sel = [("sel", h, i, 0, i + 1) for i2 in range(0, NQ, 2) for h in range(H) for i in order[i2:i2 + 2]]
    win = [("win", h, i, max(0, i - WIN_T), min(i, WIN_T) + 1) for i2 in range(0, NQ, 2)
           for h in range(H) for i in order[i2:i2 + 2]]
    both = [u for a, b in zip(sel, win) for u in (a, b)]
    return mem, fox, both


MEM_U, FOX_U, NSA_U = attention_units()
UNITS = MEM_U + FOX_U + NSA_U
G0 = [0]
for _u in UNITS:
    G0.append(G0[-1] + (_u[4] + 3) // 4)


STEPS = [("item", 0), ("item", 1), ("item", 2), ("item", 3), ("project", 0), ("item", 4),
         ("project", 1), ("natural", 0), ("item", 5), ("project", 2), ("natural", 1), ("item", 6),
         ("project", 3), ("natural", 2), ("item", 7), ("natural", 3), ("item", 8), ("item", 9), ("item", 10),
         ("project", 4), ("project", 5), ("project", 6), ("attend", 0),
         ("gates", 0), ("project", 7), ("project", 8), ("forget", 0), ("pair", 0), ("project", 9), ("pair", 1),
         ("pair", 2), ("project", 10), ("natural", 9), ("project", 11), ("pair", 3), ("natural", 10), ("pair", 4),
         ("project", 12), ("natural", 11), ("pair", 5), ("natural", 12), ("pair", 6), ("pair", 7),
         ("attend", 1),
         ("project", 13), ("project", 14), ("natural", 13), ("compress", 0), ("project", 15), ("compressed", 0),
         ("pair", 8), ("pair", 9), ("pair", 10), ("pair", 11), ("project", 16), ("natural", 15),
         ("pair", 12), ("pair", 13), ("pair", 14), ("pair", 15),
         ("compress", 1), ("project", 17), ("compressed", 1), ("project", 18), ("cmp_scores", 0), ("natural", 17),
         ("project", 19),
         ("natural", 18), ("project", 20), ("cmp_turn", 0), ("natural", 19), ("cmp_out", 0), ("natural", 20),
         ("attend", 2),
         ("project", 21), ("pool_last", 0), ("project", 22), ("pool_last", 1), ("project", 23),
         ("pool_map", 0), ("project", 24), ("sample_new", 0), ("project", 25), ("pool_map", 1), ("sample_keys", 0),
         ("sample_values", 0), ("mix", 0)]
PHASE = [(0, len(MEM_U)), (len(MEM_U), len(MEM_U) + len(FOX_U)), (len(MEM_U) + len(FOX_U), len(UNITS))]


ZK = AT["z", 3]
KEY_JOBS = [[range(10 * i + a, 10 * i + b) for a, b in ((0, 4), (4, 7), (7, 10))] for i in range(4)]


def ahead(u):
    return 4 if UNITS[u][0] == "mem" else 2


def score_bank(u):
    return u % 4 if ahead(u) == 4 else 2 * (u % 2)


def prob_slot(u):
    return u % 4 * 512 if ahead(u) == 4 else u % 2 * 1024


def even(g):
    return (g + 1) // 2


def odd(g):
    return g // 2


def build(nc, x_p, x_s, c_fox, c_lf, c_nsa, st_win, st_pool, c_mem, ptab, mem_p, norm_g, w_in, b_f, pe_, w1,
          w2, pool_w, pool_s, w_mem, w_out, fin_g,
          y_p, y_s, o_foxkv, o_lf, o_nsakv, o_nsawin, o_pool, o_memkv, o_foxkv_s, o_lf_s, o_nsakv_s, o_win_s,
          o_pool_s):
    with ExitStack() as ctx:
        def sb(name, shape, dt=F32):
            return ctx.enter_context(nc.sbuf_tensor(name, shape, dt))

        def sem(name):
            return ctx.enter_context(nc.semaphore(name))

        ctx.enter_context(nc.allow_non_contiguous_dma(reason="small strided rows"))

        HH = sb("HH", [P, KC * TT], F32R)
        HL = sb("HL", [P, KC * TT], F32R)
        WR = sb("WR", [P, 2, KC, P])
        WH = sb("WH", [P, 2, KC, P], F32R)
        WL = sb("WL", [P, 2, KC, P], F32R)
        AUG = sb("AUG", [P, 8, TT])
        XT = sb("XT", [P, TT])
        NAT = sb("NAT", [P, NQ * 512])
        VW = sb("VW", [P, NQ * P])
        KW = sb("KW", [P, 4 * P])
        PP = sb("PP", [P, 4 * 1024])
        OB = sb("OB", [P, 4096 + NJ * (R_ALL + 1)])
        ident = sb("ident", [P, P])
        identb = sb("identb", [P, P], BF16)
        m_diag = sb("m_diag", [P, P], BF16)
        m_win = sb("m_win", [P, P], BF16)
        m_cmp = sb("m_cmp", [P, NQ, NCB], BF16)
        seen0 = sb("seen0", [P, NCB])
        lf = sb("lf", [P, NQ + 1, H])
        fga = sb("fga", [P, NQ + 1, 16])
        bfb = sb("bfb", [P, H])
        stat = sb("stat", [P, 64])
        rms = sb("rms", [P, 32])
        epsc = sb("epsc", [P, 1])
        QKN = sb("QKN", [P, 12, NB])
        QNs, KNs = QKN[0:DH], QKN[DH:P, 0:8]
        VS = sb("VS", [P, 8, NB])
        KCa = sb("KCa", [DH + 2, 2, NCB])
        KCs = sb("KCs", [P, NB * SCB])
        VCP = sb("VCP", [96, 2 * P])
        VCs = VCP[0:NB * SCB, 0:P]
        pes = VCP[64:96, :].rearrange("p (k c) -> p k c", k=2)
        W2 = sb("W2", [P, 2, 2, DH])
        PLW = sb("PLW", [P, 2, DH])
        PLT = sb("PLT", [P, 2, NB])
        rcnt = sb("rcnt", [P, 2, 16])
        peb = sb("peb", [P, 2])
        cs = sb("cs", [P, 96])
        onesc = sb("onesc", [P, 1])
        SLC = sb("SLC", [P, 1])
        BC = sb("BC", [P, SCB])
        GC = sb("GC", [P, 2])
        E8 = sb("E8", [P, NB])
        XC = cs
        ptb = sb("ptb", [1, NB * NPG], I32)
        oTs = VS

        PLS = OB[:, 7168:7296].rearrange("p (j c) -> p j c", j=2)
        slope_row = OB[:, 7296:7424]
        FG = OB[:, 7424:7424 + (NQ + 1) * 16].rearrange("p (t c) -> p t c", t=NQ + 1)

        hh = HH[:, 0:KC * TT].rearrange("p (k t) -> p k t", k=KC)
        hl = HL[:, 0:KC * TT].rearrange("p (k t) -> p k t", k=KC)
        woh = HH[:, 0:KC * D].rearrange("p (k t) -> p k t", k=KC)
        wol = HL[:, 0:KC * D].rearrange("p (k t) -> p k t", k=KC)
        mth, mtl = hh[:, :, T - NMEM:T], hl[:, :, T - NMEM:T]
        TH = WH[:, :, :, :].rearrange("p s k c -> p (s k c)")
        TL = WL[:, :, :, :].rearrange("p s k c -> p (s k c)")
        nat = NAT[:, :].rearrange("p (t c) -> p t c", t=NQ)
        vw = VW[:, :].rearrange("p (t c) -> p t c", t=NQ)
        kw = KW[:, :].rearrange("p (t c) -> p t c", t=4)
        o_nat = OB[:, 0:8192].rearrange("p (g t c) -> p g t c", g=4, t=NQ)
        FT = OB[:, 4096:4096 + NJ * (R_ALL + 1)].rearrange("p (j r) -> p j r", j=NJ)
        xr = OB[:, 0:4096].rearrange("p (s c) -> p s c", s=4)
        xn = OB[:, 4096:6144].rearrange("p (s c) -> p s c", s=2)
        gbc = OB[:, 6144:7168]

        def pair_slot(q):
            if q < 16:
                where = PP[:, q * 256:(q + 1) * 256]
            elif 20 <= q < 28:
                where = NAT[:, (q - 20) * 512 + 256:(q - 19) * 512]
            else:
                where = VW[:, q % 4 * 256:(q % 4 + 1) * 256]
            return where.rearrange("p (a c) -> p a c", a=2)

        w1s = PP[:, :].rearrange("p (s j e) -> p s j e", s=2, j=8)
        HS = KW[:, 0:2 * R_ALL].rearrange("p (a r) -> p a r", a=2)

        PS = ctx.enter_context(nc.psum_tensor("PS", [P, 8, 512], F32))

        def bk(i):
            return PS[:, i, :]

        def flat(b0, blocks):
            if blocks <= 4:
                return bk(b0)[:, 0:blocks * P]
            return PS[:, b0:b0 + 2, :].rearrange("p a c -> p (a c)")[:, 0:blocks * P]

        G2 = NAT[:, 0:2048].rearrange("p (s c) -> p s c", s=2)
        gf = NAT[:, 2048:3072]
        XN8 = XC[:, 80:88]

        def ft_cols(n):
            return FT[:, :, R_PROMPT:R_ALL].rearrange("p j (g b n) -> p b g n j", g=2, b=NB)[:, n]

        def ft_prompt(par, g):
            return FT[par * DH:(par + 1) * DH, :, g * NCB:(g + 1) * NCB].rearrange("p j n -> p n j")

        def xt_pairs(par, g):
            return XT[g * DH:(g + 1) * DH, 0:T].rearrange("p (n j r) -> p r n j", n=NCB, r=2)[:, par]

        def nat_place(what, j):
            return {"memk": (nat, P * j), "memv": (nat, 256 + P * j), "foxk": (nat, P * j),
                    "foxv": (nat, 256 + P * j), "kc": (nat, 0), "vc": (nat, P), "ks": (nat, 256),
                    "vs": (nat, 384), "kw": (kw, 0), "vw": (vw, 0)}[what]

        def nat_free(eng, m):
            if m == 9:
                eng.wait_ge(s_nst, 16)
            if m == 13:
                eng.wait_ge(s_nst, 32)

        def xt_free(eng, m):
            if m in (AT["foxv", 0], AT["foxv", 1]):
                a, d = mark["natural", 11] if m == 12 else mark["gates", 0]
                eng.wait_ge(s_TA, a)
                eng.wait_ge(s_TD, d)

        s_x = [sem(f"s_x{i}") for i in range(4)]
        s_gb = sem("s_gb")
        s_std = sem("s_std")
        s_sq = sem("s_sq")
        s_xn = sem("s_xn")
        s_itT = sem("s_itT")
        s_hi = sem("s_hi")
        s_lo = sem("s_lo")
        s_w = [sem(f"s_w{i}") for i in range(2)]
        s_wcp = sem("s_wcp")
        s_split = sem("s_split")
        s_proj = sem("s_proj")
        s_zp = sem("s_zp")
        s_zt = sem("s_zt")
        s_wo = [sem(f"s_wo{i}") for i in range(4)]
        s_woh = sem("s_woh")
        s_wol = sem("s_wol")
        s_eva = sem("s_eva")
        s_evd = sem("s_evd")
        s_TA = sem("s_TA")
        s_TD = sem("s_TD")
        s_fA = sem("s_fA")
        s_fD = sem("s_fD")
        s_S = sem("s_S")
        s_nm = sem("s_nm")
        s_P = sem("s_P")
        s_pT = sem("s_pT")
        s_cD = sem("s_cD")
        s_cA = sem("s_cA")
        s_pv = sem("s_pv")
        s_on = sem("s_on")
        s_cst = sem("s_cst")
        s_pc = sem("s_pc")
        s_pb = sem("s_pb")
        s_v = sem("s_v")
        s_a = sem("s_a")
        s_fgv = sem("s_fgv")
        s_fga = sem("s_fga")
        s_c = sem("s_c")
        s_aug = sem("s_aug")
        s_st = sem("s_st")
        s_nst = sem("s_nst")
        s_pair = [sem(f"s_pair{n}") for n in range(NB)]
        s_w1 = [sem(f"s_w1{i}") for i in range(2)]
        s_w1u = sem("s_w1u")
        s_fta = sem("s_fta")
        s_ftd = sem("s_ftd")
        s_hs = sem("s_hs")
        s_cm = sem("s_cm")
        s_cmv = sem("s_cmv")
        s_cma = sem("s_cma")
        s_pd = sem("s_pd")
        s_kv = [sem(f"s_kv{i}") for i in range(4)]
        s_lfp = sem("s_lfp")
        s_sd = sem("s_sd")
        s_sS = sem("s_sS")
        s_vr = sem("s_vr")
        s_oT = sem("s_oT")
        s_g = sem("s_g")
        s_gh = sem("s_gh")
        s_gl = sem("s_gl")
        s_y = sem("s_y")
        s_y1 = sem("s_y1")
        s_ys = sem("s_ys")
        s_yo = sem("s_yo")
        s_yst = [sem(f"s_yst{i}") for i in range(2)]
        s_xf = [sem(f"s_xf{i}") for i in range(2)]
        s_pt = sem("s_pt")
        s_wg = sem("s_wg")
        s_lf = sem("s_lf")
        s_gate = sem("s_gate")
        s_qz = sem("s_qz")
        s_psum = sem("s_psum")
        s_psd = sem("s_psd")
        s_stp = sem("s_stp")
        s_lfr = sem("s_lfr")
        s_sx = sem("s_sx")
        s_se = sem("s_se")
        s_px = sem("s_px")
        s_gf = sem("s_gf")

        ring = PP[:, :].rearrange("p (s c) -> p s c", s=4)
        KTA = NAT[:, 0:1024].rearrange("p (s c) -> p s c", s=2)
        KTD = NAT[:, 1024:2048].rearrange("p (s c) -> p s c", s=2)
        QZF = NAT[:, 2048:2560].rearrange("p (a b r) -> p a b r", a=2, b=NB)
        QZM = NAT[:, 2560:3072].rearrange("p (a b r) -> p a b r", a=2, b=NB)
        QZN = NAT[:, 3072:3328].rearrange("p (b r) -> p b r", b=NB)
        KNF = NAT[:, 3328:3344].rearrange("p (a b) -> p a b", a=2)
        KNS = NAT[:, 3344:3352]
        KNW = NAT[:, 3352:3360]
        PTs = NAT[:, 3360:3872].rearrange("p (g r) -> p g r", g=NPG)
        PTn = NAT[0:NB, 3872:4000]
        PTc = NAT[0:NB * SCB, 4000:4032]
        VNEW = VW[0:NB, :]
        KNEW = KW[64:64 + NB, :]
        LFP = KW[0:32, :]
        LFR = XT[0:32, 516:516 + PAST]
        LFT = XT[32:64, 516:516 + PAST + 1]
        CT = XT[64:96, 516:516 + PAST + 1]
        BIAS = XT[:, 0:PAST + 1]
        OT0 = 4096 + 4096
        X = OB[:, OT0:OT0 + PAST + 1]
        poolp = OB[0:15, OT0 + 520:OT0 + 776]
        PSUMS = OB[0:NB, OT0 + 776:OT0 + 1032]
        STP = [PP[0:NB, 3152:3216], PP[0:NB, 3216:3408], PP[0:NB, 3408:3856], NAT[0:NB, 3096:4056]]
        POOLD = NAT[:, 0:2048].rearrange("p (j t) -> p j t", j=2)

        v_ring = [XT[:, 0:1024], PP[:, 2048:2560], PP[:, 2560:3072], PP[:, 3072:3584]]
        XW = WR[:, :, :, :].rearrange("p s k c -> p s (k c)")

        def wo_raw(j):
            if j % 4 < 2:
                return WR[:, (NT + j) % 2, :, :]
            return PP[:, (j % 2) * 1024:(j % 2 + 1) * 1024].rearrange("p (k c) -> p k c", k=KC)

        block = ctx.enter_context(nc.Block())
        mark = {}

        @block.tensor
        def _(pe):
            mm, tr = nc.tensor.matmul, nc.tensor.transpose
            nA, nD = [0], [0]

            def job_a():
                if nA[0]:
                    pe.wait_ge(s_fA, nA[0])
                nA[0] += 1
                return bk(6)

            def job_d():
                if nD[0]:
                    pe.wait_ge(s_fD, nD[0])
                nD[0] += 1
                return bk(7)

            def jobs_taken():
                pe.wait_ge(s_fA, nA[0])
                pe.wait_ge(s_fD, nD[0])

            def item(i):
                rows = NB if i == 10 else P
                if i < 2:
                    pe.wait_ge(s_x[i % 4], 16)
                    src = xr[:, i % 4, :]
                else:
                    pe.wait_ge(s_xn, i - 1)
                    src = xn[0:rows, i % 2, :]
                if i >= 2:
                    pe.wait_ge(s_lo, i - 1)
                for k in range(KC):
                    last = tr(bk(2 * (i % 2) + k // 4)[:, (k % 4) * P:(k % 4) * P + rows],
                              src[:, k * P:(k + 1) * P], ident[0:rows, 0:rows])
                last.then_inc(s_itT, 1)

            def passes(out, lhs, rhs, k, between=None):
                mm(out, lhs[0], rhs[0], start=(k == 0), stop=False)
                if between:
                    next(between, None)
                mm(out, lhs[0], rhs[1], start=False, stop=False)
                if between:
                    next(between, None)
                return mm(out, lhs[1], rhs[0], start=False, stop=(k == KC - 1))

            def project(m):
                what = TILES[m][0]
                s = m % 2
                pe.wait_ge(s_split, m + 1)
                if m >= 2:
                    pe.wait_ge(s_eva, m - 1)
                    pe.wait_ge(s_evd, DVE_TAKES[m - 1])
                if what in ("memk", "memv"):
                    for k in range(KC):
                        last = passes(bk(4 + s)[:, 0:NMEM], (WH[:, s, k, :], WL[:, s, k, :]),
                                      (mth[:, k, :], mtl[:, k, :]), k)
                else:
                    for c in range(3):
                        for k in range(KC):
                            t = slice(c * CH, (c + 1) * CH)
                            last = passes(bk(3 * s + c)[:, 0:CH], (WH[:, s, k, :], WL[:, s, k, :]),
                                          (hh[:, k, t], hl[:, k, t]), k)
                last.then_inc(s_proj, 1)

            def project_chunk(m, c):
                s = m % 2
                if c == 0:
                    pe.wait_ge(s_split, m + 1)
                    taken(m - 1)
                t = slice(c * CH, (c + 1) * CH)
                for k in range(KC):
                    last = passes(bk(1 + c)[:, 0:CH], (WH[:, s, k, :], WL[:, s, k, :]), (hh[:, k, t], hl[:, k, t]), k)
                last.then_inc(s_proj if c == 2 else s_zp, 1)

            def taken(m):
                pe.wait_ge(s_eva, m + 1)
                pe.wait_ge(s_evd, DVE_TAKES[m + 1])

            def natural(m):
                what = TILES[m][0]
                taken(m)
                halves = {"memk": ((0,), (1,)), "memv": ((0,), (1,)), "kw": ((4, 5), (6, 7))}.get(
                    what, (range(4), range(4, 8)))
                for side, tiles in enumerate(halves):
                    out = job_a() if side == 0 else job_d()
                    for n, t in enumerate(tiles):
                        if what in ("memk", "foxk", "ks", "kw"):
                            slot = 4 + {"memk": 2 * TILES[m][1], "foxk": 2 * TILES[m][1], "ks": 0, "kw": 2}[what]
                            for a in range(2):
                                last = tr(out[:, n * P + a * DH:n * P + a * DH + DH],
                                          AUG[0:DH, slot + a, t * P:(t + 1) * P], ident[0:DH, 0:DH])
                        else:
                            last = tr(out[:, n * P:(n + 1) * P], XT[:, t * P:(t + 1) * P], ident[:, :])
                    last.then_inc(s_TA if side == 0 else s_TD, 1)

            def scores(u):
                what, h, i, k0, nk = UNITS[u]
                if u >= ahead(u):
                    pe.wait_ge(s_P, u - ahead(u) + 1)
                s0 = score_bank(u)
                if what == "mem":
                    for e in range(2):
                        last = mm(bk(s0)[:, e * NMEM:(e + 1) * NMEM], AUG[0:DH, 2 * h + e, i * P:(i + 1) * P],
                                  AUG[0:DH, 4 + 2 * h + e, 0:NMEM], start=True, stop=True)
                    last.then_inc(s_S, 1)
                    return
                rows = DH + 2
                slot = {"fox": 4 + h, "sel": 4 + h // 2, "win": 6 + h // 2}[what]
                masks = {nk - 1: m_diag}
                if what == "win" and i >= WIN_T:
                    masks[0] = m_win
                for c in range(0, nk, 4):
                    n = min(4, nk - c)
                    inside = [b for b in masks if c <= b < c + n]
                    last = mm(bk(s0 + c // 4)[:, 0:n * P], AUG[0:rows, h, i * P:(i + 1) * P],
                              AUG[0:rows, slot, (k0 + c) * P:(k0 + c + n) * P], start=True, stop=not inside)
                    for b in inside:
                        last = mm(bk(s0 + c // 4)[:, (b - c) * P:(b - c + 1) * P], identb[:, :], masks[b][:, :],
                                  start=False, stop=(b == inside[-1]))
                last.then_inc(s_S, 1)

            def transpose_p(u):
                nk = UNITS[u][4]
                pe.wait_ge(s_P, u + 1)
                for c in range(0, nk, 4):
                    g = G0[u] + c // 4
                    if g >= 2:
                        pe.wait_ge(s_cA if g % 2 else s_cD, odd(g - 1) if g % 2 else even(g - 1))
                    for b in range(c, min(c + 4, nk)):
                        last = tr(bk(4 + g % 2)[:, (b - c) * P:(b - c + 1) * P],
                                  PP[:, prob_slot(u) + b * P:prob_slot(u) + (b + 1) * P], ident[:, :])
                    last.then_inc(s_pT, 1)

            def weigh_v(u):
                what, h, i, k0, nk = UNITS[u]
                if even(G0[u + 1]):
                    pe.wait_ge(s_cD, even(G0[u + 1]))
                if odd(G0[u + 1]):
                    pe.wait_ge(s_cA, odd(G0[u + 1]))
                if u >= 2:
                    pe.wait_ge(s_on, u - 1)
                for b in range(nk):
                    if what == "mem":
                        e, t = b // 2, b % 2
                        last = mm(bk(6 + u % 2)[:, e * DH:(e + 1) * DH],
                                  PP[:, 2048 + prob_slot(u) + b * P:2048 + prob_slot(u) + (b + 1) * P],
                                  nat[:, t, 256 + (2 * h + e) * DH:256 + (2 * h + e + 1) * DH],
                                  start=(t == 0), stop=(t == 1))
                        continue
                    t = k0 + b
                    v = {"fox": nat[:, t, 256 + h * DH:256 + (h + 1) * DH],
                         "sel": nat[:, t, 384 + (h // 2) * DH:384 + (h // 2 + 1) * DH],
                         "win": vw[:, t, (h // 2) * DH:(h // 2 + 1) * DH]}[what]
                    last = mm(bk(6 + u % 2)[:, 0:DH],
                              PP[:, 2048 + prob_slot(u) + b * P:2048 + prob_slot(u) + (b + 1) * P], v,
                              start=(b == 0), stop=(b == nk - 1))
                last.then_inc(s_pv, 1)

            def attend(u0, u1):
                pe.wait_ge(s_fA, nA[0])
                pe.wait_ge(s_fD, nD[0])
                n = ahead(u0)
                for u in range(u0, u0 + n):
                    scores(u)
                for u in range(u0, u1):
                    transpose_p(u)
                    if u > u0:
                        weigh_v(u - 1)
                    if u + n < u1:
                        scores(u + n)
                weigh_v(u1 - 1)
                pe.wait_ge(s_on, u1)
                if even(G0[u1]):
                    pe.wait_ge(s_cD, even(G0[u1]))
                if odd(G0[u1]):
                    pe.wait_ge(s_cA, odd(G0[u1]))

            def pair_job(n, kind):
                out = job_a() if n % 2 == 0 else job_d()
                pe.wait_ge(s_pair[n], 128 * (kind + 1))
                for a in range(2):
                    q = 16 * kind + 2 * n + a
                    for g in range(2):
                        last = tr(out[:, (2 * g + a) * P:(2 * g + a + 1) * P],
                                  pair_slot(q)[:, g, :], ident[:, :])
                last.then_inc(s_TA if n % 2 == 0 else s_TD, 1)
                mark["pair", kind, n] = (s_TA, nA[0]) if n % 2 == 0 else (s_TD, nD[0])

            def compress(kind):
                out = job_d()
                tr(out[:, 0:NJ], pes[:, kind, :], ident[64:96, 64:96]).then_inc(s_TD, 1)
                jobs_taken()
                pe.wait_ge(s_fta, kind + 1)
                pe.wait_ge(s_ftd, kind + 1)
                for c in range(4):
                    n = 4 * kind + c
                    pe.wait_ge(s_w1[n % 2], 16 * (n // 2 + 1))
                    for jj in range(8):
                        j = 8 * c + jj
                        for e in range(2):
                            last = mm(bk(e)[:, 0:R_ALL + 1], w1s[:, n % 2, jj, e * P:(e + 1) * P], FT[:, j, :],
                                      start=(j == 0), stop=(j == NJ - 1))
                    last.then_inc(s_w1u, 1)

            def compress_out(kind):
                pe.wait_ge(s_hs, kind + 1)
                if kind == 0:
                    out = job_a()
                    for a in range(2):
                        mm(out[0:DH, 0:R_PROMPT], W2[:, 0, a, :], HS[:, a, 0:R_PROMPT], start=(a == 0), stop=(a == 1))
                    for g in range(2):
                        c0 = R_PROMPT + g * NB * SCB
                        for a in range(2):
                            last = mm(out[g * DH:(g + 1) * DH, 64:64 + NB * SCB], W2[:, 0, a, :],
                                      HS[:, a, c0:c0 + NB * SCB], start=(a == 0), stop=(a == 1))
                    last.then_inc(s_TA, 1)
                else:
                    out = job_d()
                    for h in range(H):
                        g = h // 2
                        for a in range(2):
                            mm(out[32 * h:32 * h + NCB, h * DH:(h + 1) * DH], HS[:, a, g * NCB:(g + 1) * NCB],
                               W2[:, 1, a, :], start=(a == 0), stop=(a == 1))
                    for g in range(2):
                        c0 = R_PROMPT + g * NB * SCB
                        for a in range(2):
                            last = mm(out[0:NB * SCB, 256 + g * DH:256 + (g + 1) * DH], HS[:, a, c0:c0 + NB * SCB],
                                      W2[:, 1, a, :], start=(a == 0), stop=(a == 1))
                    last.then_inc(s_TD, 1)

            def gates():
                taken(6)
                out = job_d()
                for t in range(NQ + 1):
                    rows = NB if t == NQ else P
                    last = tr(out[0:rows, t * 16:(t + 1) * 16], XT[0:16, t * P:t * P + rows], ident[0:16, 0:16])
                last.then_inc(s_TD, 1)

            def forget_t():
                pe.wait_ge(s_lf, 1)
                for half in range(2):
                    out = job_d()
                    for t in range(4):
                        last = tr(out[0:H, t * P:(t + 1) * P], lf[:, 4 * half + t, :], ident[:, :])
                    last.then_inc(s_TD, 1)

            def cmp_scores():
                pe.wait_ge(s_aug, 48)
                jobs_taken()
                taken(16)
                out = job_d()
                for i in range(NQ):
                    for h in range(H):
                        last = mm(out[:, (4 * i + h) * NCB:(4 * i + h + 1) * NCB],
                                  AUG[0:DH + 2, h, i * P:(i + 1) * P], KCa[:, h // 2, :], start=True, stop=True)
                last.then_inc(s_TD, 1)

            def cmp_turn():
                pe.wait_ge(s_cm, 1)
                for half in range(2):
                    out = job_a() if half == 0 else job_d()
                    for t in range(4 * half, 4 * half + 4):
                        last = tr(out[:, (t % 4) * P:(t % 4 + 1) * P], PP[:, 1024 + t * P:1024 + (t + 1) * P], ident[:, :])
                    last.then_inc(s_TA if half == 0 else s_TD, 1)

            def cmp_out():
                jobs_taken()
                for q in range(4):
                    out = job_a() if q % 2 == 0 else job_d()
                    for a in range(2):
                        i = 2 * q + a
                        last = mm(out[:, a * 256:(a + 1) * 256], PP[:, 2048 + i * P:2048 + (i + 1) * P],
                                  PP[:, 3072:3072 + 256], start=True, stop=True)
                    last.then_inc(s_TA if q % 2 == 0 else s_TD, 1)

            def pool_last(j):
                taken(21 + j)
                out = job_d()
                tr(out[0:15, 0:P], PP[:, j * 1056 + T:j * 1056 + T + 15], ident[:, :]).then_inc(s_TD, 1)

            def pool_map(j):
                pe.wait_ge(s_pd, j + 1)
                for half in range(2):
                    for a in range(2):
                        out = job_a() if a == 0 else job_d()
                        for n in range(4):
                            t = 4 * half + n
                            last = mm(out[:, n * DH:(n + 1) * DH], POOLD[a * DH:(a + 1) * DH, j, t * P:(t + 1) * P],
                                      PLW[a * DH:(a + 1) * DH, j, :], start=True, stop=True)
                        last.then_inc(s_TA if a == 0 else s_TD, 1)

            def sample_new():
                for q in range(2):
                    out = job_a() if q == 0 else job_d()
                    for n in range(4):
                        last = tr(out[0:NB, n * P:(n + 1) * P], VS[:, 4 * q + n, :], ident[:, :])
                    last.then_inc(s_TA if q == 0 else s_TD, 1)
                out = job_a()
                for n in range(8):
                    last = tr(out[0:NB, n * DH:(n + 1) * DH], KNs[:, n, :], ident[DH:P, DH:P])
                last.then_inc(s_TA, 1)

            JOBS = [("A", 0, [(pg, 0) for pg in range(4)]), ("D", 0, [(pg, 1) for pg in range(4)]),
                    ("A", 1, [(pg, 0) for pg in range(4)]), ("D", 2, [(pg, 0) for pg in range(4)]),
                    ("A", 3, [(pg, a) for a in range(2) for pg in range(2)])]
            NTH = [0, 0, 1, 1, 2]

            def keys_t(b, jn):
                side, br, blocks = JOBS[jn]
                width = 256 if br in (0, 3) else P
                pe.wait_ge(s_kv[br], (64 if br in (0, 1) else 16) * (b + 1))
                out = job_a() if side == "A" else job_d()
                for n, (pg, a) in enumerate(blocks):
                    last = tr(out[:, n * P:(n + 1) * P], ring[:, br, pg * width + a * P:pg * width + a * P + P],
                              ident[:, :])
                last.then_inc(s_TA if side == "A" else s_TD, 1)

            def key_scores(b, jn):
                side, br, _ = JOBS[jn]
                n = (3 if side == "A" else 2) * b + NTH[jn]
                if side == "A":
                    pe.wait_ge(s_fA, mark["K"][0] + n + 1)
                else:
                    pe.wait_ge(s_fD, mark["K"][1] + n + 1)
                kt = (KTA if side == "A" else KTD)[:, n % 2, :]
                rows = slice(32 * br, 32 * br + 32)
                if br == 0:
                    a = jn
                    last = mm(PS[rows, 0, :], QZF[:, a, b, :], kt, start=(b == 0 and a == 0),
                              stop=(b == NB - 1 and a == 1))
                elif br == 3:
                    for a in range(2):
                        last = mm(PS[rows, 0, 0:256], QZM[:, a, b, :], kt[:, a * 256:(a + 1) * 256],
                                  start=(b == 0 and a == 0), stop=(b == NB - 1 and a == 1))
                else:
                    last = mm(PS[rows, 0, :], QZN[:, b, :], kt, start=(b == 0), stop=(b == NB - 1))
                last.then_inc(s_sS, 1)

            def sample_keys():
                jobs_taken()
                pe.wait_ge(s_qz, 1)
                mark["K"] = (nA[0], nD[0])
                for i in range(4):
                    for c in range(3):
                        project_chunk(ZK + i, c)
                        for n in KEY_JOBS[i][c]:
                            keys_t(n // 5, n % 5)
                            if n:
                                key_scores((n - 1) // 5, (n - 1) % 5)
                key_scores(NB - 1, 4)
                for b in range(NB):
                    for a in range(2):
                        mm(PS[0:32, 4, 0:1], QZF[:, a, b, :], KNF[:, a, b:b + 1], start=(b == 0 and a == 0),
                           stop=(b == NB - 1 and a == 1))
                for b in range(NB):
                    mm(PS[32:64, 4, 0:1], QZN[:, b, :], KNS[:, b:b + 1], start=(b == 0), stop=(b == NB - 1))
                for b in range(NB):
                    mm(PS[64:96, 4, 0:1], QZN[:, b, :], KNW[:, b:b + 1], start=(b == 0), stop=(b == NB - 1))
                for b in range(NB):
                    last = mm(PS[0:32, 5, 0:SCB], QZN[:, b, :], KCs[:, b * SCB:(b + 1) * SCB], start=(b == 0),
                              stop=(b == NB - 1))
                last.then_inc(s_sS, 1)

            def sample_values():
                for c in range(3):
                    project_chunk(NT - 1, c)
                pe.wait_ge(s_px, 1)
                out = job_a()
                for pg in range(NPG):
                    last = tr(out[:, pg * P:(pg + 1) * P], X[:, pg * P:(pg + 1) * P], ident[:, :])
                last.then_inc(s_TA, 1)
                out = job_d()
                tr(out[0:NB, 0:P], XN8[:, :], ident[:, :])
                tr(out[0:NB * SCB, P:P + 32], XC[0:32, 16:16 + NB * SCB], ident[0:32, 0:32]).then_inc(s_TD, 1)
                pe.wait_ge(s_psd, 1)
                out = job_a()
                for j in range(2):
                    last = tr(out[:, j * NB:(j + 1) * NB], PSUMS[:, j * P:(j + 1) * P], ident[0:NB, 0:NB])
                last.then_inc(s_TA, 1)
                jobs_taken()
                out = job_d()
                for j in range(2):
                    for a in range(2):
                        last = mm(out[a * DH:(a + 1) * DH, j * NB:(j + 1) * NB], PLW[a * DH:(a + 1) * DH, j, :],
                                  PLT[a * DH:(a + 1) * DH, j, :], start=True, stop=True)
                last.then_inc(s_TD, 1)

            def values(b):
                c = 4 * b

                def weigh(dst, new, tiles):
                    for n, (lhs, rhs) in enumerate(new):
                        mm(dst, lhs, rhs, start=(n == 0), stop=False)
                        yield
                    for n, (br, width, a, npg, p0) in enumerate(tiles):
                        pe.wait_ge(s_kv[br], (64 if br in (0, 1) else 16) * (NB + b + 1))
                        for pg in range(npg):
                            last = mm(dst, v_ring[br][:, pg * width + a * P:pg * width + a * P + P],
                                      PTs[:, pg, p0:p0 + dst.shape[1]], start=(not new and n == 0 and pg == 0),
                                      stop=(n == len(tiles) - 1 and pg == npg - 1))
                            if pg == npg - 1 and (br in (1, 2) or a == 1):
                                last.then_inc(s_vr, 1)
                            yield

                for a in range(2):
                    q = c + 2 * a
                    yield from weigh(bk(6)[:, 32 * a + q:32 * a + q + 2], [(VNEW[:, a * P:(a + 1) * P], PTn[:, q:q + 2])],
                          [(0, 256, a, NPG, q)])
                yield from weigh(bk(6)[:, 64 + c:68 + c],
                      [(VNEW[:, 4 * P:5 * P], PTn[:, 32 + c:36 + c]), (VNEW[:, 5 * P:6 * P], PTn[:, 64 + c:68 + c]),
                       (VCs[:, :], PTc[:, c:c + 4])],
                      [(1, P, 0, NPG, 32 + c), (2, P, 0, NPG, 64 + c)])
                for a in range(2):
                    q = c + 2 * a
                    yield from weigh(bk(6)[:, 96 + 32 * a + q:98 + 32 * a + q], [], [(3, 256, a, 2, 96 + q)])

            def turn(t):
                if t:
                    pe.wait_ge(s_g, t)
                for c in range(KC):
                    last = tr(bk(4 + c // 4)[:, (c % 4) * P:(c % 4 + 1) * P],
                              o_nat[:, O_SLOT[c // 2], t, (c % 2) * P:(c % 2 + 1) * P], ident[:, :])
                last.then_inc(s_oT, 1)

            def mix():
                jobs_taken()
                turn(0)
                for _ in values(0):
                    pass
                taken(NT - 1)
                pe.wait_ge(s_wol, KC)
                for t in range(NQ + 1):
                    if t + 1 < NQ:
                        turn(t + 1)
                    samples = values(t + 1) if t + 1 < NB else None
                    pe.wait_ge(s_gl, t + 1)
                    if t >= 2:
                        pe.wait_ge(s_y1, t - 1)
                    s = t % 2
                    for half in range(2):
                        for k in range(KC):
                            sl = slice(s * 1024 + k * P, s * 1024 + (k + 1) * P)
                            c = slice(half * 512, (half + 1) * 512)
                            last = passes(bk(2 * s + half), (TH[:, sl], TL[:, sl]), (woh[:, k, c], wol[:, k, c]), k,
                                          samples)
                    last.then_inc(s_y, 1)

            for step, n in STEPS:
                if step == "item":
                    if n == 0:
                        pe.wait_ge(s_pc, 1)
                    item(n)
                elif step == "project":
                    if n == 0:
                        pe.wait_ge(s_lo, 2)
                    if n == 4:
                        pe.wait_ge(s_lo, 11)
                    project(n)
                elif step == "natural":
                    natural(n)
                elif step == "pair":
                    pair_job(n % 8, n // 8)
                elif step == "attend":
                    if n == 0:
                        taken(6)
                        attend(0, len(MEM_U))
                    elif n == 1:
                        taken(12)
                        pe.wait_ge(s_aug, 32)
                        attend(len(MEM_U), len(MEM_U) + len(FOX_U))
                    else:
                        taken(20)
                        attend(len(MEM_U) + len(FOX_U), len(UNITS))
                elif step == "gates":
                    gates()
                elif step == "forget":
                    forget_t()
                elif step == "compress":
                    taken(14 if n == 0 else 16)
                    compress(n)
                elif step == "compressed":
                    compress_out(n)
                elif step == "cmp_scores":
                    cmp_scores()
                elif step == "cmp_turn":
                    cmp_turn()
                elif step == "cmp_out":
                    cmp_out()
                elif step == "pool_last":
                    pool_last(n)
                elif step == "pool_map":
                    pool_map(n)
                elif step == "sample_new":
                    sample_new()
                elif step == "sample_keys":
                    sample_keys()
                elif step == "sample_values":
                    sample_values()
                elif step == "mix":
                    mix()
                mark[step, n] = (nA[0], nD[0])

        @block.scalar
        def _(act):
            act1 = nc.scalar.activation
            nA, own = [0], [0]

            def link(ins):
                own[0] += 1
                ins.then_inc(s_a, 1)
                act.wait_ge(s_a, own[0])

            def job():
                nA[0] += 1
                act.wait_ge(s_TA, nA[0])
                return bk(6)

            def done(ins):
                ins.then_inc(s_fA, 1)

            def copy(out, in_, scale=None):
                if scale is None:
                    return act1(out, in_, ACT.Copy)
                return act1(out, in_, ACT.Copy, scale=scale)

            def square(i):
                j = i - 2
                rows = NB if i == 10 else P
                act.wait_ge(s_x[i % 4], 16 * (i // 4 + 1))
                if j == 0:
                    act.wait_ge(s_pc, 1)
                act1(NAT[0:rows, 3072:4096], xr[0:rows, i % 4, :], ACT.Square,
                     accum_out=rms[0:rows, j:j + 1]).then_inc(s_sq, 1)
                act.wait_ge(s_sq, j + 1)
                act1(rms[0:rows, 16 + j:17 + j], rms[0:rows, j:j + 1], ACT.Sqrt, bias=epsc[0:rows, :],
                     scale=1.0 / D).then_inc(s_std, 1)

            def hi(i):
                rows = NB if i == 10 else P
                act.wait_ge(s_itT, i + 1)
                src = PS[:, 2 * (i % 2):2 * (i % 2) + 2, :].rearrange("p a (k t) -> p (a k) t", k=4)[:, :, 0:rows]
                dst = mth[:, :, i * P:(i + 1) * P] if i < 2 else hh[:, :, (i - 2) * P:(i - 2) * P + rows]
                copy(dst, src).then_inc(s_hi, 1)

            def take(m):
                what, j, _ = TILES[m]
                s = m % 2
                act.wait_ge(s_proj, m + 1)
                src = PS[0:DH, 3 * s:3 * s + 3, 0:CH]
                news = PS[0:DH, 3 * s + 2, CH - NB:CH]
                cut = lambda ap: ap.rearrange("p (c t) -> p c t", c=3)
                if what == "gate":
                    act.wait_ge(s_TD, mark["natural", 3][1])
                    copy(cut(XT[0:16, :]), PS[0:16, 3 * s:3 * s + 3, 0:CH]).then_inc(s_eva, 1)
                elif what == "z":
                    act1(cut(AUG[:, j, :]), PS[:, 3 * s:3 * s + 3, 0:CH], ACT.Silu).then_inc(s_eva, 1)
                elif what == "memk":
                    copy(AUG[0:DH, 4 + 2 * j, 0:NMEM], bk(4 + s)[0:DH, 0:NMEM]).then_inc(s_eva, 1)
                elif what == "memv":
                    if j:
                        act.wait_ge(s_TA, 3)
                        act.wait_ge(s_TD, 3)
                    copy(XT[0:DH, 0:NMEM], bk(4 + s)[0:DH, 0:NMEM]).then_inc(s_eva, 1)
                elif what in QNI:
                    copy(QNs[:, QNI[what] + 2 * j, :], news, SCALE)
                    copy(cut(AUG[0:DH, 2 * j, :]), src, SCALE).then_inc(s_eva, 1)
                elif what in KNI:
                    slot = {"foxk": 4 + 2 * j, "ks": 4, "kw": 6}[what]
                    copy(KNs[:, KNI[what] + 2 * j, :], news)
                    copy(cut(AUG[0:DH, slot, :]), src).then_inc(s_eva, 1)
                else:
                    copy(VS[0:DH, VSI[what, j], :], news)
                    if what == "pool":
                        copy(cut(PP[0:DH, j * 1056 + 15:j * 1056 + 15 + TT]), src).then_inc(s_eva, 1)
                    else:
                        xt_free(act, m)
                        copy(cut(XT[0:DH, :]), src).then_inc(s_eva, 1)

            def take_chunk(m, c):
                if c == 2:
                    act.wait_ge(s_proj, m + 1)
                else:
                    act.wait_ge(s_zp, 2 * (m - ZK) + c + 1)
                act1(AUG[:, TILES[m][1], c * CH:(c + 1) * CH], bk(1 + c)[:, 0:CH],
                     ACT.Silu).then_inc(s_eva if c == 2 else s_zt, 1)

            def natural(m):
                what, j, _ = TILES[m]
                out = job()
                nat_free(act, m)
                n = {"memk": 1, "memv": 1, "kw": 2}.get(what, 4)
                dst, c = nat_place(what, j)
                copy(dst[:, 0:n, c:c + P], out[:, 0:n * P].rearrange("p (t c) -> p t c", c=P)).then_inc(s_fA, 1)

            def attend(u0, u1):
                n = ahead(u0)
                for u in range(u0, u1 + n - 1):
                    if u < u1:
                        act.wait_ge(s_nm, u + 1)
                        if u >= n:
                            act.wait_ge(s_pT, G0[u - n + 1])
                        c, nk, k = prob_slot(u), UNITS[u][4], u % 8
                        if UNITS[u][0] == "mem":
                            for e in range(2):
                                k = 2 * (u % 8) + e
                                last = act1(PP[:, c + e * NMEM:c + (e + 1) * NMEM],
                                            bk(score_bank(u))[:, e * NMEM:(e + 1) * NMEM], ACT.Exp,
                                            bias=stat[:, k:k + 1], accum_out=stat[:, 16 + k:17 + k])
                            last.then_inc(s_P, 1)
                        else:
                            act1(PP[:, c:c + nk * P], flat(score_bank(u), nk), ACT.Exp, bias=stat[:, k:k + 1],
                                 accum_out=stat[:, 16 + k:17 + k]).then_inc(s_P, 1)
                    v = u - n + 1
                    if v >= u0:
                        for g in range(G0[v], G0[v + 1]):
                            if g % 2:
                                act.wait_ge(s_pT, g + 1)
                                if v >= n:
                                    act.wait_ge(s_pv, v - n + 1)
                                c = 4 * (g - G0[v])
                                blocks = min(4, UNITS[v][4] - c)
                                o = 2048 + prob_slot(v) + c * P
                                copy(PP[:, o:o + blocks * P], bk(5)[:, 0:blocks * P]).then_inc(s_cA, 1)

            def const(dst, src):
                act.dma_start(dst, src).then_inc(s_cst, 16)

            act.dma_start(gbc, norm_g.partition_broadcast(P)).then_inc(s_gb, 16)
            const(bfb[:, :], b_f.partition_broadcast(P))
            const(pes[:, :, :], pe_[0].rearrange("k (j r) d -> j k (r d)", r=2))
            const(W2[:, :, :, :], w2[0].rearrange("k (a p) d -> p k a d", p=P))
            const(PLW[:, :, :], pool_w[0].rearrange("(j a) c e -> (a c) j e", a=2))
            for a in range(2):
                const(PLS[a * DH:(a + 1) * DH, :, :],
                      pool_s.rearrange("o (j a e) -> o a j e", a=2, e=DH)[:, a].partition_broadcast(DH))
            for step, n in STEPS:
                if step == "item":
                    if n < 9:
                        square(n + 2)
                    hi(n)
                elif step == "project":
                    take(n)
                elif step == "natural":
                    natural(n)
                elif step == "pair" and n % 2 == 0:
                    out = job()
                    if n >= 8:
                        act.wait_ge(s_w1u, 4)
                    done(copy(ft_cols(n % 8), out.rearrange("p (g n j) -> p g n j", g=2, n=8)))
                elif step == "attend":
                    attend(*PHASE[n])
                elif step == "gates":
                    act.wait_ge(s_fgv, 1)
                    act1(fga[:, :, 0:H], fga[:, :, 0:H], ACT.Exp, scale=-1.0)
                    act1(fga[:, :, H:16], FG[:, :, H:16], ACT.Exp, scale=-1.0).then_inc(s_fga, 1)
                    act.wait_ge(s_fga, 1)
                    act1(fga[:, :, 0:H], fga[:, :, 0:H], ACT.Ln, bias=1.0).then_inc(s_fga, 1)
                elif step == "compress":
                    act.wait_ge(s_eva, AT["vc" if n else "kc", 0] + 1)
                    if n:
                        act.wait_ge(s_w1u, 4)
                    for par in range(2):
                        last = copy(ft_prompt(par, 0), xt_pairs(par, 0))
                    last.then_inc(s_fta, 1)
                    act.wait_ge(s_w1u, 4 * (n + 1))
                    for a in range(2):
                        link(copy(peb[:, a:a + 1], bk(a)[:, R_ALL:R_ALL + 1]))
                    for a in range(2):
                        last = act1(HS[:, a, :], bk(a)[:, 0:R_ALL], ACT.Silu, bias=peb[:, a:a + 1])
                    last.then_inc(s_hs, 1)
                elif step == "compressed":
                    if n == 0:
                        out = job()
                        copy(KCa[0:DH, :, :], out[0:DH, 0:R_PROMPT].rearrange("p (g n) -> p g n", g=2))
                        done(copy(KCs[:, :], out[:, 64:64 + NB * SCB]))
                elif step == "cmp_scores":
                    act.wait_ge(s_cmv, 1)
                    act1(PP[:, 0:512], PP[:, 0:512], ACT.Exp).then_inc(s_cma, 1)
                elif step == "cmp_turn":
                    out = job()
                    done(copy(PP[:, 2048:2560], out))
                elif step == "cmp_out":
                    for q in (0, 2):
                        out = job()
                        done(copy(o_nat[:, 2, 2 * q:2 * q + 2, :], out.rearrange("p (t c) -> p t c", t=2)))
                elif step == "pool_map":
                    for half in range(2):
                        out = job()
                        done(copy(o_nat[:, 3, 4 * half:4 * half + 4, n * P:n * P + DH],
                                  out[:, 0:256].rearrange("p (t c) -> p t c", t=4)))
                elif step == "sample_new":
                    out = job()
                    act.wait_ge(s_nst, 80)
                    done(copy(VNEW[:, 0:512], out[0:NB, :]))
                    out = job()
                    done(copy(KNEW, out[0:NB, :]))
                elif step == "sample_keys":
                    act.wait_ge(s_qz, 1)
                    q = 0
                    for i in range(4):
                        for c in range(3):
                            take_chunk(ZK + i, c)
                            for n in KEY_JOBS[i][c]:
                                if n % 5 not in (0, 2, 4):
                                    continue
                                out = job()
                                if q >= 2:
                                    act.wait_ge(s_sS, 5 * ((q - 2) // 3) + 2 * ((q - 2) % 3) + 1)
                                done(copy(KTA[:, q % 2, :], out))
                                q += 1
                elif step == "sample_values":
                    take_chunk(NT - 1, 0)
                    act.wait_ge(s_sx, 1)
                    act1(X[:, :], X[:, :], ACT.Exp, bias=XC[:, 0:1], accum_out=XC[:, 1:2])
                    act1(XC[0:32, 8:16], XC[0:32, 8:16], ACT.Exp, bias=XC[0:32, 4:5],
                         accum_out=XC[0:32, 5:6]).then_inc(s_se, 1)
                    take_chunk(NT - 1, 1)
                    take_chunk(NT - 1, 2)
                    out = job()
                    done(copy(PTs.rearrange("p g r -> p (g r)"), out))
                    out = job()
                    done(copy(PLT.rearrange("p j b -> p (j b)"), out[:, 0:2 * NB]))
                    for j in range(KC):
                        act.wait_ge(s_wo[j % 4], 16 * (j // 4 + 1))
                        copy(woh[:, :, j * P:(j + 1) * P], wo_raw(j)).then_inc(s_woh, 1)
                elif step == "mix":
                    def hi_part(t):
                        cols = NB if t == NQ else P
                        act.wait_ge(s_g, t + 1)
                        if t >= 2:
                            act.wait_ge(s_y, t - 1)
                        gg = G2[:, t % 2, :].rearrange("p (k c) -> p k c", k=KC)[:, :, 0:cols]
                        hv = TH[:, (t % 2) * 1024:(t % 2 + 1) * 1024].rearrange("p (k c) -> p k c", k=KC)[:, :, 0:cols]
                        copy(hv, gg).then_inc(s_gh, 1)

                    hi_part(0)
                    for t in range(NQ + 1):
                        if t < NQ:
                            hi_part(t + 1)
                        rows = NB if t == NQ else P
                        s = t % 2
                        act.wait_ge(s_y1, t + 1)
                        act1(XW[0:rows, s, :], PP[0:rows, s * 1024:(s + 1) * 1024], ACT.Square,
                             accum_out=rms[0:rows, t:t + 1]).then_inc(s_sq, 1)
                        act.wait_ge(s_sq, NQ + 2 + t)
                        act1(rms[0:rows, 16 + t:17 + t], rms[0:rows, t:t + 1], ACT.Sqrt, bias=epsc[0:rows, :],
                             scale=1.0 / D).then_inc(s_ys, 1)
                assert (step, n) not in mark or mark[step, n][0] == nA[0], (step, n, mark[step, n], nA)

        @block.vector
        def _(dve):
            v = nc.vector
            nD, own = [0], [0]

            def link(ins):
                own[0] += 1
                ins.then_inc(s_v, 1)
                dve.wait_ge(s_v, own[0])

            def job():
                nD[0] += 1
                dve.wait_ge(s_TD, nD[0])
                return bk(7)

            def done(ins):
                ins.then_inc(s_fD, 1)

            def normalise(i):
                j = i - 2
                rows = NB if i == 10 else P
                dve.wait_ge(s_std, j + 1)
                dve.wait_ge(s_x[i % 4], 16 * (i // 4 + 1))
                if j == 0:
                    dve.wait_ge(s_gb, 16)
                if j >= 2:
                    dve.wait_ge(s_itT, i - 1)
                link(v.reciprocal(rms[0:rows, 16 + j:17 + j], rms[0:rows, 16 + j:17 + j]))
                v.scalar_tensor_tensor(out=xn[0:rows, j % 2, :], in0=xr[0:rows, i % 4, :],
                                       scalar=rms[0:rows, 16 + j:17 + j], in1=gbc[0:rows, :],
                                       op0=ALU.mult, op1=ALU.mult).then_inc(s_xn, 1)

            def lo(i):
                rows = NB if i == 10 else P
                dve.wait_ge(s_hi, i + 1)
                src = PS[:, 2 * (i % 2):2 * (i % 2) + 2, :].rearrange("p a (k t) -> p (a k) t", k=4)[:, :, 0:rows]
                if i < 2:
                    a, b = mth[:, :, i * P:(i + 1) * P], mtl[:, :, i * P:(i + 1) * P]
                else:
                    t = slice((i - 2) * P, (i - 2) * P + rows)
                    a, b = hh[:, :, t], hl[:, :, t]
                v.tensor_tensor(b, src, a.bitcast(F32), ALU.subtract).then_inc(s_lo, 1)

            def take(m):
                what, j, _ = TILES[m]
                if what in ("z", "gate"):
                    return
                s = m % 2
                dve.wait_ge(s_proj, m + 1)
                src = PS[DH:P, 3 * s:3 * s + 3, 0:CH]
                news = PS[DH:P, 3 * s + 2, CH - NB:CH]
                cut = lambda ap: ap.rearrange("p (c t) -> p c t", c=3)
                if what == "memk":
                    last = v.tensor_copy(AUG[0:DH, 5 + 2 * j, 0:NMEM], bk(4 + s)[DH:P, 0:NMEM])
                elif what == "memv":
                    if j:
                        dve.wait_ge(s_TA, 3)
                        dve.wait_ge(s_TD, 3)
                    last = v.tensor_copy(XT[DH:P, 0:NMEM], bk(4 + s)[DH:P, 0:NMEM])
                elif what in QNI:
                    v.tensor_scalar(QNs[:, QNI[what] + 2 * j + 1, :], news, SCALE, None, ALU.mult)
                    last = v.tensor_scalar(cut(AUG[0:DH, 2 * j + 1, :]), src, SCALE, None, ALU.mult)
                elif what in KNI:
                    slot = {"foxk": 5 + 2 * j, "ks": 5, "kw": 7}[what]
                    v.tensor_copy(KNs[:, KNI[what] + 2 * j + 1, :], news)
                    last = v.tensor_copy(cut(AUG[0:DH, slot, :]), src)
                else:
                    v.tensor_copy(VS[DH:P, VSI[what, j], :], news)
                    if what == "pool":
                        if j == 0:
                            v.memset(PP[:, 0:15], 0.0)
                            v.memset(PP[:, 1056:1071], 0.0)
                        last = v.tensor_copy(cut(PP[DH:P, j * 1056 + 15:j * 1056 + 15 + TT]), src)
                    else:
                        xt_free(dve, m)
                        last = v.tensor_copy(cut(XT[DH:P, :]), src)
                last.then_inc(s_evd, 1)

            def natural(m):
                what, j, _ = TILES[m]
                out = job()
                nat_free(dve, m)
                n = {"memk": 1, "memv": 1, "kw": 2}.get(what, 4)
                dst, c = nat_place(what, j)
                done(v.tensor_copy(dst[:, n:2 * n, c:c + P], out[:, 0:n * P].rearrange("p (t c) -> p t c", c=P)))

            def negmax(u):
                nk = UNITS[u][4]
                dve.wait_ge(s_S, u + 1)
                if UNITS[u][0] == "mem":
                    k = 2 * (u % 8)
                    v.tensor_reduce(stat[:, k:k + 2], bk(score_bank(u)).rearrange("p (e c) -> p e c", e=2), AX.X,
                                    ALU.max, negate=True).then_inc(s_nm, 1)
                    return
                v.tensor_reduce(stat[:, u % 8:u % 8 + 1], flat(score_bank(u), nk), AX.X, ALU.max,
                                negate=True).then_inc(s_nm, 1)

            def norm(u):
                what, h, i, _, _ = UNITS[u]
                dve.wait_ge(s_pv, u + 1)
                if what == "mem":
                    k = 2 * (u % 8)
                    r = stat[:, 32 + k:34 + k]
                    link(v.reciprocal(r, stat[:, 16 + k:18 + k]))
                    v.tensor_tensor(o_nat[:, 1, i, h * P:(h + 1) * P].rearrange("p (e d) -> p e d", e=2),
                                    bk(6 + u % 2)[:, 0:P].rearrange("p (e d) -> p e d", e=2),
                                    r.unsqueeze(2).to_broadcast([P, 2, DH]), ALU.mult).then_inc(s_on, 1)
                    return
                dst = o_nat[:, {"fox": 0, "sel": 2, "win": 2}[what], i, h * DH:(h + 1) * DH]
                src = bk(6 + u % 2)[:, 0:DH]
                r, c = stat[:, 32 + u % 8:33 + u % 8], stat[:, 48 + u % 8:49 + u % 8]
                link(v.reciprocal(r, stat[:, 16 + u % 8:17 + u % 8]))
                if what == "fox":
                    v.tensor_scalar(dst, src, r, None, ALU.mult).then_inc(s_on, 1)
                else:
                    g = H + 3 * h + (1 if what == "sel" else 2)
                    link(v.tensor_tensor(c, r, fga[:, i, g:g + 1], ALU.mult))
                    v.scalar_tensor_tensor(out=dst, in0=src, scalar=c, in1=dst, op0=ALU.mult,
                                           op1=ALU.add).then_inc(s_on, 1)

            def attend(u0, u1):
                n = ahead(u0)
                for u in range(u0, u0 + n):
                    negmax(u)
                for u in range(u0, u1):
                    for g in range(G0[u], G0[u + 1]):
                        if g % 2 == 0:
                            dve.wait_ge(s_pT, g + 1)
                            if u >= n:
                                dve.wait_ge(s_pv, u - n + 1)
                            c = 4 * (g - G0[u])
                            blocks = min(4, UNITS[u][4] - c)
                            o = 2048 + prob_slot(u) + c * P
                            v.tensor_copy(PP[:, o:o + blocks * P], bk(4)[:, 0:blocks * P]).then_inc(s_cD, 1)
                    if u > u0:
                        norm(u - 1)
                    if u + n < u1:
                        negmax(u + n)
                norm(u1 - 1)

            def pool_mean(j):
                dve.wait_ge(s_eva, 22 + j)
                dve.wait_ge(s_nst, 80)
                U = PP[:, j * 1056:j * 1056 + 15 + T]
                A, B = NAT[:, 2048:2048 + 15 + T], PP[:, 2112:2112 + 15 + T]
                n = 15 + T

                def add(out, a, lo_, shift, rows=slice(0, P)):
                    link(v.tensor_tensor(out[rows, lo_:n], a[rows, lo_:n], a[rows, lo_ - shift:n - shift], ALU.add))

                add(A, U, 1, 1)
                if j == 0:
                    add(B, A, 3, 2, slice(DH, P))
                    parts = ((0, A, 2), (1, B, 4))
                else:
                    add(B, A, 3, 2)
                    add(A, B, 7, 4)
                    add(B, A, 15, 8, slice(DH, P))
                    parts = ((0, A, 8), (1, B, 16))
                for a, S_, w in parts:
                    r = slice(a * DH, (a + 1) * DH)
                    v.scalar_tensor_tensor(out=POOLD[r, j, 16:T], in0=S_[r, 31:n], scalar=1.0 / w, in1=U[r, 31:n],
                                           op0=ALU.mult, op1=ALU.subtract)
                    link(v.tensor_tensor(POOLD[r, j, 0:16], S_[r, 15:31], rcnt[r, j, :], ALU.mult))
                    last = v.tensor_tensor(POOLD[r, j, 0:16], POOLD[r, j, 0:16], U[r, 15:31], ALU.subtract)
                last.then_inc(s_pd, 1)

            for step, n in STEPS:
                if step == "item":
                    if n == 1:
                        normalise(2)
                    if 2 <= n < 10:
                        normalise(n + 1)
                    lo(n)
                elif step == "project":
                    take(n)
                elif step == "natural":
                    natural(n)
                elif step == "pair" and n % 2 == 1:
                    out = job()
                    if n >= 8:
                        dve.wait_ge(s_w1u, 4)
                    done(v.tensor_copy(ft_cols(n % 8), out.rearrange("p (g n j) -> p g n j", g=2, n=8)))
                elif step == "attend":
                    attend(*PHASE[n])
                elif step == "gates":
                    dve.wait_ge(s_pc, 2)
                    dve.wait_ge(s_cst, 96)
                    link(v.tensor_tensor(slope_row, slope_row, ident[:, :], ALU.mult))
                    link(v.tensor_reduce(SLC[:, :], slope_row, AX.X, ALU.add))
                    link(v.tensor_scalar(BC[:, :], BC[:, :], SLC[:, 0:1], None, ALU.mult))
                    for g, w in enumerate(POOLW):
                        r = slice((g % 2) * DH, (g % 2 + 1) * DH)
                        link(v.tensor_scalar(rcnt[r, g // 2, :], rcnt[r, g // 2, :], float(w), None, ALU.min))
                    link(v.reciprocal(rcnt[:, :, :], rcnt[:, :, :]))
                    link(v.tensor_tensor(PLW[:, :, :], PLW[:, :, :], PLS[:, :, :], ALU.mult))
                    out = job()
                    v.tensor_copy(FG[:, 0:NQ, :], out[:, 0:16 * NQ].rearrange("p (t c) -> p t c", c=16))
                    link(v.memset(FG[:, NQ, :], 0.0))
                    done(v.tensor_copy(FG[0:NB, NQ, :], out[0:NB, 16 * NQ:16 * (NQ + 1)]))
                    dve.wait_ge(s_fD, nD[0])
                    link(v.tensor_tensor(lf[:, :, :], FG[:, :, 0:H],
                                         bfb[:, :].unsqueeze(1).to_broadcast([P, NQ + 1, H]), ALU.add))
                    v.scalar_tensor_tensor(out=fga[:, :, 0:H], in0=lf[:, :, :], scalar=-1.0, in1=lf[:, :, :],
                                           op0=ALU.mult, op1=ALU.max).then_inc(s_fgv, 1)
                    dve.wait_ge(s_fga, 2)
                    v.scalar_tensor_tensor(out=lf[:, :, :], in0=lf[:, :, :], scalar=0.0, in1=fga[:, :, 0:H],
                                           op0=ALU.min, op1=ALU.subtract).then_inc(s_lf, 1)
                    link(v.tensor_scalar(fga[:, :, H:16], fga[:, :, H:16], 1.0, None, ALU.add))
                    v.reciprocal(fga[:, :, H:16], fga[:, :, H:16]).then_inc(s_gate, 1)
                    dve.wait_ge(s_gate, 1)
                elif step == "forget":
                    for half in range(2):
                        out = job()
                        ini = 0.0 if half == 0 else OB[0:H, 511:512]
                        v.tensor_tensor_scan(OB[0:H, half * 512:(half + 1) * 512], onesc[0:H, 0:1].to_broadcast([H, 512]),
                                             out[0:H, :], ini, ALU.mult, ALU.add).then_inc(s_fD, 1)
                        dve.wait_ge(s_fD, nD[0])
                    v.tensor_scalar(OB[0:H, 1024:2048], OB[0:H, 0:1024], -1.0, None, ALU.mult).then_inc(s_c, 1)
                elif step == "compress":
                    if n:
                        dve.wait_ge(s_w1u, 4)
                    for par in range(2):
                        last = v.tensor_copy(ft_prompt(par, 1), xt_pairs(par, 1))
                    last.then_inc(s_ftd, 1)
                    out = job()
                    done(v.tensor_copy(FT[:, :, R_ALL], out[:, 0:NJ]))
                elif step == "compressed":
                    if n == 1:
                        out = job()
                        link(v.memset(PP[:, 3072:3328], 0.0))
                        for h in range(H):
                            r = slice(32 * h, 32 * h + NCB)
                            v.tensor_copy(PP[r, 3072 + h * DH:3072 + (h + 1) * DH], out[r, h * DH:(h + 1) * DH])
                        done(v.tensor_copy(VCs[:, :], out[0:NB * SCB, 256:384]))
                elif step == "cmp_scores":
                    out = job()
                    E = PP[:, 0:512].rearrange("p (i h n) -> p i h n", i=NQ, h=H)
                    E3 = PP[:, 0:512].rearrange("p (q n) -> p q n", n=NCB)
                    v.tensor_tensor(E, out.rearrange("p (i h n) -> p i h n", i=NQ, h=H),
                                    m_cmp[:, :, :].unsqueeze(2).to_broadcast([P, NQ, H, NCB]), ALU.add).then_inc(s_fD, 1)
                    dve.wait_ge(s_fD, nD[0])
                    link(v.tensor_reduce(cs[:, 0:32], E3, AX.X, ALU.max))
                    v.tensor_tensor(E3, E3, cs[:, 0:32].unsqueeze(2).to_broadcast([P, 32, NCB]),
                                    ALU.subtract).then_inc(s_cmv, 1)
                    dve.wait_ge(s_cma, 1)
                    link(v.tensor_tensor(E3[:, 0:H, :], E3[:, 0:H, :], seen0[:, :].unsqueeze(1).to_broadcast([P, H, NCB]),
                                         ALU.mult))
                    link(v.tensor_reduce(cs[:, 32:64], E3, AX.X, ALU.add))
                    link(v.tensor_scalar(cs[:, 32:64], cs[:, 32:64], 1e-30, None, ALU.max))
                    link(v.reciprocal(cs[:, 32:64], cs[:, 32:64]))
                    link(v.tensor_tensor(cs[:, 64:96].rearrange("p (i h) -> p i h", i=NQ),
                                         cs[:, 32:64].rearrange("p (i h) -> p i h", i=NQ),
                                         fga[:, 0:NQ, H:16:3], ALU.mult))
                    link(v.memset(PP[:, 1024:2048], 0.0))
                    v.tensor_tensor(PP[:, 1024:2048].rearrange("p (q n) -> p q n", n=32)[:, :, 0:NCB], E3,
                                    cs[:, 64:96].unsqueeze(2).to_broadcast([P, 32, NCB]), ALU.mult).then_inc(s_cm, 1)
                elif step == "cmp_turn":
                    out = job()
                    done(v.tensor_copy(PP[:, 2560:3072], out))
                elif step == "cmp_out":
                    for q in (1, 3):
                        out = job()
                        done(v.tensor_copy(o_nat[:, 2, 2 * q:2 * q + 2, :], out.rearrange("p (t c) -> p t c", t=2)))
                elif step == "pool_last":
                    out = job()
                    done(v.tensor_copy(poolp[:, n * P:(n + 1) * P], out[0:15, 0:P]))
                    pool_mean(n)
                    if n == 1:
                        dve.wait_ge(s_stp, 64)
                        for g, w in enumerate(POOLW):
                            last = v.tensor_reduce(PSUMS[:, g * DH:(g + 1) * DH],
                                                   STP[g].rearrange("p (r c) -> p c r", c=DH), AX.X, ALU.add)
                        last.then_inc(s_psum, 1)
                elif step == "pool_map":
                    for half in range(2):
                        out = job()
                        done(v.tensor_copy(o_nat[:, 3, 4 * half:4 * half + 4, n * P + DH:(n + 1) * P],
                                           out[:, 0:256].rearrange("p (t c) -> p t c", t=4)))
                elif step == "sample_new":
                    link(v.memset(NAT[:, 2048:3328], 0.0))
                    for a in range(2):
                        for p_ in range(2):
                            h = 2 * a + p_
                            r = slice(p_ * DH, (p_ + 1) * DH)
                            diag = lambda z, h_: z.rearrange("p b r -> p (b r)")[:, h_:h_ + 36 * (NB - 1) + 1:36]
                            v.tensor_copy(diag(QZF[r, a], h), QNs[:, h, :])
                            v.tensor_copy(diag(QZM[r, a], h), QNs[:, 8 + h, :])
                            v.tensor_copy(diag(QZN[a * DH:(a + 1) * DH], h), QNs[:, 4 + h, :])
                            v.tensor_copy(KNF[r, a, :], KNs[:, h, :])
                    for g in range(2):
                        r = slice(g * DH, (g + 1) * DH)
                        v.tensor_copy(KNS[r, :], KNs[:, 4 + g, :])
                        last = v.tensor_copy(KNW[r, :], KNs[:, 6 + g, :])
                    last.then_inc(s_qz, 1)
                    out = job()
                    dve.wait_ge(s_nst, 80)
                    done(v.tensor_copy(VNEW[:, 512:1024], out[0:NB, :]))
                    dve.wait_ge(s_fD, nD[0])
                    link(v.tensor_tensor(PSUMS, PSUMS, VNEW[:, 768:1024], ALU.add))
                    for g, w in enumerate(POOLW):
                        c = slice(g * DH, (g + 1) * DH)
                        last = v.scalar_tensor_tensor(out=PSUMS[:, c], in0=PSUMS[:, c], scalar=1.0 / w,
                                                      in1=VNEW[:, 768 + g * DH:768 + (g + 1) * DH], op0=ALU.mult,
                                                      op1=ALU.subtract)
                    last.then_inc(s_psd, 1)
                    dve.wait_ge(s_lfp, 16 * NB * NPG)
                    v.tensor_copy(LFR.rearrange("p (h t) -> p h t", h=H),
                                  LFP.rearrange("p (t h) -> p h t", h=H)).then_inc(s_lfr, 1)
                elif step == "sample_keys":
                    for b in range(NB):
                        for c in range(2):
                            q = 2 * b + c
                            out = job()
                            if q >= 2:
                                dve.wait_ge(s_sS, 5 * ((q - 2) // 2) + 2 * ((q - 2) % 2) + 2)
                            done(v.tensor_copy(KTD[:, q % 2, :], out))
                        if b == 0:
                            one = onesc[:, 0:1].to_broadcast([P, PAST + 1])
                            link(v.tensor_tensor_scan(BIAS, one, one, float(-PAST - 1), ALU.mult, ALU.add))
                            link(v.tensor_scalar(BIAS, BIAS, SLC[:, 0:1], None, ALU.mult))
                        if b == 1:
                            dve.wait_ge(s_sd, 16 * 8)
                            link(v.tensor_tensor_scan(CT, onesc[32:64, 0:1].to_broadcast([32, PAST + 1]), LFT, 0.0,
                                                      ALU.mult, ALU.add))
                            link(v.tensor_scalar(XT[0:32, 0:PAST + 1], CT, -1.0, CT[:, PAST:PAST + 1], ALU.mult,
                                                 ALU.add))
                elif step == "sample_values":
                    dve.wait_ge(s_sS, 5 * NB + 1)
                    v.tensor_tensor(X[0:96, 0:PAST], PS[0:96, 0, :], BIAS[0:96, 0:PAST], ALU.add)
                    v.tensor_tensor(X[0:96, PAST:PAST + 1], PS[0:96, 4, 0:1], BIAS[0:96, PAST:PAST + 1], ALU.add)
                    v.tensor_copy(X[96:P, 0:NMEM], PS[96:P, 0, 0:NMEM])
                    link(v.memset(X[96:P, NMEM:PAST + 1], NEG))
                    link(v.tensor_reduce(XC[:, 0:1], X, AX.X, ALU.max, negate=True))
                    link(v.tensor_tensor(XC[0:32, 8:16], PS[0:32, 5, 0:SCB], BC[0:32, :], ALU.add))
                    v.tensor_reduce(XC[0:32, 4:5], XC[0:32, 8:16], AX.X, ALU.max, negate=True).then_inc(s_sx, 1)
                    dve.wait_ge(s_se, 1)
                    link(v.reciprocal(XC[:, 2:3], XC[:, 1:2]))
                    link(v.tensor_tensor(XC[:, 2:3], XC[:, 2:3], GC[:, 0:1], ALU.mult))
                    link(v.tensor_scalar(X, X, XC[:, 2:3], None, ALU.mult))
                    v.tensor_scalar(XN8[:, :], E8[:, :], X[:, PAST:PAST + 1], None, ALU.mult)
                    link(v.reciprocal(XC[0:32, 6:7], XC[0:32, 5:6]))
                    link(v.tensor_tensor(XC[0:32, 6:7], XC[0:32, 6:7], GC[0:32, 1:2], ALU.mult))
                    link(v.tensor_scalar(XC[0:32, 8:16], XC[0:32, 8:16], XC[0:32, 6:7], None, ALU.mult))
                    v.tensor_tensor(XC[0:32, 16:80].rearrange("p (b n) -> p b n", b=NB),
                                    E8[0:32, :].unsqueeze(2).to_broadcast([32, NB, SCB]),
                                    XC[0:32, 8:16].unsqueeze(1).to_broadcast([32, NB, SCB]), ALU.mult).then_inc(s_px, 1)
                    out = job()
                    v.tensor_copy(PTn, out[0:NB, 0:P])
                    done(v.tensor_copy(PTc, out[0:NB * SCB, P:P + 32]))
                    out = job()
                    done(v.tensor_copy(oTs[:, 4:6, :], out[:, 0:2 * NB].rearrange("p (j b) -> p j b", j=2)))
                    for j in range(KC):
                        dve.wait_ge(s_woh, j + 1)
                        c = slice(j * P, (j + 1) * P)
                        v.tensor_tensor(wol[:, :, c], wo_raw(j), woh[:, :, c].bitcast(F32),
                                        ALU.subtract).then_inc(s_wol, 1)
                elif step == "mix":
                    def sample_outputs():
                        dve.wait_ge(s_vr, 4 * NB)
                        for a in range(2):
                            for p_ in range(2):
                                h = 2 * a + p_
                                r, q = slice(p_ * DH, (p_ + 1) * DH), slice(a * DH, (a + 1) * DH)
                                v.tensor_copy(oTs[r, a, :], bk(6)[r, 32 * a + h:32 * a + 32:4])
                                v.tensor_copy(oTs[r, 6 + a, :], bk(6)[r, 96 + 32 * a + h:128 + 32 * a:4])
                                last = v.tensor_copy(oTs[r, 2 + a, :], bk(6)[q, 64 + h:96:4])
                        link(last)

                    def gate(t):
                        cols = NB if t == NQ else P
                        gg = G2[:, t % 2, :].rearrange("p (k c) -> p k c", k=KC)[:, :, 0:cols]
                        sz = AUG[:, :, t * P:t * P + cols]
                        if t >= 2:
                            dve.wait_ge(s_gh, t - 1)
                        if t == NQ:
                            sample_outputs()
                            v.tensor_tensor(gg, oTs[:, :, :], sz, ALU.mult).then_inc(s_g, 1)
                        else:
                            dve.wait_ge(s_oT, t + 1)
                            src = PS[:, 4:6, :].rearrange("p a (k c) -> p (a k) c", k=4)
                            v.tensor_tensor(gg, src, sz, ALU.mult).then_inc(s_g, 1)
                        dve.wait_ge(s_gh, t + 1)
                        if t >= 2:
                            dve.wait_ge(s_y, t - 1)
                        part = lambda x_: x_[:, (t % 2) * 1024:(t % 2 + 1) * 1024].rearrange(
                            "p (k c) -> p k c", k=KC)[:, :, 0:cols]
                        v.tensor_tensor(part(TL), gg, part(TH).bitcast(F32), ALU.subtract).then_inc(s_gl, 1)

                    def final(t):
                        rows = NB if t == NQ else P
                        dve.wait_ge(s_ys, t + 1)
                        if t == 0:
                            dve.wait_ge(s_gf, 16)
                        y1 = PP[0:rows, (t % 2) * 1024:(t % 2 + 1) * 1024]
                        link(v.reciprocal(rms[0:rows, 16 + t:17 + t], rms[0:rows, 16 + t:17 + t]))
                        v.scalar_tensor_tensor(out=y1, in0=y1, scalar=rms[0:rows, 16 + t:17 + t], in1=gf[0:rows, :],
                                               op0=ALU.mult, op1=ALU.mult).then_inc(s_yo, 1)

                    gate(0)
                    for t in range(NQ + 1):
                        if t < NQ:
                            gate(t + 1)
                        if t > 0:
                            final(t - 1)
                        rows = NB if t == NQ else P
                        s = t % 2
                        dve.wait_ge(s_y, t + 1)
                        dve.wait_ge(s_xf[s], 16 * (t // 2 + 1))
                        if t >= 2:
                            dve.wait_ge(s_yst[s], 16 * (t // 2))
                        v.tensor_tensor(PP[0:rows, s * 1024:(s + 1) * 1024],
                                        PS[0:rows, 2 * s:2 * s + 2, :].rearrange("p a c -> p (a c)"),
                                        XW[0:rows, s, :], ALU.add).then_inc(s_y1, 1)
                    final(NQ)
                assert mark[step, n][1] == nD[0], (step, n, mark[step, n], nD)

        @block.gpsimd
        def _(pool):
            g = nc.gpsimd
            own = [0]

            def link(ins):
                own[0] += 1
                ins.then_inc(s_pb, 1)
                pool.wait_ge(s_pb, own[0])

            link(g.memset(ident[:, :], 0.0))
            link(g.affine_select(out=ident[:, :], in_=ident[:, :], compare_op=ALU.not_equal, fill=1.0, base=0,
                                 pattern=[[-1, P]], channel_multiplier=1))
            g.memset(epsc[:, :], EPS)
            g.memset(onesc[:, :], 1.0).then_inc(s_pc, 1)

            ones = onesc[:, 0:1].unsqueeze(2).to_broadcast([P, KC, P])

            def split(s, landed, hi_, lo_, count):
                pool.wait_ge(s_w[s], landed)
                g.tensor_tensor(hi_, WR[:, s, :, :], ones, ALU.mult).then_inc(s_wcp, 1)
                pool.wait_ge(s_wcp, count)
                g.tensor_tensor(lo_, WR[:, s, :, :], hi_.bitcast(F32), ALU.subtract).then_inc(s_split, 1)
                pool.wait_ge(s_split, count)

            def split_pair(it):
                for s in range(2):
                    used, landed, count = it * 2 + (s - 1), it * 16 + 16, it * 2 + (s + 1)
                    pool.wait_ge(s_proj, used)
                    split(s, landed, WH[:, s, :, :], WL[:, s, :, :], count)

            pool.wait_ge(s_pc, 1)
            for s in range(2):
                split(s, 16, WH[:, s, :, :], WL[:, s, :, :], s + 1)
            with pool.Fori(1, 3) as it:
                split_pair(it)
            pool.wait_ge(s_wg, 16)
            split_pair(3)

            for h in range(H):
                g.memset(slope_row[:, h:P:H], SLOPES[h])
            g.iota(BC[:, :], pattern=[[BLK, SCB]], base=BLK - 1 - PAST, channel_multiplier=0,
                   allow_small_or_imprecise_dtypes=True)
            g.iota(rcnt[:, :, :], pattern=[[0, 2], [1, 16]], base=1, channel_multiplier=0,
                   allow_small_or_imprecise_dtypes=True)
            g.memset(GC[:, :], 1.0)
            link(g.tensor_copy(identb[:, :], ident[:, :]))
            link(g.memset(m_diag[:, :], 0.0))
            link(g.affine_select(out=m_diag[:, :], in_=m_diag[:, :], compare_op=ALU.is_ge, fill=NEG, base=0,
                                 pattern=[[-1, P]], channel_multiplier=1))
            link(g.memset(m_win[:, :], 0.0))
            link(g.affine_select(out=m_win[:, :], in_=m_win[:, :], compare_op=ALU.is_ge, fill=NEG, base=0,
                                 pattern=[[1, P]], channel_multiplier=-1))
            link(g.memset(m_cmp[:, :, :], 0.0))
            link(g.affine_select(out=m_cmp[:, :, :], in_=m_cmp[:, :, :], compare_op=ALU.is_ge, fill=NEG,
                                 base=-(BLK - 1), pattern=[[P, NQ], [-BLK, NCB]], channel_multiplier=1))
            link(g.memset(seen0[:, :], 1.0))
            link(g.affine_select(out=seen0[:, :], in_=seen0[:, :], compare_op=ALU.is_ge, fill=0.0,
                                 base=-(BLK - 1), pattern=[[-BLK, NCB]], channel_multiplier=1))
            for br in range(4):
                r = slice(32 * br, 32 * br + 32)
                link(g.memset(E8[r, :], 1.0))
                link(g.affine_select(out=E8[r, :], in_=E8[r, :], compare_op=ALU.is_ge, fill=0.0, base=0,
                                     pattern=[[-H, NB]], channel_multiplier=1))
                link(g.affine_select(out=E8[r, :], in_=E8[r, :], compare_op=ALU.is_ge, fill=0.0, base=H - 1,
                                     pattern=[[H, NB]], channel_multiplier=-1))
            g.memset(AUG[DH:DH + 2, :, :], 1.0).then_inc(s_pc, 1)
            pool.wait_ge(s_pc, 2)
            link(g.iota(AUG[96:98, 0:4, :], pattern=[[0, 4], [1, TT]], base=0, channel_multiplier=0,
                        allow_small_or_imprecise_dtypes=True))
            for h in range(H):
                link(g.tensor_scalar(AUG[96:98, h, :], AUG[96:98, h, :], -SLOPES[h], None, ALU.mult))
                link(g.memset(AUG[96:97, h, :], SLOPES[h]))
            link(g.memset(AUG[96:98, 4:8, :], 1.0))
            link(g.iota(AUG[96:97, 4:8, :], pattern=[[0, 4], [1, TT]], base=0, channel_multiplier=0,
                        allow_small_or_imprecise_dtypes=True))
            link(g.memset(KCa[DH:DH + 2, :, :], 1.0))
            g.iota(KCa[DH:DH + 1, :, :], pattern=[[0, 2], [BLK, NCB]], base=BLK - 1, channel_multiplier=0,
                   allow_small_or_imprecise_dtypes=True).then_inc(s_pc, 1)
            pool.wait_ge(s_pc, 3)
            with pool.Fori(4, NT // 2) as it:
                split_pair(it)
            pool.wait_ge(s_proj, NT - 2)
            split(0, 16 * (NT // 2 + 1), WH[:, 0, :, :], WL[:, 0, :, :], NT)

        @block.sync
        def _(sp):
            xp, xs = x_p[0], x_s[:, 0, :]
            win, wout = w_in[0], w_out[0]

            def load_x(i):
                src = mem_p[0, i * P:(i + 1) * P, :] if i < 2 else xs if i == 10 else xp[(i - 2) * P:(i - 1) * P, :]
                rows = NB if i == 10 else P
                if 4 <= i < 6:
                    sp.wait_ge(s_itT, i - 3)
                elif i >= 6:
                    sp.wait_ge(s_xn, i - 5)
                sp.dma_start(xr[0:rows, i % 4, :], src).then_inc(s_x[i % 4], 16)

            def load_w(m):
                if m >= 2:
                    sp.wait_ge(s_split, m - 1)
                if m == AT["gate", 0]:
                    for dst, c, sem_ in ((slice(0, H), C_F, s_w[m % 2]), (slice(H, 16), C_G, s_wg)):
                        sp.dma_start(WR[:, m % 2, :, dst],
                                     win[:, c:c + dst.stop - dst.start].rearrange("(k p) c -> p k c", p=P)).then_inc(sem_, 16)
                    return
                what, _, c = TILES[m]
                src = (w_mem[0] if what in ("memk", "memv") else win)[:, c:c + P]
                sp.dma_start(WR[:, m % 2, :, :], src.rearrange("(k p) c -> p k c", p=P)).then_inc(s_w[m % 2], 16)

            def page(i):
                return sp.value_load(ptb[0:1, bass.ds(i, 1)], min_val=0, max_val=c_fox.shape[1] - 1)

            def load_pair(q):
                kind, n, half = q // 16, (q % 16) // 2, q % 2
                if q == 0:
                    sp.wait_ge(s_on, PHASE[0][1])
                if q == 20:
                    sp.wait_ge(s_nst, 32)
                if q >= 28:
                    sem_, val = mark["pair", 1, (q - 28) // 2]
                    sp.wait_ge(sem_, val)
                for a in range(2):
                    pg = page(NPG * n + 2 * half + a)
                    for g in range(2):
                        src = c_nsa[0, bass.ds(pg, 1), :, kind, g, :].rearrange("o (j r) d -> (o j) r d", r=2)
                        dst = pair_slot(q)[a * DH:(a + 1) * DH, g, :].rearrange("p (r d) -> p r d", r=2)
                        sp.dma_start(dst, src).then_inc(s_pair[n], 16)

            def load_w1(n):
                kind, c = n // 4, n % 4
                if n >= 2:
                    sp.wait_ge(s_w1u, n - 1)
                src = w1[0, kind, c * 1024:(c + 1) * 1024, :].rearrange("(j p) e -> p j e", p=P)
                sp.dma_start(w1s[:, n % 2, :, :], src).then_inc(s_w1[n % 2], 16)

            def store_nat(dst, what):
                sp.dma_start(dst, what).then_inc(s_nst, 16)

            def jobs_done(step, n):
                a, d = mark[step, n]
                sp.wait_ge(s_fA, a)
                sp.wait_ge(s_fD, d)

            sp.dma_start(ptb[:, :], ptab.rearrange("(o b) n -> o (b n)", o=1)).then_inc(s_pt, 16)
            for i in range(4):
                load_x(i)
            load_w(0)
            load_w(1)
            for i, m in zip(range(4, 11), (2, 3, 4, 5, None, None, None)):
                load_x(i)
                if m is not None and m < 4:
                    load_w(m)
            load_w(4)
            load_w(5)
            load_w(6)
            sp.wait_ge(s_pt, 16)
            jobs_done("natural", 3)
            store_nat(o_memkv[0, 0].rearrange("(t p) a h d -> p t (a h d)", p=P), nat[:, 0:2, :])
            load_w(7)
            load_w(8)
            for q in range(4):
                load_pair(q)
            sp.wait_ge(s_lf, 1)
            sp.dma_start(o_lf[0, 0].rearrange("(t p) h -> p t h", p=P), lf[:, 0:NQ, :]).then_inc(s_st, 16)
            sp.dma_start(o_lf_s[0, :, 0, :], lf[0:NB, NQ, :]).then_inc(s_st, 16)
            load_w(9)
            sp.wait_ge(s_c, 1)
            sp.wait_ge(s_pc, 2)
            sp.dma_start(AUG[65:66, 0:4, 0:T], OB[0:H, 0:1024]).then_inc(s_aug, 16)
            sp.dma_start(AUG[64:65, 4:8, 0:T], OB[0:H, 1024:2048]).then_inc(s_aug, 16)
            for n in range(5):
                load_w(10 + n)
                if n < 4:
                    for q in range(4 + 3 * n, 7 + 3 * n):
                        load_pair(q)
            jobs_done("natural", 12)
            store_nat(o_foxkv[0, 0].rearrange("(t p) a h d -> p t (a h d)", p=P), nat)
            load_w(15)
            load_w(16)
            for q in range(16, 20):
                load_pair(q)
            sp.wait_ge(s_on, PHASE[1][1])
            sp.wait_ge(s_pc, 3)
            sp.dma_start(AUG[64:66, :, :], AUG[96:98, :, :]).then_inc(s_aug, 16)
            load_w1(0)
            load_w1(1)
            for q in range(20, 23):
                load_pair(q)
            load_w(17)
            load_w1(2)
            for q in range(23, 25):
                load_pair(q)
            load_w1(3)
            for q in range(25, 28):
                load_pair(q)
            load_w(18)
            load_w1(4)
            load_w1(5)
            for q in range(28, 32):
                load_pair(q)
            load_w1(6)
            load_w1(7)
            load_w(19)
            load_w(20)
            load_w(21)
            jobs_done("natural", 18)
            store_nat(o_nsakv[0, 0].rearrange("(t p) a g d -> p t (a g d)", p=P), nat)
            jobs_done("natural", 20)
            ow = o_nsawin[0, 0].rearrange("(t p) a g d -> p t a (g d)", p=P)
            store_nat(ow[:, :, 0, :], kw)
            store_nat(ow[:, :, 1, :], vw[:, 4:8, :])
            load_w(22)
            load_w(23)
            sp.wait_ge(s_on, len(UNITS))
            sp.wait_ge(s_nst, 80)
            for g, w in enumerate(POOLW):
                src = st_pool[0, :, 16 - w:15, g * DH:(g + 1) * DH]
                sp.dma_start(STP[g].rearrange("p (r c) -> p r c", c=DH), src).then_inc(s_stp, 16)

            def load_lf(b):
                for pg in range(NPG):
                    pn = page(NPG * b + pg)
                    sp.dma_start(LFP[pg * NB + b:pg * NB + b + 1, :],
                                 c_lf[0, bass.ds(pn, 1)].rearrange("o t h -> o (t h)")).then_inc(s_lfp, 16)

            for m in range(24, 28):
                load_w(m)
                for b in (2 * m - 48, 2 * m - 47):
                    load_lf(b)

            def pages(b):
                return [page(b * NPG + pg) for pg in range(NPG)]

            def load_kv(b, br, kv, pn, slots):
                if br in (0, 1):
                    for pg in range(NPG):
                        if br == 0:
                            dst = slots[0][:, pg * 256:(pg + 1) * 256]
                            src = c_fox[0, bass.ds(pn[pg], 1), :, kv, :, :].rearrange("o t h d -> (o t) (h d)")
                        else:
                            dst = slots[1][:, pg * P:(pg + 1) * P]
                            src = c_nsa[0, bass.ds(pn[pg], 1), :, 2 + kv, :, :].rearrange("o t g d -> (o t) (g d)")
                        sp.dma_start(dst, src).then_inc(s_kv[br], 16)
                elif br == 2:
                    src = st_win[0, bass.ds(b, 1), :, kv, :, :].rearrange("o (t p) g d -> p (o t) (g d)", p=P)
                    sp.dma_start(slots[2][:, 0:512].rearrange("p (t c) -> p t c", t=4), src).then_inc(s_kv[2], 16)
                else:
                    src = c_mem[0, bass.ds(b, 1), :, kv, :, :].rearrange("o (t p) h d -> p (o t) (h d)", p=P)
                    sp.dma_start(slots[3][:, 0:512].rearrange("p (t c) -> p t c", t=2), src).then_inc(s_kv[3], 16)

            sp.wait_ge(s_pd, 2)
            sp.wait_ge(s_psum, 1)
            k_ring = [ring[:, br, :] for br in range(4)]
            first = pages(0)
            for br in range(4):
                load_kv(0, br, 0, first, k_ring)
            sp.wait_ge(s_lfr, 1)
            for pg in range(NPG):
                sp.dma_start(LFT[:, pg * P:(pg + 1) * P],
                             LFR[pg * NB:(pg + 1) * NB, :].rearrange("b (h t) -> b h t", h=H)).then_inc(s_sd, 16)
            sp.dma_start(LFT[:, PAST:PAST + 1], lf[0:NB, NQ, :]).then_inc(s_sd, 16)
            for dst, c in ((GC[32:64, 0:1], 1), (GC[64:96, 0:1], 2), (GC[0:32, 1:2], 0)):
                sp.dma_start(dst, fga[0:NB, NQ, H + c:16:3]).then_inc(s_sd, 16)
            ka, kd = mark["K"]

            def slot_read(b, br):
                if br == 0:
                    sp.wait_ge(s_TA, b * 3 + (ka + 1))
                    sp.wait_ge(s_TD, b * 2 + (kd + 1))
                elif br == 2:
                    sp.wait_ge(s_TD, b * 2 + (kd + 2))
                else:
                    sp.wait_ge(s_TA, b * 3 + (ka + (2 if br == 1 else 3)))

            for m in (28, 29, 30):
                load_w(m)
                n = m - 28
                with sp.Fori(2 * n + 1, 2 * n + 3) as b:
                    pn = pages(b)
                    for br in range(4):
                        slot_read(b - 1, br)
                        load_kv(b, br, 0, pn, k_ring)
            pn = pages(NB - 1)
            for br in range(4):
                slot_read(NB - 2, br)
                load_kv(NB - 1, br, 0, pn, k_ring)
            jobs_done("pool_last", 1)
            sp.dma_start(o_pool[0, 0], poolp).then_inc(s_st, 16)
            sp.dma_start(o_pool_s[0, :, 0:14, :], st_pool[0, :, 1:15, :]).then_inc(s_st, 16)
            sp.dma_start(o_win_s[0, :, 0:511], st_win[0, :, 1:512]).then_inc(s_st, 16)

            def load_wo(j):
                if j < 2:
                    sp.wait_ge(s_split, NT - 1 + j)
                elif j < 4:
                    slot_read(NB - 1, j - 2)
                else:
                    sp.wait_ge(s_wol, j - 3)
                sp.dma_start(wo_raw(j), wout[:, j * P:(j + 1) * P].rearrange("(k p) c -> p k c", p=P)).then_inc(s_wo[j % 4], 16)

            first = pages(0)
            load_wo(0)
            load_wo(2)
            load_wo(3)
            for br in (1, 2, 3):
                if br != 2:
                    slot_read(NB - 1, max(br, 2))
                load_kv(0, br, 1, first, v_ring)
            load_wo(1)
            sp.wait_ge(s_sx, 1)
            load_kv(0, 0, 1, first, v_ring)
            sp.dma_start(gf, fin_g.rearrange("(o d) -> o d", o=1).partition_broadcast(P)).then_inc(s_gf, 16)
            for j in range(4, KC):
                load_wo(j)

            def load_values(b):
                pn = pages(b)
                for br in range(4):
                    sp.wait_ge(s_vr, 4 * (b - 1) + (1, 2, 3, 4)[br])
                    load_kv(b, br, 1, pn, v_ring)

            load_values(1)
            sp.dma_start(o_foxkv_s[0, :, 0, 0].rearrange("b h d -> b (h d)"), KNEW[:, 0:256]).then_inc(s_st, 16)
            sp.dma_start(o_foxkv_s[0, :, 0, 1].rearrange("b h d -> b (h d)"), VNEW[:, 0:256]).then_inc(s_st, 16)
            sp.dma_start(o_nsakv_s[0, :, 0, 0:2].rearrange("b a g d -> b (a g d)"), VNEW[:, 256:512]).then_inc(s_st, 16)
            sp.dma_start(o_nsakv_s[0, :, 0, 2].rearrange("b g d -> b (g d)"), KNEW[:, 256:384]).then_inc(s_st, 16)
            sp.dma_start(o_nsakv_s[0, :, 0, 3].rearrange("b g d -> b (g d)"), VNEW[:, 512:640]).then_inc(s_st, 16)
            sp.dma_start(o_win_s[0, :, 511, 0].rearrange("b g d -> b (g d)"), KNEW[:, 384:512]).then_inc(s_st, 16)
            sp.dma_start(o_win_s[0, :, 511, 1].rearrange("b g d -> b (g d)"), VNEW[:, 640:768]).then_inc(s_st, 16)
            sp.dma_start(o_pool_s[0, :, 14, :], VNEW[:, 768:1024]).then_inc(s_st, 16)

            def load_x2(t):
                rows = NB if t == NQ else P
                if t < 2:
                    sp.wait_ge(s_wol, KC)
                else:
                    sp.wait_ge(s_ys, t - 1)
                sp.dma_start(XW[0:rows, t % 2, :], xs if t == NQ else xp[t * P:(t + 1) * P, :]).then_inc(s_xf[t % 2], 16)

            load_x2(0)
            load_x2(1)
            for t in range(NQ + 1):
                if t + 2 < NB:
                    load_values(t + 2)
                rows = NB if t == NQ else P
                sp.wait_ge(s_yo, t + 1)
                sp.dma_start(y_s[:, 0, :] if t == NQ else y_p[0, t * P:(t + 1) * P, :],
                             PP[0:rows, (t % 2) * 1024:(t % 2 + 1) * 1024]).then_inc(s_yst[t % 2], 16)
                if t + 2 <= NQ:
                    load_x2(t + 2)
            sp.wait_ge(s_yst[0], 16 * 5)
            sp.wait_ge(s_yst[1], 16 * 4)
            sp.wait_ge(s_nst, 80)
            sp.wait_ge(s_st, 16 * 13)


_INS = ["x_prompt", "x_sample", "cache_fox_kv", "cache_fox_lf", "cache_nsa_kv", "state_nsa_win", "state_pool",
        "cache_mem_kv", "page_table", "mem_prompt", "norm_g", "w_in", "b_fgt", "nsa_pe", "nsa_w1", "nsa_w2",
        "pool_w", "pool_scale", "w_mem_kv", "w_out", "final_g"]
_OUTS = [(1, T, D), (NB, 1, D), (1, 1, T, 2, H, DH), (1, 1, T, H), (1, 1, T, 4, 2, DH), (1, 1, 512, 2, 2, DH),
         (1, 1, 15, 256), (1, 1, NMEM, 2, H, DH), (1, NB, 1, 2, H, DH), (1, NB, 1, H), (1, NB, 1, 4, 2, DH),
         (1, NB, 512, 2, 2, DH), (1, NB, 15, 256)]


def kernel(**inputs):
    import numpy as np
    import concourse.bacc as bacc
    from concourse.bass_utils import run_bass_kernel_spmd

    nc = bacc.Bacc("TRN2", target_bir_lowering=False, num_devices=1)
    arrays, args = {}, []
    for name in _INS:
        a = np.ascontiguousarray(inputs[name])
        arrays[f"in_{name}"] = a
        args.append(nc.dram_tensor(f"in_{name}", a.shape, mybir.dt.from_np(a.dtype), kind="ExternalInput").ap())
    for i, shape in enumerate(_OUTS):
        args.append(nc.dram_tensor(f"out_{i}", shape, F32, kind="ExternalOutput").ap())
    build(nc, *args)
    r = run_bass_kernel_spmd(nc, [arrays], core_ids=[0])
    return tuple(r.results[0][f"out_{i}"] for i in range(len(_OUTS)))
```
